# Optimizing a Trainium2 kernel written in Bass

```python
import jax, jax.numpy as jnp
from jax import lax
import numpy as np

D_MODEL = 1024
BATCH = 1
SEQ = 512
DEPTH = 2

N_EVEN = (DEPTH + 1) // 2
N_ODD = DEPTH // 2
D_PLE = 256
EPS = 1e-6

CONV_GROUPS = 8
CONV_GROUP_DIM = 64
CONV_DIM = CONV_GROUPS * CONV_GROUP_DIM
CONV_WIDTH = 3
GMLP_HEADS = 8
GMLP_HEAD_DIM = 64
GMLP_DIM = GMLP_HEADS * GMLP_HEAD_DIM
GMLP_CHUNK = 128
EVEN_IN = 3 * CONV_DIM + 2 * GMLP_DIM
EVEN_MIX = CONV_DIM + GMLP_DIM

MLA_HEADS = 8
MLA_NOPE = 64
MLA_ROPE = 32
MLA_V = 64
MLA_QK = MLA_NOPE + MLA_ROPE
Q_LORA = 384
KV_LORA = 256
ROPE_THETA = 10000.0
ATTN_BLOCK = 128
MLSTM_HEADS = 4
MLSTM_QK = 64
MLSTM_V = 128
MLSTM_CHUNK = 64
ODD_IN = Q_LORA + KV_LORA + MLA_ROPE + 2 * MLSTM_HEADS * MLSTM_QK + 2 * MLSTM_HEADS * MLSTM_V + 2 * MLSTM_HEADS
ODD_MIX = MLA_HEADS * MLA_V + MLSTM_HEADS * MLSTM_V

D_FF = -(-8 * D_MODEL // (3 * 256)) * 256


def rmsnorm(x, g):
    xf = x.astype(jnp.float32)
    y = xf * lax.rsqrt(jnp.mean(xf * xf, axis=-1, keepdims=True) + EPS)
    return (y * g.astype(jnp.float32)).astype(x.dtype)

def swiglu(h, w_gate, w_up, w_down):
    return (jax.nn.silu(h @ w_gate) * (h @ w_up)) @ w_down

def short_gated_conv(b_gate, c_gate, x_in, w_conv):
    z = c_gate * x_in
    conv = lax.conv_general_dilated(
        z, w_conv[:, None, :].astype(z.dtype), window_strides=(1,),
        padding=[(CONV_WIDTH - 1, 0)], dimension_numbers=('NWC', 'WIO', 'NWC'),
        feature_group_count=CONV_DIM)
    return b_gate * conv

def chunked_spatial_gating(u, v, g_v, w_s, b_s):
    bsz, seq, _ = u.shape
    n_chunks = seq // GMLP_CHUNK
    shape5 = (bsz, n_chunks, GMLP_CHUNK, GMLP_HEADS, GMLP_HEAD_DIM)
    u = jax.nn.gelu(u).reshape(shape5)
    v = rmsnorm(jax.nn.gelu(v).reshape(shape5), g_v)
    causal = jnp.tril(jnp.ones((GMLP_CHUNK, GMLP_CHUNK), dtype=w_s.dtype))
    mixed = jnp.einsum('hts,bnshd->bnthd', w_s * causal, v) + b_s.T[:, :, None]
    return (u * mixed).reshape(bsz, seq, GMLP_DIM)

def rope_tables(positions, dim, dtype):
    inv_freq = ROPE_THETA ** (-jnp.arange(0, dim, 2, dtype=jnp.float32) / dim)
    ang = positions.astype(jnp.float32)[..., None] * inv_freq
    return jnp.cos(ang)[:, :, None, :].astype(dtype), jnp.sin(ang)[:, :, None, :].astype(dtype)

def apply_rope(x, cos, sin):
    half = x.shape[-1] // 2
    x1, x2 = x[..., :half], x[..., half:]
    return jnp.concatenate([x1 * cos - x2 * sin, x2 * cos + x1 * sin], axis=-1)

def causal_block_attention(q, k, v):
    bsz, seq, heads, dk = q.shape
    n_blocks = seq // ATTN_BLOCK
    q_blocks = q.reshape(bsz, n_blocks, ATTN_BLOCK, heads, dk).transpose(1, 0, 2, 3, 4)
    k_idx = jnp.arange(seq)
    scale = dk ** -0.5

    def one_block(args):
        qi, bi = args
        s = jnp.einsum('bqhd,bkhd->bhqk', qi, k).astype(jnp.float32) * scale
        q_idx = bi * ATTN_BLOCK + jnp.arange(ATTN_BLOCK)
        s = jnp.where(k_idx[None, :] <= q_idx[:, None], s, -jnp.inf)
        pr = jax.nn.softmax(s, axis=-1).astype(v.dtype)
        return jnp.einsum('bhqk,bkhv->bqhv', pr, v)

    out = lax.map(one_block, (q_blocks, jnp.arange(n_blocks)))
    return out.transpose(1, 0, 2, 3, 4).reshape(bsz, seq, heads, v.shape[-1])

def latent_attention(q_lat, kv_lat, k_pe, positions, g_qa, g_kva, w_q_up, w_kv_up, g_q, g_k):
    bsz, seq, _ = q_lat.shape
    q = (rmsnorm(q_lat, g_qa) @ w_q_up).reshape(bsz, seq, MLA_HEADS, MLA_QK)
    kv = (rmsnorm(kv_lat, g_kva) @ w_kv_up).reshape(bsz, seq, MLA_HEADS, MLA_NOPE + MLA_V)
    k_nope, v = kv[..., :MLA_NOPE], kv[..., MLA_NOPE:]
    cos, sin = rope_tables(positions, MLA_ROPE, q.dtype)
    q_nope = rmsnorm(q[..., :MLA_NOPE], g_q[:MLA_NOPE])
    q_pe = apply_rope(rmsnorm(q[..., MLA_NOPE:], g_q[MLA_NOPE:]), cos, sin)
    k_nope = rmsnorm(k_nope, g_k[:MLA_NOPE])
    k_pe = apply_rope(rmsnorm(k_pe[:, :, None, :], g_k[MLA_NOPE:]), cos, sin)
    q = jnp.concatenate([q_nope, q_pe], axis=-1)
    k = jnp.concatenate([k_nope, jnp.broadcast_to(k_pe, (bsz, seq, MLA_HEADS, MLA_ROPE))], axis=-1)
    return causal_block_attention(q, k, v).reshape(bsz, seq, MLA_HEADS * MLA_V)

def mlstm_chunkwise(q, k, v, i_pre, f_pre):
    out_dtype = v.dtype
    bsz, seq, heads, dk = q.shape
    dv = v.shape[-1]
    L = MLSTM_CHUNK
    nc = seq // L
    f32 = jnp.float32

    def to_chunks(a):
        return a.astype(f32).reshape(bsz, nc, L, heads, -1).transpose(1, 0, 3, 2, 4)

    def gate_chunks(a):
        return a.astype(f32).reshape(bsz, nc, L, heads).transpose(1, 0, 3, 2)

    qc = to_chunks(q) * (dk ** -0.5)
    kc, vc = to_chunks(k), to_chunks(v)
    ic = gate_chunks(i_pre)
    ac = jnp.cumsum(jax.nn.log_sigmoid(gate_chunks(f_pre)), axis=-1)
    causal = jnp.tril(jnp.ones((L, L), dtype=bool))

    def step(carry, xs):
        c_mat, n_vec, m = carry
        qb, kb, vb, ib, ab = xs
        d = jnp.where(causal, ab[..., :, None] - ab[..., None, :] + ib[..., None, :], -jnp.inf)
        inter = ab + m[..., None]
        m_t = jnp.maximum(inter, jnp.max(d, axis=-1))
        w_intra = jnp.exp(d - m_t[..., None])
        w_inter = jnp.exp(inter - m_t)
        s = jnp.einsum('bhtd,bhsd->bhts', qb, kb) * w_intra
        num = jnp.einsum('bhts,bhsv->bhtv', s, vb) + w_inter[..., None] * jnp.einsum('bhtd,bhvd->bhtv', qb, c_mat)
        den = jnp.sum(s, axis=-1) + w_inter * jnp.einsum('bhtd,bhd->bht', qb, n_vec)
        h = num / jnp.maximum(jnp.abs(den), jnp.exp(-m_t))[..., None]
        a_last = ab[..., -1]
        m_new = m_t[..., -1]
        w_s = jnp.exp(a_last[..., None] - ab + ib - m_new[..., None])
        decay = jnp.exp(a_last + m - m_new)
        c_new = decay[..., None, None] * c_mat + jnp.einsum('bhs,bhsv,bhsd->bhvd', w_s, vb, kb)
        n_new = decay[..., None] * n_vec + jnp.einsum('bhs,bhsd->bhd', w_s, kb)
        return (c_new, n_new, m_new), h

    init = (jnp.zeros((bsz, heads, dv, dk), f32), jnp.zeros((bsz, heads, dk), f32), jnp.zeros((bsz, heads), f32))
    _, hs = lax.scan(step, init, (qc, kc, vc, ic, ac))
    return hs.transpose(1, 0, 3, 2, 4).reshape(bsz, seq, heads, dv).astype(out_dtype)

def even_mixer(hn, w_in, w_conv, g_v, w_s, b_s, w_out):
    z = hn @ w_in
    b_gate, c_gate, x_in, u, v = jnp.split(z, [CONV_DIM, 2 * CONV_DIM, 3 * CONV_DIM, 3 * CONV_DIM + GMLP_DIM], axis=-1)
    y_a = short_gated_conv(b_gate, c_gate, x_in, w_conv)
    y_b = chunked_spatial_gating(u, v, g_v, w_s, b_s)
    return jnp.concatenate([y_a, y_b], axis=-1) @ w_out

def odd_mixer(hn, positions, w_in, b_gate, g_qa, g_kva, w_q_up, w_kv_up, g_q, g_k, g_mh, w_out):
    bsz, seq, _ = hn.shape
    z = hn @ w_in
    sizes = [Q_LORA, KV_LORA, MLA_ROPE, MLSTM_HEADS * MLSTM_QK, MLSTM_HEADS * MLSTM_QK,
             MLSTM_HEADS * MLSTM_V, MLSTM_HEADS * MLSTM_V, MLSTM_HEADS, MLSTM_HEADS]
    q_lat, kv_lat, k_pe, mq, mk, mv, mo, mi, mf = jnp.split(z, np.cumsum(sizes)[:-1].tolist(), axis=-1)
    y_c = latent_attention(q_lat, kv_lat, k_pe, positions, g_qa, g_kva, w_q_up, w_kv_up, g_q, g_k)
    h_m = mlstm_chunkwise(mq.reshape(bsz, seq, MLSTM_HEADS, MLSTM_QK),
                          mk.reshape(bsz, seq, MLSTM_HEADS, MLSTM_QK),
                          mv.reshape(bsz, seq, MLSTM_HEADS, MLSTM_V),
                          mi + b_gate[:MLSTM_HEADS], mf + b_gate[MLSTM_HEADS:])
    y_d = jax.nn.sigmoid(mo) * rmsnorm(h_m, g_mh).reshape(bsz, seq, MLSTM_HEADS * MLSTM_V)
    return jnp.concatenate([y_c, y_d], axis=-1) @ w_out

def first_inputs(seed: int = 0) -> dict:
    key = jax.random.key(seed)
    ks = list(jax.random.split(key, 40))
    f32 = jnp.float32

    def normal(shape):
        return jax.random.normal(ks.pop(), shape, f32)

    def dense(shape, fan_in):
        return normal(shape) * fan_in ** -0.5

    def gain(shape):
        return 1.0 + 0.05 * normal(shape)

    x = normal((BATCH, SEQ, D_MODEL))
    p = normal((DEPTH, BATCH, SEQ, D_PLE))
    positions = jnp.arange(SEQ, dtype=jnp.int32)[None, :] + jax.random.randint(ks.pop(), (BATCH, 1), 0, SEQ, dtype=jnp.int32)
    od_b_gate = jnp.concatenate([0.1 * normal((N_ODD, MLSTM_HEADS)), 3.0 + 0.1 * normal((N_ODD, MLSTM_HEADS))], axis=-1)
    return {
        'x': x,
        'p': p,
        'positions': positions,
        'g_mix': gain((DEPTH, D_MODEL)),
        'g_ffn': gain((DEPTH, D_MODEL)),
        'g_ple': gain((DEPTH, D_MODEL)),
        'ev_w_in': dense((N_EVEN, D_MODEL, EVEN_IN), D_MODEL),
        'ev_w_conv': dense((N_EVEN, CONV_WIDTH, CONV_DIM), CONV_WIDTH),
        'ev_g_v': gain((N_EVEN, GMLP_HEADS, GMLP_HEAD_DIM)),
        'ev_w_s': dense((N_EVEN, GMLP_HEADS, GMLP_CHUNK, GMLP_CHUNK), GMLP_CHUNK),
        'ev_b_s': 1.0 + 0.1 * normal((N_EVEN, GMLP_HEADS, GMLP_CHUNK)),
        'ev_w_out': dense((N_EVEN, EVEN_MIX, D_MODEL), EVEN_MIX),
        'od_w_in': dense((N_ODD, D_MODEL, ODD_IN), D_MODEL),
        'od_b_gate': od_b_gate,
        'od_g_qa': gain((N_ODD, Q_LORA)),
        'od_g_kva': gain((N_ODD, KV_LORA)),
        'od_w_q_up': dense((N_ODD, Q_LORA, MLA_HEADS * MLA_QK), Q_LORA),
        'od_w_kv_up': dense((N_ODD, KV_LORA, MLA_HEADS * (MLA_NOPE + MLA_V)), KV_LORA),
        'od_g_q': gain((N_ODD, MLA_QK)),
        'od_g_k': gain((N_ODD, MLA_QK)),
        'od_g_mh': gain((N_ODD, MLSTM_HEADS, MLSTM_V)),
        'od_w_out': dense((N_ODD, ODD_MIX, D_MODEL), ODD_MIX),
        'w_gate': dense((DEPTH, D_MODEL, D_FF), D_MODEL),
        'w_up': dense((DEPTH, D_MODEL, D_FF), D_MODEL),
        'w_down': dense((DEPTH, D_FF, D_MODEL), D_FF),
        'w_ple_proj': dense((DEPTH, D_PLE, D_MODEL), D_PLE),
        'w_ple_gate': dense((DEPTH, D_MODEL, D_MODEL), D_MODEL),
    }

def first_block(x, p, positions, g_mix, g_ffn, g_ple, ev_w_in, ev_w_conv, ev_g_v, ev_w_s, ev_b_s, ev_w_out,
              od_w_in, od_b_gate, od_g_qa, od_g_kva, od_w_q_up, od_w_kv_up, od_g_q, od_g_k, od_g_mh, od_w_out,
              w_gate, w_up, w_down, w_ple_proj, w_ple_gate):
    h = x
    for layer in range(DEPTH):
        j = layer // 2
        hn = rmsnorm(h, g_mix[layer])
        if layer % 2 == 0:
            mix = even_mixer(hn, ev_w_in[j], ev_w_conv[j], ev_g_v[j], ev_w_s[j], ev_b_s[j], ev_w_out[j])
        else:
            mix = odd_mixer(hn, positions, od_w_in[j], od_b_gate[j], od_g_qa[j], od_g_kva[j], od_w_q_up[j],
                            od_w_kv_up[j], od_g_q[j], od_g_k[j], od_g_mh[j], od_w_out[j])
        h = h + mix
        h = h + swiglu(rmsnorm(h, g_ffn[layer]), w_gate[layer], w_up[layer], w_down[layer])
        gate = jax.nn.sigmoid(rmsnorm(h, g_ple[layer]) @ w_ple_gate[layer])
        h = h + gate * (p[layer] @ w_ple_proj[layer])
    return h


DEPTH_2 = 1

GLA_HEADS = 4
GLA_DK_HEAD = 64
GLA_DV_HEAD = 128
GLA_DK = GLA_HEADS * GLA_DK_HEAD
GLA_DV = GLA_HEADS * GLA_DV_HEAD
GLA_GATE_RANK = 16
GLA_GATE_TAU = 16.0
GLA_CHUNK = 64
SWA_Q_HEADS = 8
SWA_KV_HEADS = 2
SWA_HEAD_DIM = 64
SWA_WINDOW = 128
SWA_BLOCK = 128
SWA_Q_DIM = SWA_Q_HEADS * SWA_HEAD_DIM
SWA_KV_DIM = SWA_KV_HEADS * SWA_HEAD_DIM
POOL_GROUPS = 4
POOL_GROUP_DIM = 128
POOL_DIM = POOL_GROUPS * POOL_GROUP_DIM
POOL_WINDOWS = (2, 4, 8, 16)
N_BRANCHES = 3
D_FF_2 = 2816
RMS_EPS = 1e-6

SPLIT_SIZES = (GLA_DK, GLA_DK, GLA_DV, GLA_GATE_RANK, GLA_DV,
               SWA_Q_DIM, SWA_KV_DIM, SWA_KV_DIM,
               POOL_DIM,
               N_BRANCHES * D_MODEL)
N_IN = sum(SPLIT_SIZES)
SPLIT_POINTS = tuple(int(v) for v in np.cumsum(SPLIT_SIZES)[:-1])


def rmsnorm_2(x, gain):
    xf = x.astype(jnp.float32)
    var = jnp.mean(xf * xf, axis=-1, keepdims=True)
    return (xf * lax.rsqrt(var + RMS_EPS) * gain.astype(jnp.float32)).astype(x.dtype)

def gla_mixer(q, k, v, gate_low, r, w_gate_up, b_gate, norm_gain):
    f32 = jnp.float32
    B, T, _ = q.shape
    nc = T // GLA_CHUNK
    logit = gate_low.astype(f32) @ w_gate_up.astype(f32) + b_gate.astype(f32)
    log_alpha = jax.nn.log_sigmoid(logit) / GLA_GATE_TAU

    def to_chunks(t, d):
        return t.astype(f32).reshape(B, nc, GLA_CHUNK, GLA_HEADS, d).transpose(1, 0, 3, 2, 4)

    qc = to_chunks(q, GLA_DK_HEAD) * (GLA_DK_HEAD ** -0.5)
    kc = to_chunks(k, GLA_DK_HEAD)
    vc = to_chunks(v, GLA_DV_HEAD)
    gc = to_chunks(log_alpha, GLA_DK_HEAD)
    causal = jnp.tril(jnp.ones((GLA_CHUNK, GLA_CHUNK), dtype=bool))

    def step(S, inp):
        qi, ki, vi, gi = inp
        b = jnp.cumsum(gi, axis=2)
        diff = b[:, :, :, None, :] - b[:, :, None, :, :]
        decay = jnp.exp(jnp.where(causal[None, None, :, :, None], diff, -jnp.inf))
        attn = jnp.einsum('bhid,bhjd,bhijd->bhij', qi, ki, decay)
        o = jnp.einsum('bhij,bhjv->bhiv', attn, vi) \
            + jnp.einsum('bhid,bhdv->bhiv', qi * jnp.exp(b), S)
        b_last = b[:, :, -1:, :]
        S_new = jnp.exp(b_last[:, :, 0, :])[..., None] * S \
            + jnp.einsum('bhjd,bhjv->bhdv', ki * jnp.exp(b_last - b), vi)
        return S_new, o

    S0 = jnp.zeros((B, GLA_HEADS, GLA_DK_HEAD, GLA_DV_HEAD), f32)
    _, o = lax.scan(step, S0, (qc, kc, vc, gc))
    o = o.transpose(1, 0, 3, 2, 4).reshape(B, T, GLA_HEADS, GLA_DV_HEAD)
    var = jnp.mean(o * o, axis=-1, keepdims=True)
    o = o * lax.rsqrt(var + RMS_EPS) * norm_gain.astype(f32).reshape(GLA_HEADS, GLA_DV_HEAD)
    o = o.reshape(B, T, GLA_DV) * jax.nn.silu(r.astype(f32))
    return o.astype(q.dtype)

def swa_mixer(q, k, v, sinks):
    f32 = jnp.float32
    B, T, _ = q.shape
    nb = T // SWA_BLOCK
    G = SWA_Q_HEADS // SWA_KV_HEADS
    qb = q.astype(f32).reshape(B, nb, SWA_BLOCK, SWA_KV_HEADS, G, SWA_HEAD_DIM) * (SWA_HEAD_DIM ** -0.5)
    kb = k.astype(f32).reshape(B, nb, SWA_BLOCK, SWA_KV_HEADS, SWA_HEAD_DIM)
    vb = v.astype(f32).reshape(B, nb, SWA_BLOCK, SWA_KV_HEADS, SWA_HEAD_DIM)

    def with_prev(t):
        prev = jnp.concatenate([jnp.zeros_like(t[:, :1]), t[:, :-1]], axis=1)
        return jnp.concatenate([prev, t], axis=2)

    kw, vw = with_prev(kb), with_prev(vb)
    s = jnp.einsum('bnqhgd,bnkhd->bnhgqk', qb, kw)
    blk = jnp.arange(nb)[:, None, None] * SWA_BLOCK
    q_pos = blk + jnp.arange(SWA_BLOCK)[None, :, None]
    k_pos = blk - SWA_BLOCK + jnp.arange(2 * SWA_BLOCK)[None, None, :]
    valid = (k_pos <= q_pos) & (q_pos - k_pos < SWA_WINDOW) & (k_pos >= 0)
    s = jnp.where(valid[None, :, None, None], s, -jnp.inf)
    sink = sinks.astype(f32).reshape(1, 1, SWA_KV_HEADS, G, 1, 1)
    m = jnp.maximum(jnp.max(s, axis=-1, keepdims=True), sink)
    p = jnp.exp(s - m)
    denom = jnp.sum(p, axis=-1, keepdims=True) + jnp.exp(sink - m)
    o = jnp.einsum('bnhgqk,bnkhd->bnqhgd', p / denom, vw)
    return o.reshape(B, T, SWA_Q_DIM).astype(q.dtype)

def pool_mixer(u, w_group, scale):
    f32 = jnp.float32
    B, T, _ = u.shape
    uf = u.astype(f32)
    cs = jnp.cumsum(uf, axis=1)
    pos = jnp.arange(1, T + 1, dtype=f32)
    means = []
    for g, w in enumerate(POOL_WINDOWS):
        cg = cs[..., g * POOL_GROUP_DIM:(g + 1) * POOL_GROUP_DIM]
        shifted = jnp.pad(cg, ((0, 0), (w, 0), (0, 0)))[:, :T]
        cnt = jnp.minimum(pos, float(w))
        means.append((cg - shifted) / cnt[None, :, None])
    pooled = jnp.stack(means, axis=2)
    d = pooled - uf.reshape(B, T, POOL_GROUPS, POOL_GROUP_DIM)
    y = jnp.einsum('btgc,gcd->btgd', d, w_group.astype(f32)).reshape(B, T, POOL_DIM)
    return (y * scale.astype(f32)).astype(u.dtype)

def conv_ffn(h, w_up, conv_w, conv_b, w_down):
    T = h.shape[1]
    up = h @ w_up
    padded = jnp.pad(up, ((0, 0), (CONV_WIDTH - 1, 0), (0, 0)))
    conv = conv_b + conv_w[0] * padded[:, 0:T]
    for i in range(1, CONV_WIDTH):
        conv = conv + conv_w[i] * padded[:, i:i + T]
    gate, val = jnp.split(conv, 2, axis=-1)
    return (jax.nn.gelu(gate, approximate=True) * val) @ w_down

def second_inputs(seed: int = 0) -> dict:
    key = jax.random.key(seed)
    ks = jax.random.split(key, 20)
    L = DEPTH_2

    def nrm(k, shape, scale):
        return jax.random.normal(k, shape, jnp.float32) * scale

    return {
        "x": nrm(ks[0], (BATCH, SEQ, D_MODEL), 1.0),
        "norm_mix_pre": 1.0 + nrm(ks[1], (L, D_MODEL), 0.05),
        "norm_mix_post": 1.0 + nrm(ks[2], (L, D_MODEL), 0.05),
        "norm_ffn_pre": 1.0 + nrm(ks[3], (L, D_MODEL), 0.05),
        "norm_ffn_post": 1.0 + nrm(ks[4], (L, D_MODEL), 0.05),
        "w_in": nrm(ks[5], (L, D_MODEL, N_IN), D_MODEL ** -0.5),
        "gla_w_gate_up": nrm(ks[6], (L, GLA_GATE_RANK, GLA_DK), GLA_GATE_RANK ** -0.5),
        "gla_b_gate": nrm(ks[7], (L, GLA_DK), 0.1),
        "gla_norm": 1.0 + nrm(ks[8], (L, GLA_DV), 0.05),
        "swa_sinks": nrm(ks[9], (L, SWA_Q_HEADS), 0.5),
        "pool_w": nrm(ks[10], (L, POOL_GROUPS, POOL_GROUP_DIM, POOL_GROUP_DIM), POOL_GROUP_DIM ** -0.5),
        "pool_scale": 1.0 + nrm(ks[11], (L, POOL_DIM), 0.05),
        "w_branch_gla": nrm(ks[12], (L, GLA_DV, D_MODEL), GLA_DV ** -0.5),
        "w_branch_swa": nrm(ks[13], (L, SWA_Q_DIM, D_MODEL), SWA_Q_DIM ** -0.5),
        "w_branch_pool": nrm(ks[14], (L, POOL_DIM, D_MODEL), POOL_DIM ** -0.5),
        "w_out": nrm(ks[15], (L, D_MODEL, D_MODEL), D_MODEL ** -0.5),
        "ffn_w_up": nrm(ks[16], (L, D_MODEL, 2 * D_FF_2), D_MODEL ** -0.5),
        "ffn_conv_w": nrm(ks[17], (L, CONV_WIDTH, 2 * D_FF_2), CONV_WIDTH ** -0.5),
        "ffn_conv_b": nrm(ks[18], (L, 2 * D_FF_2), 0.01),
        "ffn_w_down": nrm(ks[19], (L, D_FF_2, D_MODEL), D_FF_2 ** -0.5),
    }

def second_block(x, norm_mix_pre, norm_mix_post, norm_ffn_pre, norm_ffn_post, w_in,
              gla_w_gate_up, gla_b_gate, gla_norm, swa_sinks, pool_w, pool_scale,
              w_branch_gla, w_branch_swa, w_branch_pool, w_out,
              ffn_w_up, ffn_conv_w, ffn_conv_b, ffn_w_down):
    B, T, _ = x.shape
    for l in range(DEPTH_2):
        h = rmsnorm_2(x, norm_mix_pre[l])
        proj = h @ w_in[l]
        (g_q, g_k, g_v, g_low, g_r, s_q, s_k, s_v, p_u, gates) = jnp.split(proj, SPLIT_POINTS, axis=-1)
        y_a = gla_mixer(g_q, g_k, g_v, g_low, g_r, gla_w_gate_up[l], gla_b_gate[l], gla_norm[l]) @ w_branch_gla[l]
        y_b = swa_mixer(s_q, s_k, s_v, swa_sinks[l]) @ w_branch_swa[l]
        y_c = pool_mixer(p_u, pool_w[l], pool_scale[l]) @ w_branch_pool[l]
        gate = jax.nn.sigmoid(gates.reshape(B, T, N_BRANCHES, D_MODEL))
        merged = gate[:, :, 0] * y_a + gate[:, :, 1] * y_b + gate[:, :, 2] * y_c
        x = x + rmsnorm_2(merged @ w_out[l], norm_mix_post[l])
        h = rmsnorm_2(x, norm_ffn_pre[l])
        f = conv_ffn(h, ffn_w_up[l], ffn_conv_w[l], ffn_conv_b[l], ffn_w_down[l])
        x = x + rmsnorm_2(f, norm_ffn_post[l])
    return x


def setup_inputs(seed=0):
    out = dict(first_inputs(seed))
    for name, value in second_inputs(seed + 1).items():
        if name != "x":
            out[name + "_2"] = value
    return out


def reference(
    x, p, positions, g_mix, g_ffn, g_ple, ev_w_in, ev_w_conv, ev_g_v, ev_w_s, ev_b_s, ev_w_out,
    od_w_in, od_b_gate, od_g_qa, od_g_kva, od_w_q_up, od_w_kv_up, od_g_q, od_g_k, od_g_mh,
    od_w_out, w_gate, w_up, w_down, w_ple_proj, w_ple_gate, norm_mix_pre_2, norm_mix_post_2,
    norm_ffn_pre_2, norm_ffn_post_2, w_in_2, gla_w_gate_up_2, gla_b_gate_2, gla_norm_2,
    swa_sinks_2, pool_w_2, pool_scale_2, w_branch_gla_2, w_branch_swa_2, w_branch_pool_2,
    w_out_2, ffn_w_up_2, ffn_conv_w_2, ffn_conv_b_2, ffn_w_down_2,
):
    x = first_block(
        x, p, positions, g_mix, g_ffn, g_ple, ev_w_in, ev_w_conv, ev_g_v, ev_w_s, ev_b_s,
        ev_w_out, od_w_in, od_b_gate, od_g_qa, od_g_kva, od_w_q_up, od_w_kv_up, od_g_q, od_g_k,
        od_g_mh, od_w_out, w_gate, w_up, w_down, w_ple_proj, w_ple_gate,
    )
    return second_block(
        x, norm_mix_pre_2, norm_mix_post_2, norm_ffn_pre_2, norm_ffn_post_2, w_in_2,
        gla_w_gate_up_2, gla_b_gate_2, gla_norm_2, swa_sinks_2, pool_w_2, pool_scale_2,
        w_branch_gla_2, w_branch_swa_2, w_branch_pool_2, w_out_2, ffn_w_up_2, ffn_conv_w_2,
        ffn_conv_b_2, ffn_w_down_2,
    )


_drawn_inputs = setup_inputs


def setup_inputs(seed=0):
    import zlib

    import numpy as np

    out = dict(_drawn_inputs(seed))
    spreads = {}
    factors = {'g_ple': 3.712,
     'ev_g_v': 3.423,
     'od_g_qa': 8.0,
     'od_g_kva': 7.628,
     'od_g_q': 8.0,
     'od_g_k': 8.0,
     'od_g_mh': 17.177,
     'gla_b_gate_2': 4.566,
     'gla_norm_2': 29.222,
     'swa_sinks_2': 64.0,
     'ffn_conv_b_2': 24.192,
     'norm_mix_pre_2': 3.241,
     'norm_mix_post_2': 6.798,
     'norm_ffn_pre_2': 4.791,
     'norm_ffn_post_2': 7.002,
     'gla_w_gate_up_2': 2.787,
     'pool_scale_2': 8.0,
     'w_branch_swa_2': 3.461}
    for name, (base, spread) in spreads.items():
        noise = np.random.default_rng([zlib.crc32(name.encode()), seed]).standard_normal(out[name].shape)
        drawn = base * np.exp(spread * noise) if base else spread * noise
        out[name] = __import__('jax').numpy.asarray(drawn.astype(out[name].dtype))
    for name, factor in factors.items():
        out[name] = (out[name] * factor).astype(out[name].dtype)
    return out
```

```python
from contextlib import ExitStack

import concourse.bass as bass
from concourse import mybir

F32 = mybir.dt.float32
I32 = mybir.dt.int32
U32 = mybir.dt.uint32
ALU = mybir.AluOpType
ACT = mybir.ActivationFunctionType
AX_X = mybir.AxisListType.X

P = 128
T = 512
NT = T // P
D = 1024
DC = D // P
EPS = 1e-6
NEG = -1e30
FF = 2816
FC = FF // P
SLOTS = 4
SLOT = 12 * P
BANKS = 4
LNEXP = "natural_log_exp_and_others"
FFN_UNITS = 2 * FC + 2 * DC
FFN_OUTS = 2 * FC + DC

STAGES = [
    ("norm_mix0", 0, 0, 2),
    ("even_in", 20, 20, 4),
    ("even_out", 8, 8, 0),
    ("norm_ffn0", 0, 0, 2),
    ("ffn0", FFN_UNITS, FFN_OUTS, 0),
    ("norm_ple0", 0, 0, 2),
    ("ple0", 8, 16, 0),
    ("norm_mix1", 0, 0, 2),
    ("odd_in", 17, 17, 2),
    ("mlstm", 0, 0, 69),
    ("mla_up", 5, 16, 0),
    ("mla", 0, 0, 88),
    ("odd_out", 8, 8, 0),
    ("norm_ffn1", 0, 0, 2),
    ("ffn1", FFN_UNITS, FFN_OUTS, 0),
    ("norm_ple1", 0, 0, 2),
    ("ple1", 8, 16, 0),
    ("norm_mix2", 0, 0, 2),
    ("gla_in", 12, 12, 3),
    ("gla", 0, 0, 48),
    ("swa", 6, 6, 36),
    ("pool", 5, 8, 0),
    ("merge", 24, 48, 0),
    ("block_out", 8, 8, 0),
    ("norm_post", 0, 0, 2),
    ("norm_ffn2", 0, 0, 2),
    ("convffn", FFN_UNITS, FFN_OUTS, 0),
    ("norm_last", 0, 0, 2),
]

COLS = {}
COLS_N = 0
for _name, _n in (
    ("g_mix0", 8), ("g_ffn0", 8), ("g_ple0", 8), ("g_mix1", 8), ("g_ffn1", 8), ("g_ple1", 8),
    ("mix_pre", 8), ("mix_post", 8), ("ffn_pre", 8), ("ffn_post", 8),
    ("w_conv", 12), ("g_qa", 3), ("g_kva", 2), ("gla_b", 2), ("pool_scale", 4),
    ("cw0", 44), ("cw1", 44), ("cw2", 44), ("cb", 44),
):
    COLS[_name] = COLS_N
    COLS_N += _n

ROWS = {}
ROWS_N = 0
for _name, _n in (("g_v", 512), ("g_q", 96), ("g_k", 96), ("b_gate", 8), ("g_mh", 512), ("gla_norm", 512), ("sinks", 8)):
    ROWS[_name] = ROWS_N
    ROWS_N += _n


def stage_bases():
    u = g = m = 0
    base = {}
    for name, units, outs, works in STAGES:
        base[name] = (u, g, m)
        u, g, m = u + units, g + outs, m + works
    return base, u


class Turns:

    def __init__(self, banks, full, done):
        self.banks, self.full, self.done = banks, full, done

    def bank(self, n):
        return self.banks[n % BANKS]

    def wait_full(self, eng, n, more=0):
        eng.wait_ge(self.full[n % BANKS], more + n // BANKS + 1)

    def wait_done(self, eng, n, more=0):
        eng.wait_ge(self.done[n % BANKS], more + n // BANKS + 1)

    def wait_free(self, eng, n, more=0):
        if n >= BANKS:
            eng.wait_ge(self.done[n % BANKS], more + n // BANKS)


class Steps:

    def __init__(self, eng, sem):
        self.eng, self.sem, self.n = eng, sem, 0

    def did(self, ins):
        ins.then_inc(self.sem, 1)
        self.n = self.n + 1

    def settle(self):
        self.eng.wait_ge(self.sem, self.n)


RSQRTS = {"norm_mix0": 1, "norm_ffn0": 3, "norm_ple0": 4, "norm_mix1": 5, "norm_ffn1": 10, "norm_ple1": 11,
          "norm_mix2": 12, "norm_post": 14, "norm_ffn2": 15, "norm_last": 16}
DUMP = None
MLSTM_HEADS = 4
MLSTM_BLOCKS = MLSTM_HEADS * NT
MLA_HEADS = 8
GLA_HEADS = 4
LEVELS = 8
SWA_PAIRS = 4
SWA_BLOCKS = SWA_PAIRS * NT
MLA_BLOCKS = MLA_HEADS * NT
PI = 3.141592653589793
TWO_PI = 2 * PI
ROUND = 12582912.0
TURN_PARTS = (6.28125, 0.0019350051879882812, 3.0199159795074593e-07)


def on(name):
    return any(s[0] == name for s in STAGES)


def ffn_units(up, down):
    return [("out", up, i) for i in range(2 * FC)] + [(("half", "out")[i % 2], down, i) for i in range(2 * DC)]


def fm(array, n, at=0):
    return [("out", array, at + i) for i in range(n)]


def tm(array, at=0):
    return [(("part", "part", "part", "tokens")[i], array, at + i) for i in range(4)]


UNITS = {
    "even_in": fm("w_even", 16) + tm("w_even", 16),
    "even_out": fm("w_even_out", 8),
    "ffn0": ffn_units("w_up0", "w_down0"),
    "ple0": [("two", "w_ple0", i) for i in range(8)],
    "odd_in": fm("w_odd", 9) + tm("w_odd", 9) + tm("w_odd", 13),
    "mla_up": [("hold", "w_q_up", 0), ("hold", "w_q_up", 1), ("held", "w_q_up", 2), ("hold", "w_kv_up", 0),
               ("held", "w_kv_up", 1)],
    "odd_out": fm("w_odd_out", 8),
    "ffn1": ffn_units("w_up1", "w_down1"),
    "ple1": [("two", "w_ple1", i) for i in range(8)],
    "gla_in": fm("w_gla", 4) + tm("w_gla", 4) + tm("w_gla", 8),
    "swa": fm("w_swa", 6),
    "pool": fm("w_pool", 4) + [("four", "w_group", 0)],
    "merge": [("two", "w_merge", i) for i in range(24)],
    "block_out": fm("w_block_out", 8),
    "convffn": ffn_units("w_up2", "w_down2"),
}
BEFORE = {"norm_ffn0": "even_out", "norm_ple0": "ffn0", "norm_mix1": "ple0", "norm_ffn1": "odd_out",
          "norm_ple1": "ffn1", "norm_mix2": "ple1", "norm_post": "block_out", "norm_last": "convffn"}


def gla_order():
    return ([("level", n, i) for n in range(LEVELS) for i in range(NT)]
            + [(part, head) for head in range(GLA_HEADS) for part in ("far_a", "far_b")]
            + [("o", i) for i in range(NT)] + [("y", head) for head in range(GLA_HEADS)])


def swa_order():
    order = []
    for n in range(SWA_BLOCKS + 1):
        if n < SWA_BLOCKS:
            order.append(("scores", n))
        if n:
            order.append(("turned", n - 1))
        if n and n % NT == 0:
            order.append(("out", n // NT - 1))
    return order


def mlstm_order():
    order = [("sums", 0)]
    for n in range(MLSTM_BLOCKS + 1):
        if n < MLSTM_BLOCKS:
            order += [("decay", n), ("scores", n)]
        if n:
            order += [("turned", n - 1), ("out", n - 1)]
    return order + [("y", head) for head in range(MLSTM_HEADS)]


def mla_order():
    order = [("q", 0), ("k", 0)]
    for n in range(MLA_BLOCKS + 1):
        if n < MLA_BLOCKS:
            order.append(("scores", n))
        if n:
            order.append(("turned", n - 1))
        if n and n % NT == 0:
            order.append(("out", n // NT - 1))
        if n % NT == 1 and n // NT + 1 < MLA_HEADS:
            order += [("q", n // NT + 1), ("k", n // NT + 1)]
    return order


def build(nc, a, out):
    base, n_units = stage_bases()

    with ExitStack() as ctx:
        def sb(name, shape, dt=F32):
            return ctx.enter_context(nc.sbuf_tensor("s_" + name, shape, dt))

        def sem(name):
            return ctx.enter_context(nc.semaphore(name))

        def sems(name, n):
            return [sem(f"{name}{i}") for i in range(n)]

        h = sb("h", [P, DC, T])
        hn = sb("hn", [P, DC, T])
        ring = sb("ring", [P, SLOTS, SLOT])
        arena = sb("arena", [P, 26624])
        tmp = sb("tmp", [P, 4, T])
        cols = sb("cols", [P, COLS_N])
        rows = sb("rows", [P, ROWS_N])
        ident = sb("ident", [P, P])
        ones = sb("ones", [P, P])
        upto = sb("upto", [P, P])
        below = sb("below", [P, P])
        neg_after = sb("neg_after", [P, P])
        neg_until = sb("neg_until", [P, P])
        ms = sb("ms", [P, 64])
        ln_ms = sb("ln_ms", [P, 64])
        rs0 = sb("rs0", [P, 64])
        rt = sb("rt", [P, 2, 64])
        rstd = sb("rstd", [P, 64])
        rstd_rows = sb("rstd_rows", [P, T])
        pT = sb("pT", [P, 2, T])
        stat = sb("stat", [P, 64])

        def region(at, *shape):
            n = 1
            for s in shape:
                n *= s
            v = arena[:, at:at + n]
            if len(shape) == 2:
                v = v.rearrange("p (a b) -> p a b", a=shape[0])
            if len(shape) == 3:
                v = v.rearrange("p (a b c) -> p a b c", a=shape[0], b=shape[1])
            return v, at + n

        act, _ = region(0, FC, T)
        y, _ = region(0, DC, T)
        sq, _ = region(22528, DC, T)

        ws, at = region(8192, 8, P)
        z_pad, at = region(at, 2, 2 + T)
        conv, at = region(at, 2, T)
        u_g, at = region(at, 4, T)
        v_t, at = region(at, NT, 512)
        v_sq, at = region(at, 2, 512)
        b_row = sb("b_row", [1, 8, P])
        lat, at = region(8192, 5, T)
        mq, at = region(at, 2, T)
        mk, at = region(at, 2, T)
        mv, at = region(at, NT, 512)
        mo, at = region(at, NT, 512)
        lat_sq, _ = region(at, 5, T)
        rdiag, at = region(at, MLSTM_BLOCKS, P)
        dec, at = region(at, 2, T)
        sT, at = region(at, 2, T)
        hv, at = region(4096, NT, 512)
        hv_sq, _ = region(6144, NT, 512)
        q_t, at = region(8192 + 5 * T, NT, 768)
        k_t, at = region(at, NT, 768)
        kv_t, at = region(at, NT, 1024)
        qT, at = region(at, 2, T)
        kT, at = region(at, 2, T)
        prob, at = region(at, 2, T)
        probT, at = region(at, 4, T)
        probT2, _ = region(8192, 4, T)
        qk_sq, _ = region(at - 4 * T, 2, 1024)
        turn_tmp, _ = region(at - 4 * T, 4, T)
        gq, at = region(0, 2, T)
        gk, at = region(at, 2, T)
        gv, at = region(at, NT, 512)
        gr, at = region(at, NT, 512)
        cum, at = region(at, 2, T)
        branch, at = region(8192, 12, T)
        pair, at = region(at, 2, 2, T)
        near, at = region(at, NT, 512)
        far, at = region(at, GLA_HEADS, 768)
        kd, at = region(at, 2, T)
        qd, at = region(at, 2, T)
        go, at = region(at, NT, 512)
        go_sq = pair.rearrange("p a b c -> p (a b) c")
        logit = near[:, 0:2, :]
        log_p = near[:, 2:4, :]
        sqT, at = region(0, 4, T)
        skT, at = region(at, 1, T)
        sv, at = region(at, NT, P)
        sprob, at = region(at, 2, T)
        sprobT, at = region(at, NT, T)
        pu, at = region(14336, 4, 16 + T)
        psum_a, at = region(at, 2, 16 + T)
        pd, at = region(at, 4, T)
        o_buf = sq
        w_low = sb("w_low", [P, DC, 16])
        w_gate_up = sb("w_gate_up", [16, 256])
        g_low = sb("g_low", [16, T])
        level_mask = sb("level_mask", [P, LEVELS - 1, P])
        tot16 = sb("tot16", [P, 2, NT])
        exp_tot = sb("exp_tot", [P, 2, NT])
        neg_sink = sb("neg_sink", [P, 8])
        sink_m = sb("sink_m", [P, 32])
        inv_count = sb("inv_count", [P, 16])
        GW = {k: base["gla"][2] + i for i, k in enumerate(gla_order())} if on("gla") else {}
        SW = {k: base["swa"][2] + i for i, k in enumerate(swa_order())} if on("swa") else {}
        w_small = sb("w_small", [P, DC, 40])
        gates = sb("gates", [P, NT, 8])
        k_pe = sb("k_pe", [P, NT, 32])
        lat_ss = sb("lat_ss", [P, 8])
        lat_rs = sb("lat_rs", [P, 8])
        pos_i = sb("pos_i", [P, NT], I32)
        inv_freq = sb("inv_freq", [P, 16])
        angle = sb("angle", [P, 5, NT * 16])
        cos_sin = sb("cos_sin", [P, 2, NT * 16])
        lf = sb("lf", [P, NT, 4])
        gl = sb("gl", [P, 4, 16])
        neg_sum = sb("neg_sum", [P, 16])
        neg_m = sb("neg_m", [P, 32])
        exp_m = sb("exp_m", [P, 16])
        den = sb("den", [P, 32])
        rden = sb("rden", [P, 32])
        MW = {k: base["mlstm"][2] + i for i, k in enumerate(mlstm_order())} if on("mlstm") else {}
        AW = {k: base["mla"][2] + i for i, k in enumerate(mla_order())} if on("mla") else {}
        N_TABLES = 8
        N_MASKS = 1 + 3 * (LEVELS - 1)
        N_CONSTS = 12

        def col(name, c=0, n=1):
            return cols[:, COLS[name] + c:COLS[name] + c + n]

        def row(name, at, n):
            return rows[:, ROWS[name] + at:ROWS[name] + at + n]

        stream = Turns([ctx.enter_context(nc.psum_tensor(f"stream_bank{i}", [P, 512], F32)) for i in range(BANKS)],
                       sems("stream_full", BANKS), sems("stream_done", BANKS))
        work = Turns([ctx.enter_context(nc.psum_tensor(f"work_bank{i}", [P, 512], F32)) for i in range(BANKS)],
                     sems("work_full", BANKS), sems("work_done", BANKS))
        slot_loaded = sems("slot_loaded", SLOTS)
        x_loaded = sem("x_loaded")
        tables_loaded = sem("tables_loaded")
        p_loaded = sem("p_loaded")
        consts_ready = sem("consts_ready")
        sq_ready = sem("sq_ready")
        ms_ready = sem("ms_ready")
        rs_guessed = sem("rs_guessed")
        rstd_ready = sem("rstd_ready")
        hn_ready = sem("hn_ready")
        k_units = sem("k_units")
        down_half = sem("down_half")
        act_steps = sem("act_steps")
        dve_steps = sem("dve_steps")
        out_stored = sem("out_stored")
        conv_in = sem("conv_in")
        v_gelu = sem("v_gelu")
        v_square = sem("v_square")
        v_ready = sem("v_ready")
        lat_squared = sem("lat_squared")
        gates_ready = sem("gates_ready")
        log_ready = sem("log_ready")
        lf_ready = sem("lf_ready")
        rdiag_ready = sem("rdiag_ready")
        m_ready = sem("m_ready")
        exp_m_ready = sem("exp_m_ready")
        rden_ready = sem("rden_ready")
        hv_squared = sem("hv_squared")
        hv_ready = sem("hv_ready")
        lat_rs_ready = sem("lat_rs_ready")
        squared = sem("squared")
        summed = sem("summed")
        qk_ready = sem("qk_ready")
        prob_ready = sem("prob_ready")
        angle_ready = sem("angle_ready")
        turned_ready = sem("turned_ready")
        freq_ready = sem("freq_ready")
        logit_logged = sem("logit_logged")
        exponent_ready = sem("exponent_ready")
        decay_ready = sem("decay_ready")
        pair_ready = sem("pair_ready")
        near_ready = sem("near_ready")
        masks_ready = sem("masks_ready")
        far_exp = sem("far_exp")
        far_ready = sem("far_ready")
        go_squared = sem("go_squared")
        go_ready = sem("go_ready")
        sink_ready = sem("sink_ready")
        sprob_ready = sem("sprob_ready")
        pad_ready = sem("pad_ready")
        pd_ready = sem("pd_ready")
        h_updated = sem("h_updated")
        conv_started = sem("conv_started")
        gelu_ready = sem("gelu_ready")
        act_ready = sem("act_ready")

        norm_no = {n: i for i, n in enumerate(s[0] for s in STAGES if s[0].startswith("norm"))}
        hn_no = {n: i for i, n in enumerate(n for n in norm_no if n not in ("norm_post", "norm_last"))}

        def h_out(stage, c):
            g = base[stage][1]
            if "ffn" in stage:
                return g + 2 * FC + c
            return g + (2 * c + 1 if stage.startswith("ple") else c)

        def h_ready(eng, norm, c):
            if norm == "norm_ffn2":
                eng.wait_ge(h_updated, c + 1)
            elif norm == "norm_mix0":
                eng.wait_ge(x_loaded, 16)
            else:
                stream.wait_done(eng, h_out(BEFORE[norm], c))

        freed, weights = [], []
        parts = halves = 0
        for name, units, _, _ in STAGES:
            g = base[name][1]
            for kind, array, i in UNITS.get(name, []):
                weights.append((array, i))
                if kind == "part":
                    parts += 1
                    freed.append((k_units, parts))
                    continue
                if kind == "half":
                    halves += 1
                    freed.append((down_half, halves))
                    continue
                if kind == "hold":
                    freed.append((stream.full[(g + 7) % BANKS], (g + 7) // BANKS + 1))
                    continue
                g += {"out": 1, "two": 2, "tokens": NT, "held": 8, "four": 4}[kind]
                freed.append((stream.full[(g - 1) % BANKS], (g - 1) // BANKS + 1))
        assert len(weights) == n_units, (len(weights), n_units)

        def wait_unit(eng, u, more=0):
            eng.wait_ge(slot_loaded[u % SLOTS], 16 * (more + u // SLOTS + 1))

        block = ctx.enter_context(nc.Block())

        def final(sp, c):
            if on("norm_last"):
                sp.wait_ge(h_updated, DC + c + 1)
                return
            if DUMP is None:
                stream.wait_done(sp, h_out(STAGES[-1][0], c))
                return
            for r in (stream, work):
                n = sum(s[2 if r is stream else 3] for s in STAGES)
                for q in range(n - BANKS, n):
                    r.wait_done(sp, q)

        @block.sync
        def _(sp):
            sp.dma_start(h[:], a["x"]).then_inc(x_loaded, 16)
            for u, (array, i) in enumerate(weights):
                if array == "w_ple1" and i == 0:
                    stream.wait_full(sp, base["ple0"][1] + 15)
                    sp.dma_start(pT[:], a["p1"]).then_inc(p_loaded, 16)
                if u >= SLOTS:
                    sp.wait_ge(*freed[u - SLOTS])
                n = a[array].shape[2]
                sp.dma_start(ring[:, u % SLOTS, 0:n], a[array][i]).then_inc(slot_loaded[u % SLOTS], 16)
            for c in range(DC):
                final(sp, c)
                sp.dma_start(out[:, c, :], (h if DUMP is None else y)[:, c, :]).then_inc(out_stored, 16)
            sp.wait_ge(p_loaded, 32 if on("ple1") else 16)
            sp.wait_ge(turned_ready, 1)
            sp.wait_ge(out_stored, 16 * DC)

        @block.gpsimd
        def _(pool):
            steps = Steps(pool, consts_ready)
            for t, v in ((ident, 0.0), (ones, 1.0), (upto, 1.0), (below, 1.0), (neg_after, 0.0), (neg_until, 0.0)):
                steps.did(nc.gpsimd.memset(t[:], v))
            steps.settle()
            for t, op, fill, at, step, mult in (
                (ident, ALU.not_equal, 1.0, 0, -1, 1), (upto, ALU.is_ge, 0.0, 0, 1, -1),
                (below, ALU.is_ge, 0.0, -1, -1, 1), (neg_after, ALU.is_ge, NEG, 0, -1, 1),
                (neg_until, ALU.is_ge, NEG, -1, 1, -1),
            ):
                steps.did(nc.gpsimd.affine_select(out=t[:], in_=t[:], compare_op=op, fill=fill, base=at,
                                                  pattern=[[step, P]], channel_multiplier=mult))
            for j in range(16):
                last = nc.gpsimd.memset(inv_freq[:, j:j + 1], float(10000.0 ** (-j / 16)))
            last.then_inc(freq_ready, 1)
            for j in range(16):
                last = nc.gpsimd.memset(inv_count[:, j:j + 1], 1.0 / (j + 1))
            last.then_inc(freq_ready, 1)
            masks = Steps(pool, masks_ready)
            masks.did(nc.gpsimd.memset(level_mask[:], 0.0))
            for n in range(1, LEVELS):
                s = 1 << (n - 1)
                v = level_mask[:, n - 1, :].rearrange("p (n two s) -> p n two s", two=2, s=s)[:, :, 1, :]
                masks.settle()
                masks.did(nc.gpsimd.memset(v, 1.0))
                masks.settle()
                masks.did(nc.gpsimd.affine_select(out=v, in_=v, compare_op=ALU.is_ge, fill=0.0, base=0,
                                                  pattern=[[-2 * s, P // (2 * s)], [0, s]], channel_multiplier=1))
                masks.settle()
                masks.did(nc.gpsimd.affine_select(out=v, in_=v, compare_op=ALU.is_ge, fill=0.0, base=s - 1,
                                                  pattern=[[2 * s, P // (2 * s)], [0, s]], channel_multiplier=-1))
            pool.wait_ge(tables_loaded, 16 * N_TABLES)
            steps.did(nc.gpsimd.affine_select(out=ws, in_=ws, compare_op=ALU.is_ge, fill=0.0, base=0,
                                              pattern=[[0, 8], [1, P]], channel_multiplier=-1))

        @block.tensor
        def _(pe):
            def norm(stage):
                k, m = norm_no[stage], base[stage][2]
                squares = sq if stage not in ("norm_post", "norm_last") else hn
                work.wait_free(pe, m)
                for c in range(DC):
                    pe.wait_ge(sq_ready, DC * k + c + 1)
                    for t in range(NT):
                        mm = nc.tensor.matmul(work.bank(m)[:, t:t + 1], squares[:, c, t * P:(t + 1) * P], ones[:, 0:1],
                                              start=(c == 0 and t == 0), stop=(c == DC - 1), skip_group_check=True)
                mm.then_inc(work.full[m % BANKS], 1)
                work.wait_free(pe, m + 1)
                pe.wait_ge(rstd_ready, RSQRTS[stage])
                for t in range(NT):
                    mm = nc.tensor.matmul(work.bank(m + 1)[:, t * P:(t + 1) * P],
                                          rstd[:, t:t + 1].to_broadcast([P, P]), ident[:], start=True, stop=True)
                mm.then_inc(work.full[(m + 1) % BANKS], 1)

            def feature_out(u, g, x, k_tiles, at=0, more_u=0, more_g=0, wait_x=None, signal=True, start=True, stop=True, k0=0):
                wait_unit(pe, u, more_u)
                for k in range(k_tiles):
                    if wait_x is not None:
                        wait_x(k)
                    mm = nc.tensor.matmul(stream.bank(g)[:], ring[:, u % SLOTS, at + k * P:at + (k + 1) * P], x(k0 + k),
                                          start=(start and k == 0), stop=(stop and k == k_tiles - 1))
                return mm

            def hn_in(k):
                return hn[:, k, :]

            def y_in(k):
                return y[:, k, :]

            def token_outs(u, g, x, per_unit):
                for t in range(NT):
                    stream.wait_free(pe, g + t)
                for i in range(4):
                    wait_unit(pe, u + i)
                    for k in range(2):
                        for t in range(NT):
                            mm = nc.tensor.matmul(stream.bank(g + t)[:], x(2 * i + k)[:, t * P:(t + 1) * P],
                                                  ring[:, (u + i) % SLOTS, k * 512:(k + 1) * 512],
                                                  start=(i == 0 and k == 0), stop=(i == 3 and k == 1))
                            if i == 3 and k == 1:
                                mm.then_inc(stream.full[(g + t) % BANKS], 1)
                    if i < 3:
                        mm.then_inc(k_units, 1)

            def hn_wait(stage):
                return lambda k: pe.wait_ge(hn_ready, DC * hn_no[stage] + k + 1)

            def simple_outs(u, g, n, x, wait_x):
                for i in range(n):
                    stream.wait_free(pe, g + i)
                    feature_out(u + i, g + i, x, DC, wait_x=wait_x if i == 0 else None).then_inc(
                        stream.full[(g + i) % BANKS], 1)

            def even_in():
                u, g, m = base["even_in"]
                simple_outs(u, g, 16, hn_in, hn_wait("norm_mix0"))
                token_outs(u + 16, g + 16, hn_in, 2)
                pe.wait_ge(consts_ready, N_CONSTS)
                for hp in range(4):
                    work.wait_free(pe, m + hp)
                    for n in range(NT):
                        if hp == 0:
                            pe.wait_ge(v_ready, n + 1)
                        for e in range(2):
                            head = 2 * hp + e
                            o = work.bank(m + hp)[64 * e:64 * e + 64, n * P:(n + 1) * P]
                            nc.tensor.matmul(o, v_t[:, n, head * 64:head * 64 + 64], ws[:, head, :], start=True, stop=False)
                            mm = nc.tensor.matmul(o, ones[0:1, 0:64], b_row[0:1, head, :], start=False, stop=True)
                    mm.then_inc(work.full[(m + hp) % BANKS], 1)

            def ffn(stage, norm_stage):
                u, g, _ = base[stage]
                wait_hn = hn_wait(norm_stage)

                def up(i, first):
                    for j in range(4):
                        pe.wait_ge(stream.done[(g + j) % BANKS], i + (g + j) // BANKS)
                        feature_out(u + j, g + j, hn_in, DC, more_u=i,
                                    wait_x=wait_hn if first and j == 0 else None).then_inc(stream.full[(g + j) % BANKS], 1)

                up(0, True)
                with pe.Fori(1, 2 * FC // 4) as i:
                    up(i, False)
                u, g2 = u + 2 * FC, g + 2 * FC

                def act_wait(k):
                    if stage == "convffn":
                        pe.wait_ge(act_ready, k + 1)
                    else:
                        stream.wait_done(pe, g + 2 * k + 1)

                def down(i, first):
                    for j in range(4):
                        pe.wait_ge(stream.done[(g2 + j) % BANKS], i + (g2 + j) // BANKS)
                        for half in range(2):
                            ux = u + 2 * j + half
                            wait_unit(pe, ux, 2 * i)
                            for k in range(11):
                                if first and j == 0:
                                    act_wait(11 * half + k)
                                mm = nc.tensor.matmul(stream.bank(g2 + j)[:], ring[:, ux % SLOTS, k * P:(k + 1) * P],
                                                      act[:, 11 * half + k, :], start=(half == 0 and k == 0),
                                                      stop=(half == 1 and k == 10))
                            mm.then_inc(stream.full[(g2 + j) % BANKS] if half else down_half, 1)

                down(0, True)
                down(1, False)

            def ple(stage, norm_stage, layer):
                u, g, _ = base[stage]
                wait_hn = hn_wait(norm_stage)
                pe.wait_ge(p_loaded, 16 * (layer + 1))
                for c in range(DC):
                    stream.wait_free(pe, g + 2 * c)
                    feature_out(u + c, g + 2 * c, hn_in, DC, wait_x=wait_hn if c == 0 else None).then_inc(
                        stream.full[(g + 2 * c) % BANKS], 1)
                    stream.wait_free(pe, g + 2 * c + 1)
                    for k in range(2):
                        mm = nc.tensor.matmul(stream.bank(g + 2 * c + 1)[:], ring[:, (u + c) % SLOTS, (8 + k) * P:(9 + k) * P],
                                              pT[:, k, :], start=(k == 0), stop=(k == 1))
                    mm.then_inc(stream.full[(g + 2 * c + 1) % BANKS], 1)

            def odd_in():
                u, g, m = base["odd_in"]
                simple_outs(u, g, 9, hn_in, hn_wait("norm_mix1"))
                token_outs(u + 9, g + 9, hn_in, 2)
                token_outs(u + 13, g + 13, hn_in, 2)
                work.wait_free(pe, m)
                for t in range(NT):
                    for k in range(DC):
                        mm = nc.tensor.matmul(work.bank(m)[:, 40 * t:40 * t + 40], hn[:, k, t * P:(t + 1) * P],
                                              w_small[:, k, :], start=(k == 0), stop=(k == DC - 1))
                mm.then_inc(work.full[m % BANKS], 1)
                work.wait_free(pe, m + 1)
                pe.wait_ge(lat_squared, 5)
                for t in range(NT):
                    for c in range(5):
                        o = t + (NT if c >= 3 else 0)
                        mm = nc.tensor.matmul(work.bank(m + 1)[:, o:o + 1], lat_sq[:, c, t * P:(t + 1) * P], ones[:, 0:1],
                                              start=c in (0, 3), stop=c in (2, 4))
                mm.then_inc(work.full[(m + 1) % BANKS], 1)

            def mlstm():
                m = MW["sums", 0]
                work.wait_free(pe, m)
                pe.wait_ge(lf_ready, 1)
                for i in range(NT):
                    for k in range(i + 1):
                        mm = nc.tensor.matmul(work.bank(m)[:, 4 * i:4 * i + 4], (upto if k == i else ones)[:], lf[:, k, :],
                                              start=(k == 0), stop=(k == i))
                mm.then_inc(work.full[m % BANKS], 1)
                for n in range(MLSTM_BLOCKS + 1):
                    if n < MLSTM_BLOCKS:
                        head, i = divmod(n, NT)
                        m = MW["decay", n]
                        work.wait_free(pe, m)
                        pe.wait_ge(rdiag_ready, n + 1)
                        o = work.bank(m)
                        for k in range(i, -1, -1):
                            lhs = (upto if k == i else ones)[:]
                            nc.tensor.matmul(o[:, k * P:(k + 1) * P], lhs, rdiag[:, head * NT + k, :], start=(k == i), stop=(k < i),
                                             skip_group_check=True)
                            if k:
                                nc.tensor.matmul(o[:, 0:k * P], lhs, lf[:, k, head:head + 1].to_broadcast([P, k * P]),
                                                 start=False, stop=False, skip_group_check=True)
                        nc.tensor.matmul(o[:, i * P:(i + 1) * P], ident[:], neg_after[:], start=False, stop=True,
                                         skip_group_check=True).then_inc(work.full[m % BANKS], 1)
                        m = MW["scores", n]
                        work.wait_free(pe, m)
                        if n == 0:
                            for j in range(4):
                                stream.wait_done(pe, base["odd_in"][1] + 5 + j)
                        q = 64 * (head % 2)
                        nc.tensor.matmul(work.bank(m)[:, 0:(i + 1) * P], mq[q:q + 64, head // 2, i * P:(i + 1) * P],
                                         mk[q:q + 64, head // 2, 0:(i + 1) * P], start=True, stop=True).then_inc(
                            work.full[m % BANKS], 1)
                    if n:
                        n1 = n - 1
                        head, i = divmod(n1, NT)
                        m = MW["turned", n1]
                        work.wait_free(pe, m)
                        work.wait_done(pe, MW["scores", n1])
                        for j in range(i + 1):
                            mm = nc.tensor.transpose(work.bank(m)[:, j * P:(j + 1) * P], dec[:, n1 % 2, j * P:(j + 1) * P], ident[:])
                        mm.then_inc(work.full[m % BANKS], 1)
                        m = MW["out", n1]
                        work.wait_free(pe, m)
                        work.wait_done(pe, MW["turned", n1])
                        if n1 == 0:
                            for j in range(NT):
                                stream.wait_done(pe, base["odd_in"][1] + 9 + j)
                        for j in range(i + 1):
                            mm = nc.tensor.matmul(work.bank(m)[:, 0:P], sT[:, n1 % 2, j * P:(j + 1) * P],
                                                  mv[:, j, head * P:(head + 1) * P], start=(j == 0), stop=(j == i))
                        mm.then_inc(work.full[m % BANKS], 1)
                for head in range(MLSTM_HEADS):
                    m = MW["y", head]
                    work.wait_free(pe, m)
                    pe.wait_ge(hv_ready, NT)
                    for t in range(NT):
                        mm = nc.tensor.transpose(work.bank(m)[:, t * P:(t + 1) * P], hv[:, t, head * P:(head + 1) * P], ident[:])
                    mm.then_inc(work.full[m % BANKS], 1)

            def mla_up():
                u, g, _ = base["mla_up"]
                for k in range(3):
                    wait_unit(pe, u + k)
                for n in range(2 * NT):
                    t, half = divmod(n, 2)
                    stream.wait_free(pe, g + n)
                    for k in range(3):
                        mm = nc.tensor.matmul(stream.bank(g + n)[:, 0:384], lat[:, k, t * P:(t + 1) * P],
                                              ring[:, (u + k) % SLOTS, half * 384:half * 384 + 384], start=(k == 0), stop=(k == 2))
                    mm.then_inc(stream.full[(g + n) % BANKS], 1)
                u, g = u + 3, g + 8
                for k in range(2):
                    wait_unit(pe, u + k)
                for n in range(2 * NT):
                    t, half = divmod(n, 2)
                    stream.wait_free(pe, g + n)
                    for k in range(2):
                        mm = nc.tensor.matmul(stream.bank(g + n)[:], lat[:, 3 + k, t * P:(t + 1) * P],
                                              ring[:, (u + k) % SLOTS, half * 512:half * 512 + 512], start=(k == 0), stop=(k == 1))
                    mm.then_inc(stream.full[(g + n) % BANKS], 1)

            def mla():
                def turn(name, src, head):
                    m = AW[name, head]
                    work.wait_free(pe, m)
                    for t in range(NT):
                        mm = nc.tensor.transpose(work.bank(m)[0:96, t * P:(t + 1) * P], src[:, t, head * 96:head * 96 + 96], ident[:])
                    mm.then_inc(work.full[m % BANKS], 1)

                pe.wait_ge(qk_ready, 1)
                turn("q", q_t, 0)
                turn("k", k_t, 0)
                for n in range(MLA_BLOCKS + 1):
                    if n < MLA_BLOCKS:
                        head, i = divmod(n, NT)
                        m = AW["scores", n]
                        work.wait_free(pe, m)
                        if i == 0:
                            work.wait_done(pe, AW["q", head])
                            work.wait_done(pe, AW["k", head])
                        nc.tensor.matmul(work.bank(m)[:, 0:(i + 1) * P], qT[0:96, head % 2, i * P:(i + 1) * P],
                                         kT[0:96, head % 2, 0:(i + 1) * P], start=True, stop=True, skip_group_check=True)
                        nc.tensor.matmul(work.bank(m)[:, i * P:(i + 1) * P], ident[:], neg_after[:], start=False, stop=True,
                                         skip_group_check=True).then_inc(work.full[m % BANKS], 1)
                    if n:
                        head, i = divmod(n - 1, NT)
                        m = AW["turned", n - 1]
                        work.wait_free(pe, m)
                        pe.wait_ge(prob_ready, n)
                        for j in range(i + 1):
                            mm = nc.tensor.transpose(work.bank(m)[:, j * P:(j + 1) * P], prob[:, (n - 1) % 2, j * P:(j + 1) * P], ident[:])
                        mm.then_inc(work.full[m % BANKS], 1)
                    if n and n % NT == 0:
                        head = n // NT - 1
                        m = AW["out", head]
                        work.wait_free(pe, m)
                        work.wait_done(pe, AW["turned", n - 1])
                        q = 64 * (head % 2)
                        pt = (probT, probT2)[head % 2]
                        for j in range(NT):
                            mm = nc.tensor.matmul(work.bank(m)[q:q + 64, j * P:T], kv_t[:, j, head * P + 64:head * P + 128],
                                                  pt[:, j, j * P:T], start=(j == 0), stop=True, skip_group_check=True)
                        mm.then_inc(work.full[m % BANKS], 1)
                    if n % NT == 1 and n // NT + 1 < MLA_HEADS:
                        turn("q", q_t, n // NT + 1)
                        turn("k", k_t, n // NT + 1)

            def odd_out():
                u, g, _ = base["odd_out"]
                for head in range(MLSTM_HEADS):
                    work.wait_done(pe, MW["y", head])
                for head in range(MLA_HEADS):
                    work.wait_done(pe, AW["out", head])
                simple_outs(u, g, 8, y_in, None)

            def gla_in():
                u, g, m = base["gla_in"]
                wait_hn = hn_wait("norm_mix2")
                work.wait_free(pe, m)
                for k in range(DC):
                    wait_hn(k)
                    mm = nc.tensor.matmul(work.bank(m)[0:16, :], w_low[:, k, :], hn[:, k, :], start=(k == 0), stop=(k == DC - 1))
                mm.then_inc(work.full[m % BANKS], 1)
                simple_outs(u, g, 2, hn_in, None)
                work.wait_done(pe, m)
                for c in range(2):
                    work.wait_free(pe, m + 1 + c)
                    nc.tensor.matmul(work.bank(m + 1 + c)[:], w_gate_up[:, c * P:(c + 1) * P], g_low[:], start=True,
                                     stop=True).then_inc(work.full[(m + 1 + c) % BANKS], 1)
                simple_outs(u + 2, g + 2, 2, hn_in, None)
                token_outs(u + 4, g + 4, hn_in, 2)
                token_outs(u + 8, g + 8, hn_in, 2)

            def gla():
                g = base["gla_in"][1]
                for n in range(4):
                    stream.wait_done(pe, g + n)
                for n in range(LEVELS):
                    if n:
                        pe.wait_ge(pair_ready, n)
                    for q in range(NT):
                        m, r = GW["level", n, q], 64 * (q % 2)
                        work.wait_free(pe, m)
                        for o in range(4):
                            i, c = 2 * (q // 2) + o // 2, o % 2
                            cut = (slice(r, r + 64), c, slice(i * P, (i + 1) * P))
                            lhs, rhs = (pair[cut[0], n % 2, c, cut[2]],) * 2 if n else (gk[cut], gq[cut])
                            mm = nc.tensor.matmul(work.bank(m)[:, o * P:(o + 1) * P], lhs, rhs, start=True, stop=True)
                        mm.then_inc(work.full[m % BANKS], 1)
                pe.wait_ge(far_ready, 1)
                for head in range(GLA_HEADS):
                    r, c = 64 * (head % 2), head // 2
                    k = lambda n: kd[r:r + 64, c, n * P:(n + 1) * P]
                    q = lambda n, w: qd[r:r + 64, c, n * P:(n + w) * P]
                    m = GW["far_a", head]
                    work.wait_free(pe, m)
                    for o, w, lhs, rhs in ((0, 1, k(0), q(0, 1)), (1, 2, k(3), q(2, 2)), (3, 1, k(2), q(1, 1))):
                        mm = nc.tensor.matmul(work.bank(m)[:, o * P:(o + w) * P], lhs, rhs, start=True, stop=True)
                    mm.then_inc(work.full[m % BANKS], 1)
                    m = GW["far_b", head]
                    work.wait_free(pe, m)
                    nc.tensor.matmul(work.bank(m)[:, 0:2 * P], k(1), q(2, 2), start=True, stop=True).then_inc(work.full[m % BANKS], 1)
                for n in range(4, 8):
                    stream.wait_done(pe, g + n)
                where = {(0, 1): 0, (0, 2): 1, (0, 3): 2, (2, 3): 3, (1, 2): 4, (1, 3): 5}
                pe.wait_ge(near_ready, NT)
                for head in range(GLA_HEADS):
                    work.wait_done(pe, GW["far_b", head])
                    work.wait_done(pe, GW["far_a", head])
                for i in range(NT):
                    m = GW["o", i]
                    work.wait_free(pe, m)
                    for head in range(GLA_HEADS):
                        for j in range(i + 1):
                            w = near[:, i, head * P:(head + 1) * P] if j == i else far[:, head, where[j, i] * P:(where[j, i] + 1) * P]
                            mm = nc.tensor.matmul(work.bank(m)[:, head * P:(head + 1) * P], w, gv[:, j, head * P:(head + 1) * P],
                                                  start=(j == 0), stop=(j == i))
                    mm.then_inc(work.full[m % BANKS], 1)
                pe.wait_ge(go_ready, NT)
                for head in range(GLA_HEADS):
                    m = GW["y", head]
                    work.wait_free(pe, m)
                    for t in range(NT):
                        mm = nc.tensor.transpose(work.bank(m)[:, t * P:(t + 1) * P], go[:, t, head * P:(head + 1) * P], ident[:])
                    mm.then_inc(work.full[m % BANKS], 1)

            def swa():
                u, g, _ = base["swa"]
                simple_outs(u, g, 5, hn_in, None)
                stream.wait_free(pe, g + 5)
                wait_unit(pe, u + 5)
                for t in range(NT):
                    for k in range(DC):
                        mm = nc.tensor.matmul(stream.bank(g + 5)[:, t * P:(t + 1) * P], hn[:, k, t * P:(t + 1) * P],
                                              ring[:, (u + 5) % SLOTS, k * P:(k + 1) * P], start=(k == 0), stop=(k == DC - 1))
                mm.then_inc(stream.full[(g + 5) % BANKS], 1)
                for n in range(5):
                    stream.wait_done(pe, g + n)
                for n in range(SWA_BLOCKS + 1):
                    if n < SWA_BLOCKS:
                        m, r = SW["scores", n], 64 * (n % 2)
                        work.wait_free(pe, m)
                        for s in range(2):
                            i, at = 2 * (n // 2 % 2) + s, 256 * s
                            w = 256 if i else P
                            if i == 0:
                                nc.tensor.matmul(work.bank(m)[:, 0:P], ident[:], neg_until[:, 0:1].to_broadcast([P, P]),
                                                 start=True, stop=True, skip_group_check=True)
                            nc.tensor.matmul(work.bank(m)[:, at + 256 - w:at + 256], sqT[r:r + 64, n // 4, i * P:(i + 1) * P],
                                             skT[r:r + 64, 0, (i + 1) * P - w:(i + 1) * P], start=True, stop=True, skip_group_check=True)
                            if i:
                                nc.tensor.matmul(work.bank(m)[:, at:at + P], ident[:], neg_until[:], start=False, stop=True,
                                                 skip_group_check=True)
                            mm = nc.tensor.matmul(work.bank(m)[:, at + P:at + 2 * P], ident[:], neg_after[:], start=False,
                                                  stop=True, skip_group_check=True)
                        mm.then_inc(work.full[m % BANKS], 1)
                    if n:
                        m = SW["turned", n - 1]
                        work.wait_free(pe, m)
                        pe.wait_ge(sprob_ready, n)
                        for o in range(4):
                            mm = nc.tensor.transpose(work.bank(m)[:, o * P:(o + 1) * P], sprob[:, (n - 1) % 2, o * P:(o + 1) * P],
                                                     ident[:])
                        mm.then_inc(work.full[m % BANKS], 1)
                    if n and n % NT == 0:
                        j = n // NT - 1
                        m = SW["out", j]
                        work.wait_free(pe, m)
                        work.wait_done(pe, SW["turned", n - 1])
                        if j == 0:
                            stream.wait_done(pe, g + 5)
                        for i in range(NT):
                            for e in range(2):
                                for b in range(0 if i else 1, 2):
                                    mm = nc.tensor.matmul(work.bank(m)[64 * e:64 * e + 64, i * P:(i + 1) * P],
                                                          sv[:, i - 1 + b, 64 * e:64 * e + 64],
                                                          sprobT[:, i, (2 * e + b) * P:(2 * e + b + 1) * P],
                                                          start=(b == 1 or i > 0) and (b == 0 or i == 0), stop=(b == 1))
                        mm.then_inc(work.full[m % BANKS], 1)

            def pool():
                u, g, _ = base["pool"]
                simple_outs(u, g, 4, hn_in, None)
                wait_unit(pe, u + 4)
                for c in range(4):
                    stream.wait_free(pe, g + 4 + c)
                    pe.wait_ge(pd_ready, c + 1)
                    nc.tensor.matmul(stream.bank(g + 4 + c)[:], ring[:, (u + 4) % SLOTS, c * P:(c + 1) * P], pd[:, c, :],
                                     start=True, stop=True).then_inc(stream.full[(g + 4 + c) % BANKS], 1)

            def merge():
                u, g, _ = base["merge"]
                for n in range(3 * DC):
                    b = n % 3
                    stream.wait_free(pe, g + 2 * n)
                    feature_out(u + n, g + 2 * n, hn_in, DC).then_inc(stream.full[(g + 2 * n) % BANKS], 1)
                    stream.wait_free(pe, g + 2 * n + 1)
                    if n < 3:
                        for c in range(4):
                            if n == 0:
                                work.wait_done(pe, GW["y", c])
                            elif n == 1:
                                work.wait_done(pe, SW["out", c])
                            else:
                                stream.wait_done(pe, base["pool"][1] + 4 + c)
                    for k in range(4):
                        mm = nc.tensor.matmul(stream.bank(g + 2 * n + 1)[:], ring[:, (u + n) % SLOTS, (8 + k) * P:(9 + k) * P],
                                              branch[:, 4 * b + k, :], start=(k == 0), stop=(k == 3))
                    mm.then_inc(stream.full[(g + 2 * n + 1) % BANKS], 1)

            def block_out():
                u, g, _ = base["block_out"]
                simple_outs(u, g, 8, y_in, lambda k: stream.wait_done(pe, base["merge"][1] + 6 * k + 5))

            pe.wait_ge(consts_ready, 11)
            pe.wait_ge(tables_loaded, 16 * N_TABLES)
            norm("norm_mix0")
            even_in()
            u, g, _ = base["even_out"]
            simple_outs(u, g, 8, y_in, lambda k: stream.wait_done(pe, base["even_in"][1] + 3 * k + 2) if k < 4 else work.wait_done(pe, base["even_in"][2] + k - 4))
            if on("norm_ffn0"): norm("norm_ffn0")
            if on("ffn0"): ffn("ffn0", "norm_ffn0")
            if on("norm_ple0"): norm("norm_ple0")
            if on("ple0"): ple("ple0", "norm_ple0", 0)
            if on("norm_mix1"): norm("norm_mix1")
            if on("odd_in"): odd_in()
            if on("mlstm"): mlstm()
            if on("mla_up"): mla_up()
            if on("mla"): mla()
            if on("odd_out"): odd_out()
            if on("norm_ffn1"): norm("norm_ffn1")
            if on("ffn1"): ffn("ffn1", "norm_ffn1")
            if on("norm_ple1"): norm("norm_ple1")
            if on("ple1"): ple("ple1", "norm_ple1", 1)
            if on("norm_mix2"): norm("norm_mix2")
            if on("gla_in"): gla_in()
            if on("gla"): gla()
            if on("swa"): swa()
            if on("pool"): pool()
            if on("merge"): merge()
            if on("block_out"): block_out()
            if on("norm_post"): norm("norm_post")
            if on("norm_ffn2"): norm("norm_ffn2")
            if on("convffn"): ffn("convffn", "norm_ffn2")
            if on("norm_last"): norm("norm_last")

        @block.scalar
        def _(scalar):
            steps = Steps(scalar, act_steps)
            calls = [0]

            def rsqrt_guess(n):
                calls[0] += 1
                scalar.wait_ge(ms_ready, calls[0])
                steps.did(nc.scalar.activation(ln_ms[:, 0:n], ms[:, 0:n], ACT.Ln))
                steps.settle()
                nc.scalar.activation(rs0[:, 0:n], ln_ms[:, 0:n], ACT.Exp, scale=-0.5).then_inc(rs_guessed, 1)

            def norm(stage, src=None, ready=None):
                m = base[stage][2]
                scalar.preload_act_table_set(LNEXP)
                post = stage in ("norm_post", "norm_last")
                for c in range(DC):
                    if post:
                        n = h_out(BEFORE[stage], c)
                        stream.wait_full(scalar, n)
                        nc.scalar.activation(o_buf[:, c, :], stream.bank(n)[:], ACT.Copy).then_inc(stream.done[n % BANKS], 1)
                for c in range(DC):
                    h_ready(scalar, stage, c)
                    nc.scalar.activation((hn if post else sq)[:, c, :], (o_buf if post else h)[:, c, :],
                                         ACT.Square).then_inc(sq_ready, 1)
                rsqrt_guess(NT)
                work.wait_full(scalar, m + 1)
                nc.scalar.activation(rstd_rows[:], work.bank(m + 1)[:], ACT.Copy).then_inc(work.done[(m + 1) % BANKS], 1)

            def even_in():
                u, g, m = base["even_in"]
                for j in range(4):
                    n = g + 3 * j
                    stream.wait_full(scalar, n)
                    if j >= 2:
                        stream.wait_done(scalar, n - 5)
                    nc.scalar.activation(tmp[:, j % 2, :], stream.bank(n)[:], ACT.Copy).then_inc(stream.done[n % BANKS], 1)
                for j in range(4):
                    n = g + 12 + j
                    stream.wait_full(scalar, n)
                    nc.scalar.activation(u_g[:, j, :], stream.bank(n)[:], ACT.Gelu_apprx_tanh).then_inc(stream.done[n % BANKS], 1)
                for t in range(NT):
                    n = g + 16 + t
                    stream.wait_full(scalar, n)
                    nc.scalar.activation(v_t[:, t, :], stream.bank(n)[:], ACT.Gelu_apprx_tanh).then_inc(stream.done[n % BANKS], 1)
                for t in range(NT):
                    stream.wait_done(scalar, g + 16 + t)
                    if t >= 2:
                        scalar.wait_ge(v_square, t - 1)
                    nc.scalar.activation(v_sq[:, t % 2, :], v_t[:, t, :], ACT.Square).then_inc(v_gelu, 1)
                scalar.preload_act_table_set(LNEXP)
                rsqrt_guess(32)

            def ffn(stage):
                g = base[stage][1]
                scalar.preload_act_table_set("silu_and_others")
                with scalar.Fori(0, 2 * FC // 4) as i:
                    for j in (0, 2):
                        scalar.wait_ge(stream.full[(g + j) % BANKS], i + (g + j) // BANKS + 1)
                        scalar.wait_ge(stream.done[(g + j + 1) % BANKS], i + (g + j + 1) // BANKS)
                        nc.scalar.activation(tmp[:, j // 2, :], stream.bank(g + j)[:], ACT.Silu).then_inc(
                            stream.done[(g + j) % BANKS], 1)

            def ple(stage):
                g = base[stage][1]
                for c in range(DC):
                    n = g + 2 * c
                    stream.wait_full(scalar, n)
                    if c >= 2:
                        stream.wait_done(scalar, n - 3)
                    nc.scalar.activation(tmp[:, c % 2, :], stream.bank(n)[:], ACT.Sigmoid).then_inc(stream.done[n % BANKS], 1)

            def odd_in():
                g, m = base["odd_in"][1:]
                for c in range(5):
                    stream.wait_full(scalar, g + c)
                    nc.scalar.activation(lat_sq[:, c, :], stream.bank(g + c)[:], ACT.Square).then_inc(lat_squared, 1)
                for c in range(2):
                    n = g + 5 + c
                    stream.wait_full(scalar, n)
                    nc.scalar.activation(mq[:, c, :], stream.bank(n)[:], ACT.Copy, scale=64 ** -0.5).then_inc(stream.done[n % BANKS], 1)
                for c in range(2):
                    n = g + 7 + c
                    stream.wait_full(scalar, n)
                    nc.scalar.activation(mk[:, c, :], stream.bank(n)[:], ACT.Copy).then_inc(stream.done[n % BANKS], 1)
                for t in range(NT):
                    n = g + 9 + t
                    stream.wait_full(scalar, n)
                    nc.scalar.activation(mv[:, t, :], stream.bank(n)[:], ACT.Copy).then_inc(stream.done[n % BANKS], 1)
                for t in range(NT):
                    n = g + 13 + t
                    stream.wait_full(scalar, n)
                    nc.scalar.activation(mo[:, t, :], stream.bank(n)[:], ACT.Sigmoid).then_inc(stream.done[n % BANKS], 1)

            def mlstm():
                scalar.preload_act_table_set(LNEXP)
                scalar.wait_ge(gates_ready, 1)
                steps.did(nc.scalar.activation(gl[:, 0, :], gl[:, 3, :], ACT.Abs))
                steps.settle()
                steps.did(nc.scalar.activation(gl[:, 1, :], gl[:, 0, :], ACT.Exp, scale=-1.0))
                steps.settle()
                nc.scalar.activation(gl[:, 2, :], gl[:, 1, :], ACT.Ln, bias=1.0).then_inc(log_ready, 1)
                for n in range(MLSTM_BLOCKS + 1):
                    if n < MLSTM_BLOCKS:
                        head, i = divmod(n, NT)
                        m = MW["decay", n]
                        scalar.wait_ge(m_ready, n + 1)
                        nc.scalar.activation(exp_m[:, n:n + 1], neg_m[:, n:n + 1], ACT.Exp).then_inc(exp_m_ready, 1)
                        nc.scalar.activation(dec[:, n % 2, 0:(i + 1) * P], work.bank(m)[:, 0:(i + 1) * P], ACT.Exp,
                                             bias=neg_m[:, n:n + 1]).then_inc(work.done[m % BANKS], 1)
                    if n:
                        head, i = divmod(n - 1, NT)
                        m = MW["turned", n - 1]
                        work.wait_full(scalar, m)
                        nc.scalar.activation(sT[:, (n - 1) % 2, 0:(i + 1) * P], work.bank(m)[:, 0:(i + 1) * P],
                                             ACT.Copy).then_inc(work.done[m % BANKS], 1)
                        m = MW["out", n - 1]
                        work.wait_full(scalar, m)
                        scalar.wait_ge(rden_ready, n)
                        nc.scalar.activation(hv[:, i, head * P:(head + 1) * P], work.bank(m)[:, 0:P], ACT.Copy,
                                             scale=rden[:, n - 1:n]).then_inc(work.done[m % BANKS], 1)
                work.wait_done(scalar, MW["out", MLSTM_BLOCKS - 1])
                for t in range(NT):
                    nc.scalar.activation(hv_sq[:, t, :], hv[:, t, :], ACT.Square).then_inc(hv_squared, 1)
                rsqrt_guess(16)
                for head in range(MLSTM_HEADS):
                    m = MW["y", head]
                    work.wait_full(scalar, m)
                    nc.scalar.activation(y[:, 4 + head, :], work.bank(m)[:], ACT.Copy).then_inc(work.done[m % BANKS], 1)

            def mla_up():
                g = base["mla_up"][1]
                rsqrt_guess(8)
                scalar.wait_ge(lat_rs_ready, 1)
                for n in range(16):
                    t, half = divmod(n % 8, 2)
                    kv = n // 8
                    w = (384, 512)[kv]
                    stream.wait_full(scalar, g + n)
                    nc.scalar.activation((q_t, kv_t)[kv][:, t, half * w:half * w + w], stream.bank(g + n)[:, 0:w], ACT.Copy,
                                         scale=lat_rs[:, NT * kv + t:NT * kv + t + 1]).then_inc(stream.done[(g + n) % BANKS], 1)
                for n in range(8):
                    t, kv = n % 4, n // 4
                    stream.wait_done(scalar, g + 8 * kv + 2 * t + 1)
                    stream.wait_done(scalar, g + 8 * kv + 2 * t)
                    if n >= 2:
                        scalar.wait_ge(summed, n - 1)
                    w = (768, 1024)[kv]
                    nc.scalar.activation(qk_sq[:, n % 2, 0:w], (q_t, kv_t)[kv][:, t, :], ACT.Square).then_inc(squared, 1)
                    if n == 3:
                        rsqrt_guess(64)
                rsqrt_guess(36)

            def mla():
                for n in range(MLA_BLOCKS + 1):
                    if n < MLA_BLOCKS:
                        head, i = divmod(n, NT)
                        m = AW["scores", n]
                        scalar.wait_ge(m_ready, MLSTM_BLOCKS + n + 1)
                        if n >= 2:
                            work.wait_full(scalar, AW["turned", n - 2])
                        nc.scalar.activation(prob[:, n % 2, 0:(i + 1) * P], work.bank(m)[:, 0:(i + 1) * P], ACT.Exp,
                                             bias=neg_m[:, n:n + 1], accum_out=den[:, n:n + 1]).then_inc(work.done[m % BANKS], 1)
                    if n:
                        head, i = divmod(n - 1, NT)
                        m = AW["turned", n - 1]
                        work.wait_full(scalar, m)
                        if i == 0 and head >= 2:
                            work.wait_full(scalar, AW["out", head - 2])
                        nc.scalar.activation((probT, probT2)[head % 2][:, 0:i + 1, i * P:(i + 1) * P],
                                             work.bank(m)[:, 0:(i + 1) * P].rearrange("p (a b) -> p a b", b=P),
                                             ACT.Copy).then_inc(work.done[m % BANKS], 1)

            def gla_in():
                g, m = base["gla_in"][1:]

                def copy(dst, n, scale=1.0, func=ACT.Copy):
                    stream.wait_full(scalar, n)
                    nc.scalar.activation(dst, stream.bank(n)[:], func, scale=scale).then_inc(stream.done[n % BANKS], 1)

                work.wait_full(scalar, m)
                nc.scalar.activation(g_low[:], work.bank(m)[0:16, :], ACT.Copy).then_inc(work.done[m % BANKS], 1)
                for c in range(2):
                    copy(gq[:, c, :], g + c, 64 ** -0.5)
                for c in range(2):
                    work.wait_full(scalar, m + 1 + c)
                    nc.scalar.activation(logit[:, c, :], work.bank(m + 1 + c)[:], ACT.Identity, bias=col("gla_b", c)).then_inc(
                        work.done[(m + 1 + c) % BANKS], 1)
                for c in range(2):
                    work.wait_done(scalar, m + 1 + c)
                steps.did(nc.scalar.activation(log_p, logit, ACT.Abs))
                steps.settle()
                steps.did(nc.scalar.activation(log_p, log_p, ACT.Exp, scale=-1.0))
                steps.settle()
                nc.scalar.activation(log_p, log_p, ACT.Ln, bias=1.0).then_inc(logit_logged, 1)
                for c in range(2):
                    copy(gk[:, c, :], g + 2 + c)
                decays(1)
                for t in range(NT):
                    copy(gv[:, t, :], g + 4 + t)
                decays(2)
                scalar.preload_act_table_set("silu_and_others")
                for t in range(NT):
                    copy(gr[:, t, :], g + 8 + t, func=ACT.Silu)

            def decays(n):
                scalar.wait_ge(exponent_ready, n)
                nc.scalar.activation(pair[:, n % 2], pair[:, n % 2], ACT.Exp, scale=1.0 / 16).then_inc(decay_ready, 1)

            def gla():
                scalar.preload_act_table_set(LNEXP)
                for n in range(3, LEVELS):
                    decays(n)
                scalar.wait_ge(exponent_ready, LEVELS)
                for c in range(2):
                    for i in range(NT - 1):
                        nc.scalar.activation(kd[:, c, i * P:(i + 1) * P], cum[:, c, i * P:(i + 1) * P], ACT.Exp, scale=-1.0 / 16,
                                             bias=tot16[:, c, i:i + 1])
                    for slot, i in enumerate((1, 3, 2)):
                        nc.scalar.activation(qd[:, c, slot * P:(slot + 1) * P], cum[:, c, i * P:(i + 1) * P], ACT.Exp, scale=1.0 / 16)
                nc.scalar.activation(exp_tot[:], tot16[:], ACT.Exp).then_inc(far_exp, 1)
                for head in range(GLA_HEADS):
                    for part, lo, w in (("far_a", 0, 512), ("far_b", 512, 256)):
                        m = GW[part, head]
                        work.wait_full(scalar, m)
                        nc.scalar.activation(far[:, head, lo:lo + w], work.bank(m)[:, 0:w], ACT.Copy).then_inc(work.done[m % BANKS], 1)
                for i in range(NT):
                    m = GW["o", i]
                    work.wait_full(scalar, m)
                    nc.scalar.activation(go[:, i, :], work.bank(m)[:], ACT.Copy).then_inc(work.done[m % BANKS], 1)
                for i in range(NT):
                    work.wait_done(scalar, GW["o", i])
                    nc.scalar.activation(go_sq[:, i, :], go[:, i, :], ACT.Square).then_inc(go_squared, 1)
                rsqrt_guess(16)
                for head in range(GLA_HEADS):
                    m = GW["y", head]
                    work.wait_full(scalar, m)
                    nc.scalar.activation(branch[:, head, :], work.bank(m)[:], ACT.Copy).then_inc(work.done[m % BANKS], 1)

            def swa():
                g = base["swa"][1]
                for c in range(6):
                    dst = (sqT[:, c, :] if c < 4 else skT[:, 0, :] if c == 4 else sv.rearrange("p a b -> p (a b)"))
                    stream.wait_full(scalar, g + c)
                    nc.scalar.activation(dst, stream.bank(g + c)[:], ACT.Copy, scale=64 ** -0.5 if c < 4 else 1.0).then_inc(
                        stream.done[(g + c) % BANKS], 1)
                for n in range(SWA_BLOCKS + 1):
                    if n < SWA_BLOCKS:
                        m = SW["scores", n]
                        scalar.wait_ge(m_ready, MLSTM_BLOCKS + MLA_BLOCKS + n + 1)
                        scalar.wait_ge(sink_ready, n + 2)
                        if n >= 2:
                            work.wait_full(scalar, SW["turned", n - 2])
                        nc.scalar.activation(sink_m[:, 2 * n:2 * n + 2], sink_m[:, 2 * n:2 * n + 2], ACT.Exp)
                        for s in range(2):
                            x = nc.scalar.activation(sprob[:, n % 2, 256 * s:256 * s + 256], work.bank(m)[:, 256 * s:256 * s + 256],
                                                     ACT.Exp, bias=neg_m[:, 2 * n + s:2 * n + s + 1],
                                                     accum_out=den[:, 2 * n + s:2 * n + s + 1])
                        x.then_inc(work.done[m % BANKS], 1)
                    if n:
                        j, b = divmod(n - 1, 4)
                        m = SW["turned", n - 1]
                        work.wait_full(scalar, m)
                        if j and b == 0:
                            work.wait_full(scalar, SW["out", j - 1])
                        i, e = 2 * (b // 2), b % 2
                        nc.scalar.activation(sprobT[:, i:i + 2, 256 * e:256 * e + 256],
                                             work.bank(m)[:].rearrange("p (a b) -> p a b", a=2), ACT.Copy).then_inc(work.done[m % BANKS], 1)

            def pool():
                g = base["pool"][1]
                scalar.wait_ge(pad_ready, 1)
                for c in range(4):
                    stream.wait_full(scalar, g + c)
                    nc.scalar.activation(pu[:, c, 16:16 + T], stream.bank(g + c)[:], ACT.Copy).then_inc(stream.done[(g + c) % BANKS], 1)
                for c in range(4):
                    n = g + 4 + c
                    stream.wait_full(scalar, n)
                    nc.scalar.activation(branch[:, 8 + c, :], stream.bank(n)[:], ACT.Copy, scale=col("pool_scale", c)).then_inc(
                        stream.done[n % BANKS], 1)

            def merge():
                g = base["merge"][1]
                for n in range(3 * DC):
                    o = g + 2 * n
                    stream.wait_full(scalar, o)
                    if n >= 2:
                        stream.wait_done(scalar, o - 3)
                    nc.scalar.activation(tmp[:, n % 2, :], stream.bank(o)[:], ACT.Sigmoid).then_inc(stream.done[o % BANKS], 1)

            def convffn():
                g = base["convffn"][1]
                scalar.preload_act_table_set("gelu_apprx_tanh_and_others")

                def body(i, first):
                    for j in range(4):
                        b, gate = j // 2, j % 2 == 0
                        c = 2 * i + b + (0 if gate else FC)
                        scalar.wait_ge(stream.full[(g + j) % BANKS], i + (g + j) // BANKS + 1)
                        if not first:
                            scalar.wait_ge(act_ready, 2 * (i - 1) + b + 1)
                        nc.scalar.activation(tmp[:, j, :].unsqueeze(1), stream.bank(g + j)[:].unsqueeze(1), ACT.Identity,
                                             scale=cols[:, bass.ds(c + COLS["cw2"], 1)],
                                             bias=cols[:, bass.ds(c + COLS["cb"], 1)]).then_inc(conv_started, 1)
                        if not gate:
                            scalar.wait_ge(stream.done[(g + j - 1) % BANKS], i + (g + j - 1) // BANKS + 1)
                            nc.scalar.activation(tmp[:, j - 1, :], tmp[:, j - 1, :], ACT.Gelu_apprx_tanh).then_inc(gelu_ready, 1)

                body(0, True)
                with scalar.Fori(1, 2 * FC // 4) as i:
                    body(i, False)

            scalar.dma_start(w_small[:], a["w_small"]).then_inc(tables_loaded, 16)
            scalar.dma_start(w_low[:], a["w_low"]).then_inc(tables_loaded, 16)
            scalar.dma_start(w_gate_up[:], a["w_gate_up"]).then_inc(tables_loaded, 16)
            scalar.dma_start(pos_i[:], a["positions"]).then_inc(tables_loaded, 16)
            scalar.dma_start(cols[:], a["cols"]).then_inc(tables_loaded, 16)
            scalar.dma_start(rows[:], a["rows"].partition_broadcast(P)).then_inc(tables_loaded, 16)
            scalar.dma_start(ws, a["w_s"]).then_inc(tables_loaded, 16)
            scalar.dma_start(b_row[:], a["b_s"]).then_inc(tables_loaded, 16)
            scalar.dma_start(pT[:], a["p0"]).then_inc(p_loaded, 16)
            scalar.preload_act_table_set("silu_and_others")
            scalar.wait_ge(angle_ready, 1)
            nc.scalar.activation(cos_sin[:], angle[:, 3:5, :], ACT.Sin).then_inc(turned_ready, 1)
            norm("norm_mix0")
            even_in()
            if on("norm_ffn0"): norm("norm_ffn0")
            if on("ffn0"): ffn("ffn0")
            if on("norm_ple0"): norm("norm_ple0")
            if on("ple0"): ple("ple0")
            if on("norm_mix1"): norm("norm_mix1")
            if on("odd_in"): odd_in()
            if on("mlstm"): mlstm()
            if on("mla_up"): mla_up()
            if on("mla"): mla()
            if on("norm_ffn1"): norm("norm_ffn1")
            if on("ffn1"): ffn("ffn1")
            if on("norm_ple1"): norm("norm_ple1")
            if on("ple1"): ple("ple1")
            if on("norm_mix2"): norm("norm_mix2")
            if on("gla_in"): gla_in()
            if on("gla"): gla()
            if on("swa"): swa()
            if on("pool"): pool()
            if on("merge"): merge()
            if on("norm_post"): norm("norm_post")
            if on("norm_ffn2"): norm("norm_ffn2")
            if on("convffn"): convffn()
            if on("norm_last"): norm("norm_last")

        @block.vector
        def _(dve):
            steps = Steps(dve, dve_steps)
            calls = [0]

            def rsqrt(n):
                calls[0] += 1
                dve.wait_ge(rs_guessed, calls[0])
                steps.did(nc.vector.tensor_tensor(rt[:, 0, 0:n], rs0[:, 0:n], rs0[:, 0:n], ALU.mult))
                steps.settle()
                steps.did(nc.vector.scalar_tensor_tensor(rt[:, 1, 0:n], rt[:, 0, 0:n], -0.5, ms[:, 0:n], ALU.mult, ALU.mult))
                steps.settle()
                nc.vector.scalar_tensor_tensor(rstd[:, 0:n], rt[:, 1, 0:n], 1.5, rs0[:, 0:n], ALU.add, ALU.mult).then_inc(rstd_ready, 1)

            def norm(stage, gain):
                m, k = base[stage][2], norm_no[stage]
                work.wait_full(dve, m)
                nc.vector.tensor_copy(stat[:, 0:NT], work.bank(m)[:, 0:NT]).then_inc(work.done[m % BANKS], 1)
                work.wait_done(dve, m)
                nc.vector.tensor_scalar(ms[:, 0:NT], stat[:, 0:NT], 1.0 / D, EPS, ALU.mult, ALU.add).then_inc(ms_ready, 1)
                rsqrt(NT)
                work.wait_done(dve, m + 1)
                if k == 0:
                    dve.wait_ge(tables_loaded, 16 * N_TABLES)
                if stage in ("norm_post", "norm_last"):
                    for c in range(DC):
                        steps.did(nc.vector.scalar_tensor_tensor(tmp[:, c % 4, :], o_buf[:, c, :], col(gain, c), rstd_rows[:],
                                                                 ALU.mult, ALU.mult))
                        steps.settle()
                        nc.vector.tensor_tensor(h[:, c, :], h[:, c, :], tmp[:, c % 4, :], ALU.add).then_inc(h_updated, 1)
                    dve.wait_ge(h_updated, DC * (1 if stage == "norm_post" else 2))
                    return
                for c in range(DC):
                    nc.vector.scalar_tensor_tensor(hn[:, c, :], h[:, c, :], col(gain, c), rstd_rows[:], ALU.mult,
                                                   ALU.mult).then_inc(hn_ready, 1)

            def even_in():
                u, g, m = base["even_in"]
                for e in range(2):
                    steps.did(nc.vector.memset(z_pad[:, e, 0:2], 0.0))
                for j in range(4):
                    n, z, cv = g + 3 * j, z_pad[:, j % 2, :], conv[:, j % 2, :]
                    stream.wait_full(dve, n + 1)
                    stream.wait_done(dve, n)
                    if j >= 2:
                        stream.wait_done(dve, n - 4)
                    steps.settle()
                    nc.vector.tensor_tensor(z[:, 2:2 + T], stream.bank(n + 1)[:], tmp[:, j % 2, :], ALU.mult).then_inc(
                        stream.done[(n + 1) % BANKS], 1)
                    stream.wait_done(dve, n + 1)
                    steps.settle()
                    steps.did(nc.vector.tensor_scalar(cv, z[:, 2:2 + T], col("w_conv", 8 + j), None, ALU.mult))
                    for w in (1, 0):
                        steps.settle()
                        steps.did(nc.vector.scalar_tensor_tensor(cv, z[:, w:w + T], col("w_conv", 4 * w + j), cv, ALU.mult, ALU.add))
                    stream.wait_full(dve, n + 2)
                    steps.settle()
                    nc.vector.tensor_tensor(y[:, j, :], stream.bank(n + 2)[:], cv, ALU.mult).then_inc(
                        stream.done[(n + 2) % BANKS], 1)
                for t in range(NT):
                    dve.wait_ge(v_gelu, t + 1)
                    nc.vector.tensor_reduce(stat[:, 16 + 8 * t:24 + 8 * t], v_sq[:, t % 2, :].rearrange("p (a b) -> p a b", a=8),
                                            AX_X, ALU.add).then_inc(v_square, 1)
                dve.wait_ge(v_square, NT)
                nc.vector.tensor_scalar(ms[:, 0:32], stat[:, 16:48], 1.0 / 64, EPS, ALU.mult, ALU.add).then_inc(ms_ready, 1)
                rsqrt(32)
                dve.wait_ge(rstd_ready, calls[0])
                for t in range(NT):
                    vt = v_t[:, t, :].rearrange("p (a b) -> p a b", a=8)
                    steps.did(nc.vector.tensor_tensor(vt, vt, rstd[:, 8 * t:8 * t + 8].unsqueeze(2).to_broadcast([P, 8, 64]), ALU.mult))
                    steps.settle()
                    nc.vector.tensor_tensor(v_t[:, t, :], v_t[:, t, :], row("g_v", 0, 512), ALU.mult).then_inc(v_ready, 1)
                for hp in range(4):
                    work.wait_full(dve, m + hp)
                    stream.wait_done(dve, g + 12 + hp)
                    nc.vector.tensor_tensor(y[:, 4 + hp, :], work.bank(m + hp)[:], u_g[:, hp, :], ALU.mult).then_inc(
                        work.done[(m + hp) % BANKS], 1)

            def add_outs(g, n):
                for c in range(n):
                    stream.wait_full(dve, g + c)
                    nc.vector.tensor_tensor(h[:, c, :], stream.bank(g + c)[:], h[:, c, :], ALU.add).then_inc(
                        stream.done[(g + c) % BANKS], 1)

            def ffn(stage):
                g = base[stage][1]
                with dve.Fori(0, 2 * FC // 4) as i:
                    for j in (1, 3):
                        dve.wait_ge(stream.full[(g + j) % BANKS], i + (g + j) // BANKS + 1)
                        dve.wait_ge(stream.done[(g + j - 1) % BANKS], i + (g + j - 1) // BANKS + 1)
                        nc.vector.tensor_tensor(act[:, bass.ds(2 * i + j // 2, 1), :], stream.bank(g + j)[:].unsqueeze(1),
                                                tmp[:, j // 2, :].unsqueeze(1), ALU.mult).then_inc(stream.done[(g + j) % BANKS], 1)
                add_outs(g + 2 * FC, DC)

            def ple(stage):
                g = base[stage][1]
                for c in range(DC):
                    n = g + 2 * c + 1
                    stream.wait_full(dve, n)
                    stream.wait_done(dve, n - 1)
                    if c >= 2:
                        stream.wait_done(dve, n - 4)
                    steps.did(nc.vector.tensor_tensor(tmp[:, 2 + c % 2, :], stream.bank(n)[:], tmp[:, c % 2, :], ALU.mult))
                    steps.settle()
                    nc.vector.tensor_tensor(h[:, c, :], tmp[:, 2 + c % 2, :], h[:, c, :], ALU.add).then_inc(
                        stream.done[n % BANKS], 1)

            def rope_angles():
                dve.wait_ge(tables_loaded, 16 * N_TABLES)
                dve.wait_ge(freq_ready, 1)
                ang, turns, off = angle[:, 0, :], angle[:, 1, :], angle[:, 2, :]
                a3 = ang.rearrange("p (a b) -> p a b", a=NT)
                steps.did(nc.vector.tensor_copy(stat[:, 60:64], pos_i[:]))
                steps.settle()
                steps.did(nc.vector.tensor_copy(a3, inv_freq[:].unsqueeze(1).to_broadcast([P, NT, 16])))
                steps.settle()
                steps.did(nc.vector.tensor_tensor(a3, a3, stat[:, 60:64].unsqueeze(2).to_broadcast([P, NT, 16]), ALU.mult))
                for j, (quarter, shift) in enumerate(((0.25, PI / 2), (0.0, 0.0))):
                    r = angle[:, 3 + j, :]
                    steps.settle()
                    steps.did(nc.vector.tensor_scalar(off, ang, 1.0 / TWO_PI, quarter, ALU.mult, ALU.add))
                    steps.settle()
                    steps.did(nc.vector.tensor_scalar(turns, off, ROUND, ROUND, ALU.add, ALU.subtract))
                    steps.settle()
                    steps.did(nc.vector.tensor_copy(r, ang))
                    for part in TURN_PARTS:
                        steps.settle()
                        steps.did(nc.vector.scalar_tensor_tensor(r, turns, -part, r, ALU.mult, ALU.add))
                    steps.settle()
                    steps.did(nc.vector.tensor_scalar(r, r, shift, 3.1415925, ALU.add, ALU.min))
                    steps.settle()
                    if j == 0:
                        steps.did(nc.vector.tensor_scalar(r, r, -3.1415925, None, ALU.max))
                    else:
                        nc.vector.tensor_scalar(r, r, -3.1415925, None, ALU.max).then_inc(angle_ready, 1)

            def odd_in():
                g, m = base["odd_in"][1:]
                for c in range(5):
                    stream.wait_full(dve, g + c)
                    dve.wait_ge(lat_squared, c + 1)
                    nc.vector.tensor_scalar(lat[:, c, :], stream.bank(g + c)[:], col("g_qa", c), None, ALU.mult).then_inc(
                        stream.done[(g + c) % BANKS], 1)
                for t in range(NT):
                    stream.wait_done(dve, g + 13 + t)
                    steps.did(nc.vector.tensor_tensor(mo[:, t, :], mo[:, t, :], row("g_mh", 0, 512), ALU.mult))
                work.wait_full(dve, m)
                small = work.bank(m)[:, 0:160].rearrange("p (a b) -> p a b", a=NT)
                steps.did(nc.vector.tensor_copy(k_pe[:], small[:, :, 0:32]))
                nc.vector.tensor_tensor(gates[:], small[:, :, 32:40], row("b_gate", 0, 8).unsqueeze(1).to_broadcast([P, NT, 8]),
                                        ALU.add).then_inc(work.done[m % BANKS], 1)
                work.wait_full(dve, m + 1)
                nc.vector.tensor_copy(lat_ss[:], work.bank(m + 1)[:, 0:8]).then_inc(work.done[(m + 1) % BANKS], 1)

            def mlstm():
                work.wait_done(dve, base["odd_in"][2])
                f = gl[:, 3, :].rearrange("p (a b) -> p a b", a=NT)
                nc.vector.tensor_copy(f, gates[:, :, 4:8]).then_inc(gates_ready, 1)
                dve.wait_ge(log_ready, 1)
                nc.vector.scalar_tensor_tensor(lf[:], f, 0.0, gl[:, 2, :].rearrange("p (a b) -> p a b", a=NT), ALU.min,
                                               ALU.subtract).then_inc(lf_ready, 1)
                dve.wait_ge(lf_ready, 1)
                work.wait_full(dve, base["odd_in"][2] + 1)
                for n in range(MLSTM_BLOCKS):
                    head, k = divmod(n, NT)
                    steps.did(nc.vector.tensor_scalar(rdiag[:, n, :], ident[:], gates[:, k, head:head + 1], None, ALU.mult))
                    steps.settle()
                    nc.vector.scalar_tensor_tensor(rdiag[:, n, :], below[:], lf[:, k, head:head + 1], rdiag[:, n, :], ALU.mult,
                                                   ALU.add).then_inc(rdiag_ready, 1)
                m = MW["sums", 0]
                work.wait_full(dve, m)
                nc.vector.tensor_scalar(neg_sum[:], work.bank(m)[:, 0:16], -1.0, None, ALU.mult).then_inc(work.done[m % BANKS], 1)
                work.wait_done(dve, m)
                for n in range(MLSTM_BLOCKS):
                    head, i = divmod(n, NT)
                    m = MW["decay", n]
                    work.wait_full(dve, m)
                    steps.did(nc.vector.tensor_reduce(neg_m[:, n:n + 1], work.bank(m)[:, 0:(i + 1) * P], AX_X, ALU.max, negate=True))
                    steps.settle()
                    nc.vector.tensor_tensor(neg_m[:, n:n + 1], neg_m[:, n:n + 1], neg_sum[:, 4 * i + head:4 * i + head + 1],
                                            ALU.min).then_inc(m_ready, 1)
                    work.wait_done(dve, m)
                    m = MW["scores", n]
                    work.wait_full(dve, m)
                    w = dec[:, n % 2, 0:(i + 1) * P]
                    nc.vector.scalar_tensor_tensor(w, work.bank(m)[:, 0:(i + 1) * P], 1.0, w, ALU.mult, ALU.mult,
                                                   accum_out=den[:, n:n + 1]).then_inc(work.done[m % BANKS], 1)
                    work.wait_done(dve, m)
                    dve.wait_ge(exp_m_ready, n + 1)
                    steps.did(nc.vector.scalar_tensor_tensor(den[:, n:n + 1], den[:, n:n + 1], -1.0, den[:, n:n + 1], ALU.mult, ALU.max))
                    steps.settle()
                    steps.did(nc.vector.tensor_tensor(den[:, n:n + 1], den[:, n:n + 1], exp_m[:, n:n + 1], ALU.max))
                    steps.settle()
                    nc.vector.reciprocal(rden[:, n:n + 1], den[:, n:n + 1]).then_inc(rden_ready, 1)
                for t in range(NT):
                    dve.wait_ge(hv_squared, t + 1)
                    steps.did(nc.vector.tensor_reduce(stat[:, 4 * t:4 * t + 4], hv_sq[:, t, :].rearrange("p (a b) -> p a b", a=4),
                                                      AX_X, ALU.add))
                steps.settle()
                nc.vector.tensor_scalar(ms[:, 0:16], stat[:, 0:16], 1.0 / P, EPS, ALU.mult, ALU.add).then_inc(ms_ready, 1)
                rsqrt(16)
                dve.wait_ge(rstd_ready, calls[0])
                for t in range(NT):
                    v = hv[:, t, :].rearrange("p (a b) -> p a b", a=4)
                    steps.did(nc.vector.tensor_tensor(v, v, rstd[:, 4 * t:4 * t + 4].unsqueeze(2).to_broadcast([P, 4, P]), ALU.mult))
                    steps.settle()
                    nc.vector.tensor_tensor(hv[:, t, :], hv[:, t, :], mo[:, t, :], ALU.mult).then_inc(hv_ready, 1)

            def mla_up():
                work.wait_done(dve, base["odd_in"][2] + 1)
                steps.did(nc.vector.tensor_scalar(ms[:, 0:4], lat_ss[:, 0:4], 1.0 / 384, EPS, ALU.mult, ALU.add))
                nc.vector.tensor_scalar(ms[:, 4:8], lat_ss[:, 4:8], 1.0 / 256, EPS, ALU.mult, ALU.add).then_inc(ms_ready, 1)
                rsqrt(8)
                dve.wait_ge(rstd_ready, calls[0])
                nc.vector.tensor_copy(lat_rs[:], rstd[:, 0:8]).then_inc(lat_rs_ready, 1)
                steps.did(nc.vector.tensor_scalar(row("g_q", 0, 96), row("g_q", 0, 96), 96 ** -0.5, None, ALU.mult))
                st = stat[:].rearrange("p (a b) -> p a b", a=NT)
                for t in range(NT):
                    dve.wait_ge(squared, t + 1)
                    s3 = qk_sq[:, t % 2, 0:768].rearrange("p (a b) -> p a b", a=8)
                    steps.did(nc.vector.tensor_reduce(st[:, t, 0:8], s3[:, :, 0:64], AX_X, ALU.add))
                    nc.vector.tensor_reduce(st[:, t, 8:16], s3[:, :, 64:96], AX_X, ALU.add).then_inc(summed, 1)
                dve.wait_ge(summed, NT)
                m3 = ms[:].rearrange("p (a b) -> p a b", a=NT)
                steps.did(nc.vector.tensor_scalar(m3[:, :, 0:8], st[:, :, 0:8], 1.0 / 64, EPS, ALU.mult, ALU.add))
                nc.vector.tensor_scalar(m3[:, :, 8:16], st[:, :, 8:16], 1.0 / 32, EPS, ALU.mult, ALU.add).then_inc(ms_ready, 1)
                rsqrt(64)
                dve.wait_ge(rstd_ready, calls[0])
                r3 = rstd[:].rearrange("p (a b) -> p a b", a=NT)
                for t in range(NT):
                    q3 = q_t[:, t, :].rearrange("p (a b) -> p a b", a=8)
                    steps.did(nc.vector.tensor_tensor(q3[:, :, 0:64], q3[:, :, 0:64],
                                                      r3[:, t, 0:8].unsqueeze(2).to_broadcast([P, 8, 64]), ALU.mult))
                    steps.did(nc.vector.tensor_tensor(q3[:, :, 64:96], q3[:, :, 64:96],
                                                      r3[:, t, 8:16].unsqueeze(2).to_broadcast([P, 8, 32]), ALU.mult))
                    steps.settle()
                    steps.did(nc.vector.tensor_tensor(q3, q3, row("g_q", 0, 96).unsqueeze(1).to_broadcast([P, 8, 96]), ALU.mult))
                for t in range(NT):
                    dve.wait_ge(squared, NT + t + 1)
                    s3 = qk_sq[:, t % 2, :].rearrange("p (a b) -> p a b", a=8)
                    nc.vector.tensor_reduce(stat[:, 8 * t:8 * t + 8], s3[:, :, 0:64], AX_X, ALU.add).then_inc(summed, 1)
                steps.did(nc.vector.tensor_tensor(angle[:, 0:2, :].rearrange("p a (b c) -> p (a b) c", c=32), k_pe[:], k_pe[:], ALU.mult))
                steps.settle()
                steps.did(nc.vector.tensor_reduce(stat[:, 32:36], angle[:, 0:2, :].rearrange("p a (b c) -> p (a b) c", c=32), AX_X, ALU.add))
                steps.settle()
                steps.did(nc.vector.tensor_scalar(ms[:, 0:32], stat[:, 0:32], 1.0 / 64, EPS, ALU.mult, ALU.add))
                nc.vector.tensor_scalar(ms[:, 32:36], stat[:, 32:36], 1.0 / 32, EPS, ALU.mult, ALU.add).then_inc(ms_ready, 1)
                rsqrt(36)
                dve.wait_ge(rstd_ready, calls[0])
                k4 = k_t.rearrange("p t (a b) -> p t a b", a=8)
                for t in range(NT):
                    k3, kv3 = k4[:, t], kv_t[:, t, :].rearrange("p (a b) -> p a b", a=8)
                    steps.did(nc.vector.tensor_tensor(k3[:, :, 0:64], kv3[:, :, 0:64],
                                                      rstd[:, 8 * t:8 * t + 8].unsqueeze(2).to_broadcast([P, 8, 64]), ALU.mult))
                    steps.settle()
                    steps.did(nc.vector.tensor_tensor(k3[:, :, 0:64], k3[:, :, 0:64],
                                                      row("g_k", 0, 64).unsqueeze(1).to_broadcast([P, 8, 64]), ALU.mult))
                steps.did(nc.vector.tensor_tensor(k_pe[:], k_pe[:], rstd[:, 32:36].unsqueeze(2).to_broadcast([P, NT, 32]), ALU.mult))
                steps.settle()
                steps.did(nc.vector.tensor_tensor(k_pe[:], k_pe[:], row("g_k", 64, 32).unsqueeze(1).to_broadcast([P, NT, 32]), ALU.mult))
                dve.wait_ge(turned_ready, 1)
                cos, sin = (cos_sin[:, j, :].rearrange("p (a b) -> p a b", a=NT) for j in range(2))

                def turn(x1, x2, c, s, t4):
                    for j, (x, f) in enumerate(((x1, c), (x2, s), (x2, c), (x1, s))):
                        steps.settle()
                        steps.did(nc.vector.tensor_tensor(t4[j], x, f, ALU.mult))
                    steps.settle()
                    steps.did(nc.vector.tensor_tensor(x1, t4[0], t4[1], ALU.subtract))
                    steps.did(nc.vector.tensor_tensor(x2, t4[2], t4[3], ALU.add))

                dve.wait_ge(squared, 2 * NT)
                q4 = q_t.rearrange("p t (a b) -> p t a b", a=8)
                wide = [P, NT, 8, 16]
                turn(q4[:, :, :, 64:80], q4[:, :, :, 80:96], cos.unsqueeze(2).to_broadcast(wide), sin.unsqueeze(2).to_broadcast(wide),
                     [turn_tmp[:, j, :].rearrange("p (t a b) -> p t a b", t=NT, a=8) for j in range(4)])
                turn(k_pe[:, :, 0:16], k_pe[:, :, 16:32], cos, sin,
                     [turn_tmp[:, j, 0:64].rearrange("p (t b) -> p t b", t=NT) for j in range(4)])
                for t in range(NT):
                    steps.settle()
                    steps.did(nc.vector.tensor_copy(k4[:, t, :, 64:96], k_pe[:, t, :].unsqueeze(1).to_broadcast([P, 8, 32])))
                steps.settle()
                nc.vector.tensor_copy(stat[:, 0:1], k_pe[:, 0, 0:1]).then_inc(qk_ready, 1)

            def mla():
                def take_turned(name, dst, head):
                    m = AW[name, head]
                    work.wait_full(dve, m)
                    nc.vector.tensor_copy(dst[0:96, head % 2, :], work.bank(m)[0:96, :]).then_inc(work.done[m % BANKS], 1)

                take_turned("q", qT, 0)
                take_turned("k", kT, 0)
                for n in range(MLA_BLOCKS + 1):
                    if n < MLA_BLOCKS:
                        head, i = divmod(n, NT)
                        m = AW["scores", n]
                        work.wait_full(dve, m)
                        nc.vector.tensor_reduce(neg_m[:, n:n + 1], work.bank(m)[:, 0:(i + 1) * P], AX_X, ALU.max,
                                                negate=True).then_inc(m_ready, 1)
                        work.wait_done(dve, m)
                        steps.did(nc.vector.reciprocal(rden[:, n:n + 1], den[:, n:n + 1]))
                        steps.settle()
                        p = prob[:, n % 2, 0:(i + 1) * P]
                        nc.vector.tensor_scalar(p, p, rden[:, n:n + 1], None, ALU.mult).then_inc(prob_ready, 1)
                    if n and n % NT == 0:
                        head = n // NT - 1
                        m, q = AW["out", head], 64 * (head % 2)
                        work.wait_full(dve, m)
                        nc.vector.tensor_copy(y[q:q + 64, head // 2, :], work.bank(m)[q:q + 64, :]).then_inc(work.done[m % BANKS], 1)
                    if n % NT == 1 and n // NT + 1 < MLA_HEADS:
                        take_turned("q", qT, n // NT + 1)
                        take_turned("k", kT, n // NT + 1)

            def exponents(n):
                s = 1 << (n - 1)
                c4 = cum.rearrange("p c (n two s) -> p (c n) two s", two=2, s=s)
                e4 = pair[:, n % 2].rearrange("p c (n two s) -> p (c n) two s", two=2, s=s)
                left, right = c4[:, :, 0, :], c4[:, :, 1, :]
                mid = c4[:, :, 0, s - 1:s].to_broadcast([P, T // s, s])
                steps.did(nc.vector.tensor_tensor(e4[:, :, 0, :], mid, left, ALU.subtract))
                nc.vector.tensor_tensor(e4[:, :, 1, :], right, mid, ALU.subtract).then_inc(exponent_ready, 1)

            def pairs_of(n):
                s = 1 << (n - 1)
                cut = lambda x, half: x.rearrange("p c (n two s) -> p (c n) two s", two=2, s=s)[:, :, half, :]
                e = pair[:, n % 2]
                dve.wait_ge(decay_ready, n)
                steps.did(nc.vector.tensor_tensor(cut(e, 0), cut(e, 0), cut(gk, 0), ALU.mult))
                nc.vector.tensor_tensor(cut(e, 1), cut(e, 1), cut(gq, 1), ALU.mult).then_inc(pair_ready, 1)

            def take_level(n):
                for q in range(NT):
                    m = GW["level", n, q]
                    work.wait_full(dve, m)
                    acc = near[:, 2 * (q // 2):2 * (q // 2) + 2, :].rearrange("p t (c r b) -> p (t c) r b", c=2, r=2)[:, :, q % 2, :]
                    o = work.bank(m)[:].rearrange("p (a b) -> p a b", a=4)
                    if n == 0:
                        x = nc.vector.tensor_tensor(acc, o, ident[:].unsqueeze(1).to_broadcast([P, 4, P]), ALU.mult)
                    else:
                        work.wait_done(dve, GW["level", n - 1, q])
                        x = nc.vector.copy_predicated(
                            acc, level_mask[:, n - 1, :].bitcast(U32).unsqueeze(1).to_broadcast([P, 4, P]), o)
                    x.then_inc(work.done[m % BANKS], 1)

            def gla():
                g, m = base["gla_in"][1:]
                dve.wait_ge(logit_logged, 1)
                dve.wait_ge(masks_ready, N_MASKS)
                steps.did(nc.vector.scalar_tensor_tensor(logit, logit, 0.0, log_p, ALU.min, ALU.subtract))
                steps.settle()
                for c in range(2):
                    for i in range(NT):
                        tile = slice(i * P, (i + 1) * P)
                        steps.did(nc.vector.tensor_tensor_scan(cum[:, c, tile], ones[:], logit[:, c, tile], 0.0, ALU.mult, ALU.add))
                steps.settle()
                for c in range(2):
                    steps.did(nc.vector.tensor_scalar(tot16[:, c, :], cum[:, c, :].rearrange("p (a b) -> p a b", b=P)[:, :, P - 1],
                                                      1.0 / 16, None, ALU.mult))
                for c in range(4):
                    stream.wait_done(dve, g + c)
                exponents(1)
                pairs_of(1)
                exponents(2)
                take_level(0)
                pairs_of(2)
                for n in range(3, LEVELS):
                    take_level(n - 2)
                    exponents(n)
                    if n == 3:
                        for t in range(NT):
                            stream.wait_done(dve, g + 8 + t)
                            steps.did(nc.vector.tensor_tensor(gr[:, t, :], gr[:, t, :], row("gla_norm", 0, 512), ALU.mult))
                    pairs_of(n)
                steps.settle()
                nc.vector.tensor_copy(stat[:, 0:1], tot16[:, 0, 0:1]).then_inc(exponent_ready, 1)
                take_level(LEVELS - 2)
                dve.wait_ge(far_exp, 1)
                for c in range(2):
                    steps.did(nc.vector.tensor_tensor(kd[:, c, 0:3 * P], kd[:, c, 0:3 * P], gk[:, c, 0:3 * P], ALU.mult))
                    for slot, i in enumerate((1, 3, 2)):
                        v = qd[:, c, slot * P:(slot + 1) * P]
                        steps.did(nc.vector.tensor_tensor(v, v, gq[:, c, i * P:(i + 1) * P], ALU.mult))
                    steps.settle()
                    steps.did(nc.vector.tensor_scalar(kd[:, c, 3 * P:4 * P], kd[:, c, 0:P], exp_tot[:, c, 1:2], None, ALU.mult))
                    x = nc.vector.tensor_scalar(qd[:, c, 3 * P:4 * P], qd[:, c, P:2 * P], exp_tot[:, c, 2:3], None, ALU.mult)
                    if c == 0:
                        steps.did(x)
                    else:
                        x.then_inc(far_ready, 1)
                take_level(LEVELS - 1)
                for i in range(NT):
                    work.wait_done(dve, GW["level", LEVELS - 1, i])
                for i in range(NT):
                    nc.vector.tensor_copy(stat[:, 60 + i:61 + i], near[:, i, 0:1]).then_inc(near_ready, 1)
                for t in range(NT):
                    dve.wait_ge(go_squared, t + 1)
                    steps.did(nc.vector.tensor_reduce(stat[:, 4 * t:4 * t + 4], go_sq[:, t, :].rearrange("p (a b) -> p a b", a=4),
                                                      AX_X, ALU.add))
                steps.settle()
                nc.vector.tensor_scalar(ms[:, 0:16], stat[:, 0:16], 1.0 / P, EPS, ALU.mult, ALU.add).then_inc(ms_ready, 1)
                rsqrt(16)
                dve.wait_ge(rstd_ready, calls[0])
                for t in range(NT):
                    v = go[:, t, :].rearrange("p (a b) -> p a b", a=4)
                    steps.did(nc.vector.tensor_tensor(v, v, rstd[:, 4 * t:4 * t + 4].unsqueeze(2).to_broadcast([P, 4, P]), ALU.mult))
                    steps.settle()
                    nc.vector.tensor_tensor(go[:, t, :], go[:, t, :], gr[:, t, :], ALU.mult).then_inc(go_ready, 1)

            def swa():
                nc.vector.tensor_scalar(neg_sink[:], row("sinks", 0, 8), -1.0, None, ALU.mult).then_inc(sink_ready, 1)
                dve.wait_ge(sink_ready, 1)
                for n in range(SWA_BLOCKS + 1):
                    if n < SWA_BLOCKS:
                        m = SW["scores", n]
                        two = slice(2 * n, 2 * n + 2)
                        q_head = 4 * (n % 2) + n // 4
                        own = lambda x: x[:, q_head:q_head + 1].to_broadcast([P, 2])
                        work.wait_full(dve, m)
                        steps.did(nc.vector.tensor_reduce(neg_m[:, two], work.bank(m)[:].rearrange("p (s b) -> p s b", s=2),
                                                          AX_X, ALU.max, negate=True))
                        steps.settle()
                        nc.vector.tensor_tensor(neg_m[:, two], neg_m[:, two], own(neg_sink), ALU.min).then_inc(m_ready, 1)
                        dve.wait_ge(m_ready, MLSTM_BLOCKS + MLA_BLOCKS + n + 1)
                        nc.vector.tensor_tensor(sink_m[:, two], neg_m[:, two], own(row("sinks", 0, 8)), ALU.add).then_inc(sink_ready, 1)
                        work.wait_done(dve, m)
                        steps.did(nc.vector.tensor_tensor(den[:, two], den[:, two], sink_m[:, two], ALU.add))
                        steps.settle()
                        steps.did(nc.vector.reciprocal(rden[:, two], den[:, two]))
                        steps.settle()
                        for s in range(2):
                            p = sprob[:, n % 2, 256 * s:256 * s + 256]
                            x = nc.vector.tensor_scalar(p, p, rden[:, 2 * n + s:2 * n + s + 1], None, ALU.mult)
                            if s == 0:
                                steps.did(x)
                        x.then_inc(sprob_ready, 1)
                    if n and n % NT == 0:
                        j = n // NT - 1
                        m = SW["out", j]
                        work.wait_full(dve, m)
                        nc.vector.tensor_copy(branch[:, 4 + j, :], work.bank(m)[:]).then_inc(work.done[m % BANKS], 1)

            def pool():
                g = base["pool"][1]
                nc.vector.memset(pu[:, :, 0:16], 0.0).then_inc(pad_ready, 1)
                dve.wait_ge(pad_ready, 1)
                dve.wait_ge(freq_ready, 2)
                for c in range(4):
                    stream.wait_done(dve, g + c)
                    src = pu[:, c, :]
                    for r in range(c + 1):
                        k, lo = 1 << r, (2 << r) - 1
                        dst = psum_a[:, r % 2, :]
                        steps.did(nc.vector.tensor_tensor(dst[:, lo:16 + T], src[:, lo:16 + T], src[:, lo - k:16 + T - k], ALU.add))
                        steps.settle()
                        src = dst
                    w = 2 << c
                    steps.did(nc.vector.tensor_tensor(stat[:, 0:w], src[:, 16:16 + w], inv_count[:, 0:w], ALU.mult))
                    steps.did(nc.vector.scalar_tensor_tensor(pd[:, c, w:T], src[:, 16 + w:16 + T], 1.0 / w, pu[:, c, 16 + w:16 + T],
                                                             ALU.mult, ALU.subtract))
                    steps.settle()
                    nc.vector.tensor_tensor(pd[:, c, 0:w], stat[:, 0:w], pu[:, c, 16:16 + w], ALU.subtract).then_inc(pd_ready, 1)
                    dve.wait_ge(pd_ready, c + 1)

            def merge():
                g = base["merge"][1]
                for n in range(3 * DC):
                    c, b = divmod(n, 3)
                    o = g + 2 * n + 1
                    stream.wait_full(dve, o)
                    stream.wait_done(dve, o - 1)
                    if n == 0:
                        for i in range(NT):
                            work.wait_full(dve, SW["out", SWA_PAIRS - 1])
                    if b == 0:
                        nc.vector.tensor_tensor(y[:, c, :], stream.bank(o)[:], tmp[:, n % 2, :], ALU.mult).then_inc(stream.done[o % BANKS], 1)
                        stream.wait_done(dve, o)
                    else:
                        steps.did(nc.vector.tensor_tensor(tmp[:, 2 + n % 2, :], stream.bank(o)[:], tmp[:, n % 2, :], ALU.mult))
                        steps.settle()
                        nc.vector.tensor_tensor(y[:, c, :], y[:, c, :], tmp[:, 2 + n % 2, :], ALU.add).then_inc(stream.done[o % BANKS], 1)
                        stream.wait_done(dve, o)

            def convffn():
                g = base["convffn"][1]

                def body(i):
                    for j in range(4):
                        b, gate = j // 2, j % 2 == 0
                        c = 2 * i + b + (0 if gate else FC)
                        dve.wait_ge(conv_started, 4 * i + j + 1)
                        o = stream.bank(g + j)
                        nc.vector.scalar_tensor_tensor(tmp[:, j, 1:T], o[:, 0:T - 1], cols[:, bass.ds(c + COLS["cw1"], 1)],
                                                       tmp[:, j, 1:T], ALU.mult, ALU.add).then_inc(dve_steps, 1)
                        dve.wait_ge(dve_steps, steps.n + 4 * i + j + 1)
                        nc.vector.scalar_tensor_tensor(tmp[:, j, 2:T], o[:, 0:T - 2], cols[:, bass.ds(c + COLS["cw0"], 1)],
                                                       tmp[:, j, 2:T], ALU.mult, ALU.add).then_inc(stream.done[(g + j) % BANKS], 1)
                        if not gate:
                            dve.wait_ge(gelu_ready, 2 * i + b + 1)
                            dve.wait_ge(stream.done[(g + j) % BANKS], i + (g + j) // BANKS + 1)
                            nc.vector.tensor_tensor(act[:, bass.ds(2 * i + b, 1), :], tmp[:, j - 1, :].unsqueeze(1),
                                                    tmp[:, j, :].unsqueeze(1), ALU.mult).then_inc(act_ready, 1)

                with dve.Fori(0, 2 * FC // 4) as i:
                    body(i)
                steps.n += 2 * FC

            rope_angles()
            norm("norm_mix0", "g_mix0")
            even_in()
            add_outs(base["even_out"][1], DC)
            if on("norm_ffn0"): norm("norm_ffn0", "g_ffn0")
            if on("ffn0"): ffn("ffn0")
            if on("norm_ple0"): norm("norm_ple0", "g_ple0")
            if on("ple0"): ple("ple0")
            if on("norm_mix1"): norm("norm_mix1", "g_mix1")
            if on("odd_in"): odd_in()
            if on("mlstm"): mlstm()
            if on("mla_up"): mla_up()
            if on("mla"): mla()
            if on("odd_out"): add_outs(base["odd_out"][1], DC)
            if on("norm_ffn1"): norm("norm_ffn1", "g_ffn1")
            if on("ffn1"): ffn("ffn1")
            if on("norm_ple1"): norm("norm_ple1", "g_ple1")
            if on("ple1"): ple("ple1")
            if on("norm_mix2"): norm("norm_mix2", "mix_pre")
            if on("gla"): gla()
            if on("swa"): swa()
            if on("pool"): pool()
            if on("merge"): merge()
            if on("norm_post"): norm("norm_post", "mix_post")
            if on("norm_ffn2"): norm("norm_ffn2", "ffn_pre")
            if on("convffn"): convffn()
            if on("norm_last"): norm("norm_last", "ffn_post")


def feature_units(w):
    k, n = w.shape
    return w.reshape(k // P, P, n // P, P).transpose(2, 1, 0, 3).reshape(n // P, P, k)


def token_units(w):
    return w.reshape(4, 2, P, 512).transpose(0, 2, 1, 3).reshape(4, P, 1024)


def down_units(w):
    return w.reshape(2, 11, P, DC, P).transpose(3, 0, 2, 1, 4).reshape(2 * DC, P, 11 * P)


def pairs(gate, up):
    import numpy as np
    return np.stack([feature_units(gate), feature_units(up)], 1).reshape(2 * FC, P, D)


def chunks(v):
    return v.reshape(-1, P).T


def tokens_first(x):
    return x.reshape(T, -1, P).transpose(2, 1, 0)


def lay_out(i):
    import numpy as np
    o = {}
    o["x"] = tokens_first(i["x"][0])
    o["p0"] = tokens_first(i["p"][0, 0])
    c = {"g_mix0": i["g_mix"][0], "g_ffn0": i["g_ffn"][0], "g_ple0": i["g_ple"][0],
         "g_mix1": i["g_mix"][1], "g_ffn1": i["g_ffn"][1], "g_ple1": i["g_ple"][1],
         "mix_pre": i["norm_mix_pre_2"], "mix_post": i["norm_mix_post_2"],
         "ffn_pre": i["norm_ffn_pre_2"], "ffn_post": i["norm_ffn_post_2"],
         "w_conv": i["ev_w_conv"], "g_qa": i["od_g_qa"], "g_kva": i["od_g_kva"], "gla_b": i["gla_b_gate_2"],
         "pool_scale": i["pool_scale_2"], "cw0": i["ffn_conv_w_2"][0, 0], "cw1": i["ffn_conv_w_2"][0, 1],
         "cw2": i["ffn_conv_w_2"][0, 2], "cb": i["ffn_conv_b_2"]}
    o["cols"] = np.concatenate([chunks(c[n]) for n in COLS], 1)
    r = {"g_v": i["ev_g_v"], "g_q": i["od_g_q"], "g_k": i["od_g_k"], "b_gate": i["od_b_gate"], "g_mh": i["od_g_mh"],
         "gla_norm": i["gla_norm_2"], "sinks": i["swa_sinks_2"]}
    o["rows"] = np.concatenate([r[n].reshape(-1) for n in ROWS])
    o["w_s"] = i["ev_w_s"][0].transpose(2, 0, 1)
    o["b_s"] = i["ev_b_s"]
    w = i["ev_w_in"][0]
    fu = feature_units(w[:, :2048]).reshape(4, 4, P, D)
    o["w_even"] = np.concatenate([fu[[1, 2, 0]].transpose(1, 0, 2, 3).reshape(12, P, D), fu[3], token_units(w[:, 2048:])])
    o["w_even_out"] = feature_units(i["ev_w_out"][0])
    for l in range(2):
        o[f"w_up{l}"] = pairs(i["w_gate"][l], i["w_up"][l])
        o[f"w_down{l}"] = down_units(i["w_down"][l])
        o[f"w_ple{l}"] = np.concatenate([feature_units(i["w_ple_gate"][l]), feature_units(i["w_ple_proj"][l])], 2)
    o["p1"] = tokens_first(i["p"][1, 0])
    w = i["od_w_in"][0]
    at = np.cumsum([0, 384, 256, 32, 256, 256, 512, 512, 8])
    q_lat, kv_lat, k_pe, mq, mk, mv, mo, gates = (w[:, x:y] for x, y in zip(at[:-1], at[1:]))
    o["w_odd"] = np.concatenate([feature_units(v) for v in (q_lat, kv_lat, mq, mk)] + [token_units(v) for v in (mv, mo)])
    o["w_small"] = np.concatenate([k_pe, gates], 1).reshape(DC, P, 40).transpose(1, 0, 2)
    o["positions"] = i["positions"].reshape(NT, P).T
    o["w_q_up"] = i["od_w_q_up"][0].reshape(3, P, 768)
    o["w_kv_up"] = i["od_w_kv_up"][0].reshape(2, P, 1024)
    o["w_odd_out"] = feature_units(i["od_w_out"][0])
    w = i["w_in_2"][0]
    at = np.cumsum([0, 256, 256, 512, 16, 512, 512, 128, 128, 512, 3072])
    g_q, g_k, g_v, low, g_r, s_q, s_k, s_v, p_u, gate = (w[:, x:y] for x, y in zip(at[:-1], at[1:]))
    o["w_gla"] = np.concatenate([feature_units(g_q), feature_units(g_k), token_units(g_v), token_units(g_r)])
    o["w_low"] = low.reshape(DC, P, 16).transpose(1, 0, 2)
    o["w_gate_up"] = i["gla_w_gate_up_2"][0]
    s_q = s_q.reshape(D, 2, 4, 64).transpose(0, 2, 1, 3).reshape(D, 512)
    o["w_swa"] = np.concatenate([feature_units(s_q), feature_units(s_k), feature_units(s_v)])
    o["w_pool"] = feature_units(p_u)
    o["w_group"] = i["pool_w_2"][0].transpose(1, 0, 2).reshape(1, P, 512)
    swa = i["w_branch_swa_2"][0].reshape(2, 4, 64, D).transpose(1, 0, 2, 3).reshape(512, D)
    o["w_merge"] = np.stack([np.concatenate([feature_units(gate[:, D * b:D * b + D]), feature_units(v)], 2)
                             for b, v in enumerate((i["w_branch_gla_2"][0], swa, i["w_branch_pool_2"][0]))], 1).reshape(3 * DC, P, 12 * P)
    o["w_block_out"] = feature_units(i["w_out_2"][0])
    w = i["ffn_w_up_2"][0]
    o["w_up2"] = pairs(w[:, :FF], w[:, FF:])
    o["w_down2"] = down_units(i["ffn_w_down_2"][0])
    return o


def kernel(**inputs):
    import numpy as np
    import concourse.bacc as bacc
    from concourse.bass_utils import run_bass_kernel_spmd

    nc = bacc.Bacc("TRN2", target_bir_lowering=False, num_devices=1)
    arrays, aps = {}, {}
    for name, v in lay_out({k: np.asarray(v) for k, v in inputs.items()}).items():
        arrays[f"in_{name}"] = np.ascontiguousarray(v)
        aps[name] = nc.dram_tensor(f"in_{name}", v.shape, mybir.dt.from_np(v.dtype), kind="ExternalInput").ap()
    out = nc.dram_tensor("out_dram", (P, DC, T), F32, kind="ExternalOutput").ap()
    build(nc, aps, out)
    r = run_bass_kernel_spmd(nc, [arrays], core_ids=[0])
    return r.results[0]["out_dram"].transpose(2, 1, 0).reshape(1, T, D)
```

```python
from contextlib import ExitStack

import concourse.bass as bass
from concourse import mybir

F32 = mybir.dt.float32
F32R = mybir.dt.float32r
I32 = mybir.dt.int32
U32 = mybir.dt.uint32
ALU = mybir.AluOpType
ACT = mybir.ActivationFunctionType
AX_X = mybir.AxisListType.X

P = 128
T = 512
NT = T // P
D = 1024
DC = D // P
EPS = 1e-6
NEG = -1e30
FF = 2816
FC = FF // P
SLOTS = 2
SLOT = 12 * P
BANKS = 4
LNEXP = "natural_log_exp_and_others"
FFN_UNITS = 2 * FC + 2 * DC
FFN_OUTS = 2 * FC + DC

STAGES = [
    ("norm_mix0", 0, 0, 2),
    ("even_in", 20, 20, 4),
    ("even_out", 8, 8, 0),
    ("norm_ffn0", 0, 0, 2),
    ("ffn0", FFN_UNITS, FFN_OUTS, 0),
    ("norm_ple0", 0, 0, 2),
    ("ple0", 8, 16, 0),
    ("norm_mix1", 0, 0, 2),
    ("odd_in", 17, 17, 2),
    ("mlstm", 0, 0, 69),
    ("mla_up", 4, 16, 0),
    ("mla", 0, 0, 88),
    ("odd_out", 8, 8, 0),
    ("norm_ffn1", 0, 0, 2),
    ("ffn1", FFN_UNITS, FFN_OUTS, 0),
    ("norm_ple1", 0, 0, 2),
    ("ple1", 8, 16, 0),
    ("norm_mix2", 0, 0, 2),
    ("gla_in", 12, 12, 3),
    ("gla", 0, 0, 48),
    ("swa", 6, 6, 36),
    ("pool", 5, 8, 0),
    ("merge", 24, 48, 0),
    ("block_out", 8, 8, 0),
    ("norm_post", 0, 0, 2),
    ("norm_ffn2", 0, 0, 2),
    ("convffn", FFN_UNITS, FFN_OUTS, 0),
    ("norm_last", 0, 0, 2),
]

COLS = {}
COLS_N = 0
for _name, _n in (
    ("g_mix0", 8), ("g_ffn0", 8), ("g_ple0", 8), ("g_mix1", 8), ("g_ffn1", 8), ("g_ple1", 8),
    ("mix_pre", 8), ("mix_post", 8), ("ffn_pre", 8), ("ffn_post", 8),
    ("w_conv", 12), ("g_qa", 3), ("g_kva", 2), ("gla_b", 2), ("pool_scale", 4),
    ("cw0", 44), ("cw1", 44), ("cw2", 44), ("cb", 44),
):
    COLS[_name] = COLS_N
    COLS_N += _n

ROWS = {}
ROWS_N = 0
for _name, _n in (("g_v", 512), ("g_q", 96), ("g_k", 96), ("b_gate", 8), ("g_mh", 512), ("gla_norm", 512), ("sinks", 8)):
    ROWS[_name] = ROWS_N
    ROWS_N += _n


def stage_bases():
    u = g = m = 0
    base = {}
    for name, units, outs, works in STAGES:
        base[name] = (u, g, m)
        u, g, m = u + units, g + outs, m + works
    return base, u


class Turns:

    def __init__(self, banks, full, done):
        self.banks, self.full, self.done = banks, full, done

    def bank(self, n):
        return self.banks[n % BANKS]

    def wait_full(self, eng, n, more=0):
        eng.wait_ge(self.full[n % BANKS], more + n // BANKS + 1)

    def wait_done(self, eng, n, more=0):
        eng.wait_ge(self.done[n % BANKS], more + n // BANKS + 1)

    def wait_free(self, eng, n, more=0):
        if n >= BANKS:
            eng.wait_ge(self.done[n % BANKS], more + n // BANKS)


class Steps:

    def __init__(self, eng, sem):
        self.eng, self.sem, self.n = eng, sem, 0

    def did(self, ins):
        ins.then_inc(self.sem, 1)
        self.n = self.n + 1

    def settle(self):
        self.eng.wait_ge(self.sem, self.n)


RSQRTS = {"norm_mix0": 1, "norm_ffn0": 3, "norm_ple0": 4, "norm_mix1": 5, "norm_ffn1": 10, "norm_ple1": 11,
          "norm_mix2": 12, "norm_post": 14, "norm_ffn2": 15, "norm_last": 16}
DUMP = None
FFN_NO = {"ffn0": 0, "ffn1": 1, "convffn": 2}
MLSTM_HEADS = 4
MLSTM_BLOCKS = MLSTM_HEADS * NT
MLA_HEADS = 8
GLA_HEADS = 4
LEVELS = 8
SWA_PAIRS = 4
SWA_BLOCKS = SWA_PAIRS * NT
MLA_BLOCKS = MLA_HEADS * NT
PI = 3.141592653589793
TWO_PI = 2 * PI
ROUND = 12582912.0
TURN_PARTS = (6.28125, 0.0019350051879882812, 3.0199159795074593e-07)


def on(name):
    return any(s[0] == name for s in STAGES)


def ffn_units(up, down):
    return [("out", up, i) for i in range(2 * FC)] + [(("half", "out")[i % 2], down, i) for i in range(2 * DC)]


def fm(array, n, at=0):
    return [("out", array, at + i) for i in range(n)]


def tm(array, at=0):
    return [(("part", "part", "part", "tokens")[i], array, at + i) for i in range(4)]


UNITS = {
    "even_in": fm("w_even", 16) + tm("w_even", 16),
    "even_out": fm("w_even_out", 8),
    "ffn0": ffn_units("w_up0", "w_down0"),
    "ple0": [("two", "w_ple0", i) for i in range(8)],
    "odd_in": fm("w_odd", 9) + tm("w_odd", 9) + tm("w_odd", 13),
    "mla_up": [("tokens", "w_q_up", 0), ("tokens", "w_q_up", 1), ("tokens", "w_kv_up", 0), ("tokens", "w_kv_up", 1)],
    "odd_out": fm("w_odd_out", 8),
    "ffn1": ffn_units("w_up1", "w_down1"),
    "ple1": [("two", "w_ple1", i) for i in range(8)],
    "gla_in": fm("w_gla", 4) + tm("w_gla", 4) + tm("w_gla", 8),
    "swa": fm("w_swa", 6),
    "pool": fm("w_pool", 4) + [("four", "w_group", 0)],
    "merge": [("two", "w_merge", i) for i in range(24)],
    "block_out": fm("w_block_out", 8),
    "convffn": ffn_units("w_up2", "w_down2"),
}
BEFORE = {"norm_ffn0": "even_out", "norm_ple0": "ffn0", "norm_mix1": "ple0", "norm_ffn1": "odd_out",
          "norm_ple1": "ffn1", "norm_mix2": "ple1", "norm_post": "block_out", "norm_last": "convffn"}


def gla_order():
    return ([("level", n, i) for n in range(LEVELS) for i in range(NT)]
            + [(part, head) for head in range(GLA_HEADS) for part in ("far_a", "far_b")]
            + [("o", i) for i in range(NT)] + [("y", head) for head in range(GLA_HEADS)])


def swa_order():
    order = []
    for n in range(SWA_BLOCKS + 1):
        if n < SWA_BLOCKS:
            order.append(("scores", n))
        if n:
            order.append(("turned", n - 1))
        if n and n % NT == 0:
            order.append(("out", n // NT - 1))
    return order


def mlstm_order():
    order = [("sums", 0)]
    for n in range(MLSTM_BLOCKS + 1):
        if n < MLSTM_BLOCKS:
            order += [("decay", n), ("scores", n)]
        if n:
            order += [("turned", n - 1), ("out", n - 1)]
    return order + [("y", head) for head in range(MLSTM_HEADS)]


def mla_order():
    order = [("q", 0), ("k", 0)]
    for n in range(MLA_BLOCKS + 1):
        if n < MLA_BLOCKS:
            order.append(("scores", n))
        if n:
            order.append(("turned", n - 1))
        if n and n % NT == 0:
            order.append(("out", n // NT - 1))
        if n % NT == 1 and n // NT + 1 < MLA_HEADS:
            order += [("q", n // NT + 1), ("k", n // NT + 1)]
    return order


def build(nc, a, out):
    base, n_units = stage_bases()

    with ExitStack() as ctx:
        def sb(name, shape, dt=F32):
            return ctx.enter_context(nc.sbuf_tensor("s_" + name, shape, dt))

        def sem(name):
            return ctx.enter_context(nc.semaphore(name))

        def sems(name, n):
            return [sem(f"{name}{i}") for i in range(n)]

        h = sb("h", [P, DC, T])
        ring = sb("ring", [P, SLOTS, SLOT])
        split_ring = sb("split_ring", [P, SLOTS, 2, SLOT], F32R)
        arena_at = nc.sbuf_base
        arena = sb("arena", [P, 2 * DC * T + 2 * FC * T])
        tmp = sb("tmp", [P, 4, T])
        cols = sb("cols", [P, COLS_N])
        rows = sb("rows", [P, ROWS_N])
        zero = sb("zero", [P, 1])
        ident = sb("ident", [P, P])
        ones = sb("ones", [P, P])
        upto = sb("upto", [P, P])
        below = sb("below", [P, P])
        neg_after = sb("neg_after", [P, P])
        neg_until = sb("neg_until", [P, P])
        ms = sb("ms", [P, 64])
        ln_ms = sb("ln_ms", [P, 64])
        rs0 = sb("rs0", [P, 64])
        rt = sb("rt", [P, 2, 64])
        rstd = sb("rstd", [P, 64])
        rstd_rows = sb("rstd_rows", [P, T])
        stat = sb("stat", [P, 64])

        def region(at, *shape):
            n = 1
            for s in shape:
                n *= s
            v = arena[:, at:at + n]
            if len(shape) == 2:
                v = v.rearrange("p (a b) -> p a b", a=shape[0])
            if len(shape) == 3:
                v = v.rearrange("p (a b c) -> p a b c", a=shape[0], b=shape[1])
            return v, at + n

        def halves_of(name, at, n):
            v = nc.alloc_sbuf_tensor_at("s_" + name, [P, 2, n, T], F32R, offset=arena_at + 4 * at)
            return v[:], at + 2 * n * T

        hn, A = halves_of("hn", 0, DC)
        act, _ = halves_of("act", A, FC)
        y, Y_END = halves_of("y", A, DC)
        sq_hn, at = region(0, DC, T)
        o_buf, _ = region(at, DC, T)
        sq_rest, _ = region(A, DC, T)
        p_raw, at = region(Y_END + 4096, 2, T)
        p_in, _ = halves_of("p_in", at, 2)

        ws, at = region(Y_END, 8, P)
        z_pad, at = region(at, 2, 2 + T)
        conv, at = region(at, 2, T)
        u_g, at = region(at, 4, T)
        v_t, at = region(at, NT, 512)
        v_sq, at = region(at, 2, 512)
        b_row = arena[0:1, at:at + 8 * P].rearrange("p (a b) -> p a b", a=8)
        lat, LAT_END = halves_of("lat", Y_END, 5)
        mq, at = region(LAT_END, 2, T)
        mk, at = region(at, 2, T)
        mv, at = region(at, NT, 512)
        mo, at = region(at, NT, 512)
        lat_sq, _ = region(at, 5, T)
        rdiag, at = region(0, MLSTM_BLOCKS, P)
        dec, at = region(at, 2, T)
        sT, at = region(at, 2, T)
        hv, at = region(at, NT, 512)
        hv_sq, at = region(at, NT, 512)
        assert at <= A
        kv_t, at = region(0, NT, 1024)
        qk_sq, _ = region(at, 2, 1024)
        turn_tmp, _ = region(at, 4, T)
        probT, at = region(at, 4, T)
        probT2, at = region(at, 4, T)
        q_t, at = region(LAT_END, NT, 768)
        k_t, at = region(at, NT, 768)
        qT, at = region(at, 2, T)
        kT, at = region(at, 2, T)
        prob, at = region(at, 2, T)
        branch = []
        at = A
        for b in range(3):
            v, at = halves_of(f"branch{b}", at, 4)
            branch.append(v)
        BRANCH_END = at
        gq, at = region(A, 2, T)
        gk, at = region(at, 2, T)
        cum, at = region(at, 2, T)
        kd, at = region(at, 2, T)
        gv, at = region(at, NT, 512)
        gr, at = region(at, NT, 512)
        pair, at = region(at, 2, 2, T)
        near, at = region(at, NT, 512)
        far, at = region(at, GLA_HEADS, 768)
        qd, at = region(at, 2, T)
        go, at = region(at, NT, 512)
        go_sq = pair.rearrange("p a b c -> p (a b) c")
        logit = near[:, 0:2, :]
        log_p = near[:, 2:4, :]
        sqT, at = region(BRANCH_END, 4, T)
        skT, at = region(at, 1, T)
        sv, at = region(at, NT, P)
        sprob, at = region(at, 2, T)
        sprobT, at = region(at, NT, T)
        pu, at = region(BRANCH_END, 4, 16 + T)
        psum_a, at = region(at, 2, 16 + T)
        pd, at = halves_of("pd", at, 4)
        merged, at = halves_of("merged", BRANCH_END, DC)
        g_low = tmp[0:16, 3, :]
        w_low = sb("w_low", [P, DC, 16])
        w_gate_up = sb("w_gate_up", [16, 256])
        level_mask = sb("level_mask", [P, LEVELS - 1, P])
        tot16 = sb("tot16", [P, 2, NT])
        exp_tot = sb("exp_tot", [P, 2, NT])
        neg_sink = sb("neg_sink", [P, 8])
        sink_m = sb("sink_m", [P, 32])
        inv_count = sb("inv_count", [P, 16])
        GW = {k: base["gla"][2] + i for i, k in enumerate(gla_order())} if on("gla") else {}
        SW = {k: base["swa"][2] + i for i, k in enumerate(swa_order())} if on("swa") else {}
        w_small = sb("w_small", [P, DC, 40])
        gates = sb("gates", [P, NT, 8])
        k_pe = sb("k_pe", [P, NT, 32])
        lat_ss = sb("lat_ss", [P, 8])
        lat_rs = sb("lat_rs", [P, 8])
        pos_i = sb("pos_i", [P, NT], I32)
        inv_freq = sb("inv_freq", [P, 16])
        angle = sb("angle", [P, 5, NT * 16])
        cos_sin = sb("cos_sin", [P, 2, NT * 16])
        lf = sb("lf", [P, NT, 4])
        gl = sb("gl", [P, 4, 16])
        neg_sum = sb("neg_sum", [P, 16])
        neg_m = sb("neg_m", [P, 32])
        exp_m = sb("exp_m", [P, 16])
        den = sb("den", [P, 32])
        rden = sb("rden", [P, 32])
        MW = {k: base["mlstm"][2] + i for i, k in enumerate(mlstm_order())} if on("mlstm") else {}
        AW = {k: base["mla"][2] + i for i, k in enumerate(mla_order())} if on("mla") else {}
        N_TABLES = 8
        N_MASKS = 1 + 3 * (LEVELS - 1)
        N_CONSTS = 12

        def col(name, c=0, n=1):
            return cols[:, COLS[name] + c:COLS[name] + c + n]

        def row(name, at, n):
            return rows[:, ROWS[name] + at:ROWS[name] + at + n]

        stream = Turns([ctx.enter_context(nc.psum_tensor(f"stream_bank{i}", [P, 512], F32)) for i in range(BANKS)],
                       sems("stream_full", BANKS), sems("stream_done", BANKS))
        work = Turns([ctx.enter_context(nc.psum_tensor(f"work_bank{i}", [P, 512], F32)) for i in range(BANKS)],
                     sems("work_full", BANKS), sems("work_done", BANKS))
        slot_loaded = sems("slot_loaded", SLOTS)
        x_loaded = sem("x_loaded")
        tables_loaded = sem("tables_loaded")
        p_loaded = sem("p_loaded")
        consts_ready = sem("consts_ready")
        sq_ready = sem("sq_ready")
        ms_ready = sem("ms_ready")
        rs_guessed = sem("rs_guessed")
        rstd_ready = sem("rstd_ready")
        hn_ready = sem("hn_ready")
        k_units = sem("k_units")
        down_half = sem("down_half")
        act_steps = sem("act_steps")
        dve_steps = sem("dve_steps")
        out_stored = sem("out_stored")
        conv_in = sem("conv_in")
        v_gelu = sem("v_gelu")
        v_square = sem("v_square")
        v_ready = sem("v_ready")
        lat_squared = sem("lat_squared")
        gates_ready = sem("gates_ready")
        log_ready = sem("log_ready")
        lf_ready = sem("lf_ready")
        rdiag_ready = sem("rdiag_ready")
        m_ready = sem("m_ready")
        exp_m_ready = sem("exp_m_ready")
        rden_ready = sem("rden_ready")
        hv_squared = sem("hv_squared")
        hv_ready = sem("hv_ready")
        lat_rs_ready = sem("lat_rs_ready")
        squared = sem("squared")
        summed = sem("summed")
        qk_ready = sem("qk_ready")
        prob_ready = sem("prob_ready")
        angle_ready = sem("angle_ready")
        turned_ready = sem("turned_ready")
        freq_ready = sem("freq_ready")
        logit_logged = sem("logit_logged")
        exponent_ready = sem("exponent_ready")
        decay_ready = sem("decay_ready")
        pair_ready = sem("pair_ready")
        near_ready = sem("near_ready")
        masks_ready = sem("masks_ready")
        far_exp = sem("far_exp")
        far_ready = sem("far_ready")
        go_squared = sem("go_squared")
        go_ready = sem("go_ready")
        sink_ready = sem("sink_ready")
        sprob_ready = sem("sprob_ready")
        pad_ready = sem("pad_ready")
        pd_ready = sem("pd_ready")
        h_updated = sem("h_updated")
        conv_started = sem("conv_started")
        gelu_ready = sem("gelu_ready")
        act_ready = sem("act_ready")
        split_ready = sems("split_ready", SLOTS)
        w_high = sem("w_high")
        conv_product = sem("conv_product")
        v_made = sem("v_made")
        hi_made = sem("hi_made")
        y_ready = sem("y_ready")
        lat_ready = sem("lat_ready")
        branch_ready = sem("branch_ready")
        p_split = sem("p_split")

        norm_no = {n: i for i, n in enumerate(s[0] for s in STAGES if s[0].startswith("norm"))}
        hn_no = {n: i for i, n in enumerate(n for n in norm_no if n not in ("norm_post", "norm_last"))}

        def h_out(stage, c):
            g = base[stage][1]
            if "ffn" in stage:
                return g + 2 * FC + c
            return g + (2 * c + 1 if stage.startswith("ple") else c)

        def squares_of(stage):
            return sq_rest if stage in ("norm_mix0", "norm_mix1", "norm_mix2") else sq_hn

        def h_ready(eng, norm, c):
            if norm == "norm_ffn2":
                eng.wait_ge(h_updated, c + 1)
            elif norm == "norm_mix0":
                eng.wait_ge(x_loaded, 16)
            else:
                stream.wait_done(eng, h_out(BEFORE[norm], c))

        freed, weights = [], []
        quarters = firsts = 0
        for name, units, _, _ in STAGES:
            g = base[name][1]
            for kind, array, i in UNITS.get(name, []):
                weights.append((array, i))
                if kind == "part":
                    quarters += 1
                    freed.append((k_units, quarters))
                    continue
                if kind == "half":
                    firsts += 1
                    freed.append((down_half, firsts))
                    continue
                g += {"out": 1, "two": 2, "tokens": NT, "four": 4}[kind]
                freed.append((stream.full[(g - 1) % BANKS], (g - 1) // BANKS + 1))
        assert len(weights) == n_units, (len(weights), n_units)

        def wait_unit(eng, u, more=0):
            eng.wait_ge(split_ready[u % SLOTS], more + u // SLOTS + 1)

        block = ctx.enter_context(nc.Block())

        def final(sp, c):
            if on("norm_last"):
                sp.wait_ge(h_updated, DC + c + 1)
                return
            if DUMP is None:
                stream.wait_done(sp, h_out(STAGES[-1][0], c))
                return
            for r in (stream, work):
                n = sum(s[2 if r is stream else 3] for s in STAGES)
                for q in range(n - BANKS, n):
                    r.wait_done(sp, q)

        @block.sync
        def _(sp):
            sp.dma_start(h[:], a["x"]).then_inc(x_loaded, 16)
            for name, units, _, _ in STAGES:
                u0 = base[name][0]
                u = u0
                while u < u0 + units:
                    array, i = weights[u]
                    n = a[array].shape[2]
                    if u - u0 == SLOTS and FFN_UNITS == units:
                        with sp.Fori(1, 2 * FC // SLOTS) as r:
                            for j in range(SLOTS):
                                sp.wait_ge(split_ready[(u + j) % SLOTS], r + (u0 + j) // SLOTS)
                                sp.dma_start(ring[:, (u + j) % SLOTS, 0:n].unsqueeze(1),
                                             a[array][bass.ds(SLOTS * r + j, 1)].rearrange("a p n -> p a n")).then_inc(
                                    slot_loaded[(u + j) % SLOTS], 16)
                        u = u0 + 2 * FC
                        continue
                    if u >= SLOTS:
                        sp.wait_ge(split_ready[u % SLOTS], u // SLOTS)
                    sp.dma_start(ring[:, u % SLOTS, 0:n], a[array][i]).then_inc(slot_loaded[u % SLOTS], 16)
                    u += 1
            for c in range(DC):
                final(sp, c)
                sp.dma_start(out[:, c, :], h[:, c, :]).then_inc(out_stored, 16)
            sp.wait_ge(turned_ready, 1)
            sp.wait_ge(out_stored, 16 * DC)

        @block.gpsimd
        def _(pool):
            def split(u, n, r=0, more=None, free=None):
                s = u % SLOTS
                pool.wait_ge(slot_loaded[s], 16 * (r + u // SLOTS + 1))
                if free is not None:
                    pool.wait_ge(*free)
                hi = split_ring[:, s, 0, 0:n]
                nc.gpsimd.tensor_tensor(hi, ring[:, s, 0:n], zero[:].to_broadcast([P, n]), ALU.add).then_inc(w_high, 1)
                pool.wait_ge(w_high, (u if more is None else more) + 1)
                nc.gpsimd.tensor_tensor(split_ring[:, s, 1, 0:n], ring[:, s, 0:n], hi.bitcast(F32), ALU.subtract).then_inc(
                    split_ready[s], 1)

            def split_stage(name, skip=0):
                u0, g, _ = base[name]
                units = dict((s[0], s[1]) for s in STAGES)[name]
                u = u0 + skip
                while u < u0 + units:
                    if u - u0 == 4 and units == FFN_UNITS:
                        with pool.Fori(1, 2 * FC // 4) as i:
                            for j in range(4):
                                q = g + j - SLOTS
                                split(u0 + j, D, r=(4 // SLOTS) * i, more=u0 + j + 4 * i, free=(stream.full[q % BANKS], i + q // BANKS + 1))
                        u = u0 + 2 * FC
                        continue
                    split(u, a[weights[u][0]].shape[2], free=freed[u - SLOTS] if u >= SLOTS else None)
                    u += 1

            steps = Steps(pool, consts_ready)
            nc.gpsimd.memset(zero[:], 0.0)
            for t, v in ((ident, 0.0), (ones, 1.0), (upto, 1.0), (below, 1.0), (neg_after, 0.0), (neg_until, 0.0)):
                steps.did(nc.gpsimd.memset(t[:], v))
            steps.settle()
            for t, op, fill, at, step, mult in (
                (ident, ALU.not_equal, 1.0, 0, -1, 1), (upto, ALU.is_ge, 0.0, 0, 1, -1),
                (below, ALU.is_ge, 0.0, -1, -1, 1), (neg_after, ALU.is_ge, NEG, 0, -1, 1),
                (neg_until, ALU.is_ge, NEG, -1, 1, -1),
            ):
                steps.did(nc.gpsimd.affine_select(out=t[:], in_=t[:], compare_op=op, fill=fill, base=at,
                                                  pattern=[[step, P]], channel_multiplier=mult))
            for j in range(16):
                last = nc.gpsimd.memset(inv_freq[:, j:j + 1], float(10000.0 ** (-j / 16)))
            last.then_inc(freq_ready, 1)
            for j in range(16):
                last = nc.gpsimd.memset(inv_count[:, j:j + 1], 1.0 / (j + 1))
            last.then_inc(freq_ready, 1)
            masks = Steps(pool, masks_ready)
            masks.did(nc.gpsimd.memset(level_mask[:], 0.0))
            for n in range(1, LEVELS):
                s = 1 << (n - 1)
                v = level_mask[:, n - 1, :].rearrange("p (n two s) -> p n two s", two=2, s=s)[:, :, 1, :]
                masks.settle()
                masks.did(nc.gpsimd.memset(v, 1.0))
                masks.settle()
                masks.did(nc.gpsimd.affine_select(out=v, in_=v, compare_op=ALU.is_ge, fill=0.0, base=0,
                                                  pattern=[[-2 * s, P // (2 * s)], [0, s]], channel_multiplier=1))
                masks.settle()
                masks.did(nc.gpsimd.affine_select(out=v, in_=v, compare_op=ALU.is_ge, fill=0.0, base=s - 1,
                                                  pattern=[[2 * s, P // (2 * s)], [0, s]], channel_multiplier=-1))
            for u in range(SLOTS):
                split(u, D)
            pool.wait_ge(tables_loaded, 16 * N_TABLES)
            steps.did(nc.gpsimd.affine_select(out=ws, in_=ws, compare_op=ALU.is_ge, fill=0.0, base=0,
                                              pattern=[[0, 8], [1, P]], channel_multiplier=-1))
            split_stage("even_in", skip=SLOTS)
            for name, units, _, _ in STAGES:
                if units and name != "even_in":
                    split_stage(name)

        @block.tensor
        def _(pe):
            def norm(stage):
                k, m = norm_no[stage], base[stage][2]
                squares = squares_of(stage)
                work.wait_free(pe, m)
                for c in range(DC):
                    pe.wait_ge(sq_ready, DC * k + c + 1)
                    for t in range(NT):
                        mm = nc.tensor.matmul(work.bank(m)[:, t:t + 1], squares[:, c, t * P:(t + 1) * P], ones[:, 0:1],
                                              start=(c == 0 and t == 0), stop=(c == DC - 1), skip_group_check=True)
                mm.then_inc(work.full[m % BANKS], 1)
                work.wait_free(pe, m + 1)
                pe.wait_ge(rstd_ready, RSQRTS[stage])
                for t in range(NT):
                    mm = nc.tensor.matmul(work.bank(m + 1)[:, t * P:(t + 1) * P],
                                          rstd[:, t:t + 1].to_broadcast([P, P]), ident[:], start=True, stop=True)
                mm.then_inc(work.full[(m + 1) % BANKS], 1)

            def product(o, w, x, start, stop):
                nc.tensor.matmul(o, w(0), x(0), start=start, stop=False)
                nc.tensor.matmul(o, w(0), x(1), start=False, stop=False)
                return nc.tensor.matmul(o, w(1), x(0), start=False, stop=stop)

            def feature_out(u, g, x, k_tiles, at=0, more_u=0, more_g=0, wait_x=None, signal=True, start=True, stop=True, k0=0):
                wait_unit(pe, u, more_u)
                for k in range(k_tiles):
                    if wait_x is not None:
                        wait_x(k)
                    mm = product(stream.bank(g)[:], lambda p: split_ring[:, u % SLOTS, p, at + k * P:at + (k + 1) * P],
                                 lambda p: x(k0 + k, p), start and k == 0, stop and k == k_tiles - 1)
                return mm

            def hn_in(k, p):
                return hn[:, p, k, :]

            def y_in(k, p):
                return y[:, p, k, :]

            def token_outs(u, g, x, per_unit):
                for t in range(NT):
                    stream.wait_free(pe, g + t)
                for i in range(4):
                    wait_unit(pe, u + i)
                    for k in range(2):
                        for t in range(NT):
                            mm = product(stream.bank(g + t)[:], lambda p: x(2 * i + k, p)[:, t * P:(t + 1) * P],
                                         lambda p: split_ring[:, (u + i) % SLOTS, p, k * 512:(k + 1) * 512],
                                         i == 0 and k == 0, i == 3 and k == 1)
                            if i == 3 and k == 1:
                                mm.then_inc(stream.full[(g + t) % BANKS], 1)
                    if i < 3:
                        mm.then_inc(k_units, 1)

            def hn_wait(stage):
                return lambda k: pe.wait_ge(hn_ready, DC * hn_no[stage] + k + 1)

            def simple_outs(u, g, n, x, wait_x):
                for i in range(n):
                    stream.wait_free(pe, g + i)
                    feature_out(u + i, g + i, x, DC, wait_x=wait_x if i == 0 else None).then_inc(
                        stream.full[(g + i) % BANKS], 1)

            def even_in():
                u, g, m = base["even_in"]
                simple_outs(u, g, 16, hn_in, hn_wait("norm_mix0"))
                token_outs(u + 16, g + 16, hn_in, 2)
                pe.wait_ge(consts_ready, N_CONSTS)
                for hp in range(4):
                    work.wait_free(pe, m + hp)
                    for n in range(NT):
                        if hp == 0:
                            pe.wait_ge(v_ready, n + 1)
                        for e in range(2):
                            head = 2 * hp + e
                            o = work.bank(m + hp)[64 * e:64 * e + 64, n * P:(n + 1) * P]
                            nc.tensor.matmul(o, v_t[:, n, head * 64:head * 64 + 64], ws[:, head, :], start=True, stop=False)
                            mm = nc.tensor.matmul(o, ones[0:1, 0:64], b_row[0:1, head, :], start=False, stop=True)
                    mm.then_inc(work.full[(m + hp) % BANKS], 1)

            def ffn(stage, norm_stage):
                u, g, _ = base[stage]
                wait_hn = hn_wait(norm_stage)

                def up(i, first):
                    for j in range(4):
                        pe.wait_ge(stream.done[(g + j) % BANKS], i + (g + j) // BANKS)
                        feature_out(u + j, g + j, hn_in, DC, more_u=i * (4 // SLOTS),
                                    wait_x=wait_hn if first and j == 0 else None).then_inc(stream.full[(g + j) % BANKS], 1)

                up(0, True)
                with pe.Fori(1, 2 * FC // 4) as i:
                    up(i, False)
                u, g2 = u + 2 * FC, g + 2 * FC

                def act_wait(k):
                    pe.wait_ge(act_ready, FC * FFN_NO[stage] + k + 1)

                def down(i, first):
                    for j in range(4):
                        pe.wait_ge(stream.done[(g2 + j) % BANKS], i + (g2 + j) // BANKS)
                        for half in range(2):
                            ux = u + 2 * j + half
                            wait_unit(pe, ux, 8 // SLOTS * i)
                            for k in range(11):
                                if first and j == 0:
                                    act_wait(11 * half + k)
                                mm = product(stream.bank(g2 + j)[:], lambda p: split_ring[:, ux % SLOTS, p, k * P:(k + 1) * P],
                                             lambda p: act[:, p, 11 * half + k, :], half == 0 and k == 0, half == 1 and k == 10)
                            mm.then_inc(stream.full[(g2 + j) % BANKS] if half else down_half, 1)

                down(0, True)
                down(1, False)

            def ple(stage, norm_stage, layer):
                u, g, _ = base[stage]
                wait_hn = hn_wait(norm_stage)
                for c in range(DC):
                    stream.wait_free(pe, g + 2 * c)
                    feature_out(u + c, g + 2 * c, hn_in, DC, wait_x=wait_hn if c == 0 else None).then_inc(
                        stream.full[(g + 2 * c) % BANKS], 1)
                    stream.wait_free(pe, g + 2 * c + 1)
                    if c == 0:
                        pe.wait_ge(p_split, layer + 1)
                    for k in range(2):
                        mm = product(stream.bank(g + 2 * c + 1)[:],
                                     lambda p: split_ring[:, (u + c) % SLOTS, p, (8 + k) * P:(9 + k) * P],
                                     lambda p: p_in[:, p, k, :], k == 0, k == 1)
                    mm.then_inc(stream.full[(g + 2 * c + 1) % BANKS], 1)

            def odd_in():
                u, g, m = base["odd_in"]
                simple_outs(u, g, 9, hn_in, hn_wait("norm_mix1"))
                token_outs(u + 9, g + 9, hn_in, 2)
                token_outs(u + 13, g + 13, hn_in, 2)
                work.wait_free(pe, m)
                for t in range(NT):
                    for k in range(2 * DC):
                        mm = nc.tensor.matmul(work.bank(m)[:, 40 * t:40 * t + 40], hn[:, k % 2, k // 2, t * P:(t + 1) * P].bitcast(F32),
                                              w_small[:, k // 2, :], start=(k == 0), stop=(k == 2 * DC - 1))
                mm.then_inc(work.full[m % BANKS], 1)
                work.wait_free(pe, m + 1)
                pe.wait_ge(lat_squared, 5)
                for t in range(NT):
                    for c in range(5):
                        o = t + (NT if c >= 3 else 0)
                        mm = nc.tensor.matmul(work.bank(m + 1)[:, o:o + 1], lat_sq[:, c, t * P:(t + 1) * P], ones[:, 0:1],
                                              start=c in (0, 3), stop=c in (2, 4))
                mm.then_inc(work.full[(m + 1) % BANKS], 1)

            def mlstm():
                m = MW["sums", 0]
                work.wait_free(pe, m)
                pe.wait_ge(lf_ready, 1)
                for i in range(NT):
                    for k in range(i + 1):
                        mm = nc.tensor.matmul(work.bank(m)[:, 4 * i:4 * i + 4], (upto if k == i else ones)[:], lf[:, k, :],
                                              start=(k == 0), stop=(k == i))
                mm.then_inc(work.full[m % BANKS], 1)
                for n in range(MLSTM_BLOCKS + 1):
                    if n < MLSTM_BLOCKS:
                        head, i = divmod(n, NT)
                        m = MW["decay", n]
                        work.wait_free(pe, m)
                        pe.wait_ge(rdiag_ready, n + 1)
                        o = work.bank(m)
                        for k in range(i, -1, -1):
                            lhs = (upto if k == i else ones)[:]
                            nc.tensor.matmul(o[:, k * P:(k + 1) * P], lhs, rdiag[:, head * NT + k, :], start=(k == i), stop=(k < i),
                                             skip_group_check=True)
                            if k:
                                nc.tensor.matmul(o[:, 0:k * P], lhs, lf[:, k, head:head + 1].to_broadcast([P, k * P]),
                                                 start=False, stop=False, skip_group_check=True)
                        nc.tensor.matmul(o[:, i * P:(i + 1) * P], ident[:], neg_after[:], start=False, stop=True,
                                         skip_group_check=True).then_inc(work.full[m % BANKS], 1)
                        m = MW["scores", n]
                        work.wait_free(pe, m)
                        if n == 0:
                            for j in range(4):
                                stream.wait_done(pe, base["odd_in"][1] + 5 + j)
                        q = 64 * (head % 2)
                        nc.tensor.matmul(work.bank(m)[:, 0:(i + 1) * P], mq[q:q + 64, head // 2, i * P:(i + 1) * P],
                                         mk[q:q + 64, head // 2, 0:(i + 1) * P], start=True, stop=True).then_inc(
                            work.full[m % BANKS], 1)
                    if n:
                        n1 = n - 1
                        head, i = divmod(n1, NT)
                        m = MW["turned", n1]
                        work.wait_free(pe, m)
                        work.wait_done(pe, MW["scores", n1])
                        for j in range(i + 1):
                            mm = nc.tensor.transpose(work.bank(m)[:, j * P:(j + 1) * P], dec[:, n1 % 2, j * P:(j + 1) * P], ident[:])
                        mm.then_inc(work.full[m % BANKS], 1)
                        m = MW["out", n1]
                        work.wait_free(pe, m)
                        work.wait_done(pe, MW["turned", n1])
                        if n1 == 0:
                            for j in range(NT):
                                stream.wait_done(pe, base["odd_in"][1] + 9 + j)
                        for j in range(i + 1):
                            mm = nc.tensor.matmul(work.bank(m)[:, 0:P], sT[:, n1 % 2, j * P:(j + 1) * P],
                                                  mv[:, j, head * P:(head + 1) * P], start=(j == 0), stop=(j == i))
                        mm.then_inc(work.full[m % BANKS], 1)
                for head in range(MLSTM_HEADS):
                    m = MW["y", head]
                    work.wait_free(pe, m)
                    pe.wait_ge(hv_ready, NT)
                    for t in range(NT):
                        mm = nc.tensor.transpose(work.bank(m)[:, t * P:(t + 1) * P], hv[:, t, head * P:(head + 1) * P], ident[:])
                    mm.then_inc(work.full[m % BANKS], 1)

            def mla_up():
                u, g, _ = base["mla_up"]
                pe.wait_ge(lat_ready, 5)
                for n in range(4 * NT):
                    part, t = divmod(n, NT)
                    k0, k_tiles, w = ((0, 3, 384), (3, 2, 512))[part // 2]
                    if t == 0:
                        wait_unit(pe, u + part)
                    stream.wait_free(pe, g + n)
                    for k in range(k_tiles):
                        mm = product(stream.bank(g + n)[:, 0:w], lambda p: lat[:, p, k0 + k, t * P:(t + 1) * P],
                                     lambda p: split_ring[:, (u + part) % SLOTS, p, k * w:(k + 1) * w], k == 0, k == k_tiles - 1)
                    mm.then_inc(stream.full[(g + n) % BANKS], 1)

            def mla():
                def turn(name, src, head):
                    m = AW[name, head]
                    work.wait_free(pe, m)
                    for t in range(NT):
                        mm = nc.tensor.transpose(work.bank(m)[0:96, t * P:(t + 1) * P], src[:, t, head * 96:head * 96 + 96], ident[:])
                    mm.then_inc(work.full[m % BANKS], 1)

                pe.wait_ge(qk_ready, 1)
                turn("q", q_t, 0)
                turn("k", k_t, 0)
                for n in range(MLA_BLOCKS + 1):
                    if n < MLA_BLOCKS:
                        head, i = divmod(n, NT)
                        m = AW["scores", n]
                        work.wait_free(pe, m)
                        if i == 0:
                            work.wait_done(pe, AW["q", head])
                            work.wait_done(pe, AW["k", head])
                        nc.tensor.matmul(work.bank(m)[:, 0:(i + 1) * P], qT[0:96, head % 2, i * P:(i + 1) * P],
                                         kT[0:96, head % 2, 0:(i + 1) * P], start=True, stop=True, skip_group_check=True)
                        nc.tensor.matmul(work.bank(m)[:, i * P:(i + 1) * P], ident[:], neg_after[:], start=False, stop=True,
                                         skip_group_check=True).then_inc(work.full[m % BANKS], 1)
                    if n:
                        head, i = divmod(n - 1, NT)
                        m = AW["turned", n - 1]
                        work.wait_free(pe, m)
                        pe.wait_ge(prob_ready, n)
                        for j in range(i + 1):
                            mm = nc.tensor.transpose(work.bank(m)[:, j * P:(j + 1) * P], prob[:, (n - 1) % 2, j * P:(j + 1) * P], ident[:])
                        mm.then_inc(work.full[m % BANKS], 1)
                    if n and n % NT == 0:
                        head = n // NT - 1
                        m = AW["out", head]
                        work.wait_free(pe, m)
                        work.wait_done(pe, AW["turned", n - 1])
                        q = 64 * (head % 2)
                        pt = (probT, probT2)[head % 2]
                        for j in range(NT):
                            mm = nc.tensor.matmul(work.bank(m)[q:q + 64, j * P:T], kv_t[:, j, head * P + 64:head * P + 128],
                                                  pt[:, j, j * P:T], start=(j == 0), stop=True, skip_group_check=True)
                        mm.then_inc(work.full[m % BANKS], 1)
                    if n % NT == 1 and n // NT + 1 < MLA_HEADS:
                        turn("q", q_t, n // NT + 1)
                        turn("k", k_t, n // NT + 1)

            def odd_out():
                u, g, _ = base["odd_out"]
                for head in range(MLSTM_HEADS):
                    work.wait_done(pe, MW["y", head])
                for head in range(MLA_HEADS):
                    work.wait_done(pe, AW["out", head])
                simple_outs(u, g, 8, y_in, None)

            def gla_in():
                u, g, m = base["gla_in"]
                wait_hn = hn_wait("norm_mix2")
                work.wait_free(pe, m)
                for k in range(DC):
                    wait_hn(k)
                    for p in range(2):
                        mm = nc.tensor.matmul(work.bank(m)[0:16, :], w_low[:, k, :], hn[:, p, k, :].bitcast(F32),
                                              start=(k == 0 and p == 0), stop=(k == DC - 1 and p == 1))
                mm.then_inc(work.full[m % BANKS], 1)
                simple_outs(u, g, 2, hn_in, None)
                work.wait_done(pe, m)
                for c in range(2):
                    work.wait_free(pe, m + 1 + c)
                    nc.tensor.matmul(work.bank(m + 1 + c)[:], w_gate_up[:, c * P:(c + 1) * P], g_low, start=True,
                                     stop=True).then_inc(work.full[(m + 1 + c) % BANKS], 1)
                simple_outs(u + 2, g + 2, 2, hn_in, None)
                token_outs(u + 4, g + 4, hn_in, 2)
                token_outs(u + 8, g + 8, hn_in, 2)

            def gla():
                g = base["gla_in"][1]
                for n in range(4):
                    stream.wait_done(pe, g + n)
                for n in range(LEVELS):
                    if n:
                        pe.wait_ge(pair_ready, n)
                    for q in range(NT):
                        m, r = GW["level", n, q], 64 * (q % 2)
                        work.wait_free(pe, m)
                        for o in range(4):
                            i, c = 2 * (q // 2) + o // 2, o % 2
                            cut = (slice(r, r + 64), c, slice(i * P, (i + 1) * P))
                            lhs, rhs = (pair[cut[0], n % 2, c, cut[2]],) * 2 if n else (gk[cut], gq[cut])
                            mm = nc.tensor.matmul(work.bank(m)[:, o * P:(o + 1) * P], lhs, rhs, start=True, stop=True)
                        mm.then_inc(work.full[m % BANKS], 1)
                pe.wait_ge(far_ready, 1)
                for head in range(GLA_HEADS):
                    r, c = 64 * (head % 2), head // 2
                    k = lambda n: kd[r:r + 64, c, n * P:(n + 1) * P]
                    q = lambda n, w: qd[r:r + 64, c, n * P:(n + w) * P]
                    m = GW["far_a", head]
                    work.wait_free(pe, m)
                    for o, w, lhs, rhs in ((0, 1, k(0), q(0, 1)), (1, 2, k(3), q(2, 2)), (3, 1, k(2), q(1, 1))):
                        mm = nc.tensor.matmul(work.bank(m)[:, o * P:(o + w) * P], lhs, rhs, start=True, stop=True)
                    mm.then_inc(work.full[m % BANKS], 1)
                    m = GW["far_b", head]
                    work.wait_free(pe, m)
                    nc.tensor.matmul(work.bank(m)[:, 0:2 * P], k(1), q(2, 2), start=True, stop=True).then_inc(work.full[m % BANKS], 1)
                for n in range(4, 8):
                    stream.wait_done(pe, g + n)
                where = {(0, 1): 0, (0, 2): 1, (0, 3): 2, (2, 3): 3, (1, 2): 4, (1, 3): 5}
                pe.wait_ge(near_ready, NT)
                for head in range(GLA_HEADS):
                    work.wait_done(pe, GW["far_b", head])
                    work.wait_done(pe, GW["far_a", head])
                for i in range(NT):
                    m = GW["o", i]
                    work.wait_free(pe, m)
                    for head in range(GLA_HEADS):
                        for j in range(i + 1):
                            w = near[:, i, head * P:(head + 1) * P] if j == i else far[:, head, where[j, i] * P:(where[j, i] + 1) * P]
                            mm = nc.tensor.matmul(work.bank(m)[:, head * P:(head + 1) * P], w, gv[:, j, head * P:(head + 1) * P],
                                                  start=(j == 0), stop=(j == i))
                    mm.then_inc(work.full[m % BANKS], 1)
                pe.wait_ge(go_ready, NT)
                for head in range(GLA_HEADS):
                    m = GW["y", head]
                    work.wait_free(pe, m)
                    for t in range(NT):
                        mm = nc.tensor.transpose(work.bank(m)[:, t * P:(t + 1) * P], go[:, t, head * P:(head + 1) * P], ident[:])
                    mm.then_inc(work.full[m % BANKS], 1)

            def swa():
                u, g, _ = base["swa"]
                simple_outs(u, g, 5, hn_in, None)
                stream.wait_free(pe, g + 5)
                wait_unit(pe, u + 5)
                for t in range(NT):
                    for k in range(DC):
                        mm = product(stream.bank(g + 5)[:, t * P:(t + 1) * P], lambda p: hn[:, p, k, t * P:(t + 1) * P],
                                     lambda p: split_ring[:, (u + 5) % SLOTS, p, k * P:(k + 1) * P], k == 0, k == DC - 1)
                mm.then_inc(stream.full[(g + 5) % BANKS], 1)
                for n in range(5):
                    stream.wait_done(pe, g + n)
                for n in range(SWA_BLOCKS + 1):
                    if n < SWA_BLOCKS:
                        m, r = SW["scores", n], 64 * (n % 2)
                        work.wait_free(pe, m)
                        for s in range(2):
                            i, at = 2 * (n // 2 % 2) + s, 256 * s
                            w = 256 if i else P
                            if i == 0:
                                nc.tensor.matmul(work.bank(m)[:, 0:P], ident[:], neg_until[:, 0:1].to_broadcast([P, P]),
                                                 start=True, stop=True, skip_group_check=True)
                            nc.tensor.matmul(work.bank(m)[:, at + 256 - w:at + 256], sqT[r:r + 64, n // 4, i * P:(i + 1) * P],
                                             skT[r:r + 64, 0, (i + 1) * P - w:(i + 1) * P], start=True, stop=True, skip_group_check=True)
                            if i:
                                nc.tensor.matmul(work.bank(m)[:, at:at + P], ident[:], neg_until[:], start=False, stop=True,
                                                 skip_group_check=True)
                            mm = nc.tensor.matmul(work.bank(m)[:, at + P:at + 2 * P], ident[:], neg_after[:], start=False,
                                                  stop=True, skip_group_check=True)
                        mm.then_inc(work.full[m % BANKS], 1)
                    if n:
                        m = SW["turned", n - 1]
                        work.wait_free(pe, m)
                        pe.wait_ge(sprob_ready, n)
                        for o in range(4):
                            mm = nc.tensor.transpose(work.bank(m)[:, o * P:(o + 1) * P], sprob[:, (n - 1) % 2, o * P:(o + 1) * P],
                                                     ident[:])
                        mm.then_inc(work.full[m % BANKS], 1)
                    if n and n % NT == 0:
                        j = n // NT - 1
                        m = SW["out", j]
                        work.wait_free(pe, m)
                        work.wait_done(pe, SW["turned", n - 1])
                        if j == 0:
                            stream.wait_done(pe, g + 5)
                        for i in range(NT):
                            for e in range(2):
                                for b in range(0 if i else 1, 2):
                                    mm = nc.tensor.matmul(work.bank(m)[64 * e:64 * e + 64, i * P:(i + 1) * P],
                                                          sv[:, i - 1 + b, 64 * e:64 * e + 64],
                                                          sprobT[:, i, (2 * e + b) * P:(2 * e + b + 1) * P],
                                                          start=(b == 1 or i > 0) and (b == 0 or i == 0), stop=(b == 1))
                        mm.then_inc(work.full[m % BANKS], 1)

            def pool():
                u, g, _ = base["pool"]
                simple_outs(u, g, 4, hn_in, None)
                wait_unit(pe, u + 4)
                for c in range(4):
                    stream.wait_free(pe, g + 4 + c)
                    pe.wait_ge(pd_ready, c + 1)
                    product(stream.bank(g + 4 + c)[:], lambda p: split_ring[:, (u + 4) % SLOTS, p, c * P:(c + 1) * P],
                            lambda p: pd[:, p, c, :], True, True).then_inc(stream.full[(g + 4 + c) % BANKS], 1)

            def merge():
                u, g, _ = base["merge"]
                for n in range(3 * DC):
                    b = n % 3
                    stream.wait_free(pe, g + 2 * n)
                    feature_out(u + n, g + 2 * n, hn_in, DC).then_inc(stream.full[(g + 2 * n) % BANKS], 1)
                    stream.wait_free(pe, g + 2 * n + 1)
                    if n < 3:
                        for c in range(4):
                            if n == 2:
                                pe.wait_ge(branch_ready, c + 1)
                            else:
                                work.wait_done(pe, (SW["out", c] if n else GW["y", c]))
                    for k in range(4):
                        mm = product(stream.bank(g + 2 * n + 1)[:], lambda p: split_ring[:, (u + n) % SLOTS, p, (8 + k) * P:(9 + k) * P],
                                     lambda p: branch[b][:, p, k, :], k == 0, k == 3)
                    mm.then_inc(stream.full[(g + 2 * n + 1) % BANKS], 1)

            def block_out():
                u, g, _ = base["block_out"]
                simple_outs(u, g, 8, lambda k, p: merged[:, p, k, :], lambda k: pe.wait_ge(y_ready, DC + k + 1))

            pe.wait_ge(consts_ready, 11)
            pe.wait_ge(tables_loaded, 16 * N_TABLES)
            norm("norm_mix0")
            even_in()
            u, g, _ = base["even_out"]
            simple_outs(u, g, 8, y_in, lambda k: pe.wait_ge(y_ready, k + 1))
            if on("norm_ffn0"): norm("norm_ffn0")
            if on("ffn0"): ffn("ffn0", "norm_ffn0")
            if on("norm_ple0"): norm("norm_ple0")
            if on("ple0"): ple("ple0", "norm_ple0", 0)
            if on("norm_mix1"): norm("norm_mix1")
            if on("odd_in"): odd_in()
            if on("mlstm"): mlstm()
            if on("mla_up"): mla_up()
            if on("mla"): mla()
            if on("odd_out"): odd_out()
            if on("norm_ffn1"): norm("norm_ffn1")
            if on("ffn1"): ffn("ffn1", "norm_ffn1")
            if on("norm_ple1"): norm("norm_ple1")
            if on("ple1"): ple("ple1", "norm_ple1", 1)
            if on("norm_mix2"): norm("norm_mix2")
            if on("gla_in"): gla_in()
            if on("gla"): gla()
            if on("swa"): swa()
            if on("pool"): pool()
            if on("merge"): merge()
            if on("block_out"): block_out()
            if on("norm_post"): norm("norm_post")
            if on("norm_ffn2"): norm("norm_ffn2")
            if on("convffn"): ffn("convffn", "norm_ffn2")
            if on("norm_last"): norm("norm_last")

        @block.scalar
        def _(scalar):
            steps = Steps(scalar, act_steps)
            calls = [0]

            def rsqrt_guess(n):
                calls[0] += 1
                scalar.wait_ge(ms_ready, calls[0])
                steps.did(nc.scalar.activation(ln_ms[:, 0:n], ms[:, 0:n], ACT.Ln))
                steps.settle()
                nc.scalar.activation(rs0[:, 0:n], ln_ms[:, 0:n], ACT.Exp, scale=-0.5).then_inc(rs_guessed, 1)

            def norm(stage, src=None, ready=None):
                m = base[stage][2]
                scalar.preload_act_table_set(LNEXP)
                post = stage in ("norm_post", "norm_last")
                for c in range(DC):
                    if post:
                        n = h_out(BEFORE[stage], c)
                        stream.wait_full(scalar, n)
                        nc.scalar.activation(o_buf[:, c, :], stream.bank(n)[:], ACT.Copy).then_inc(stream.done[n % BANKS], 1)
                for c in range(DC):
                    h_ready(scalar, stage, c)
                    nc.scalar.activation(squares_of(stage)[:, c, :], (o_buf if post else h)[:, c, :],
                                         ACT.Square).then_inc(sq_ready, 1)
                if stage.startswith("norm_ple"):
                    scalar.dma_start(p_raw, a["p" + stage[-1]]).then_inc(p_loaded, 16)
                rsqrt_guess(NT)
                work.wait_full(scalar, m + 1)
                nc.scalar.activation(rstd_rows[:], work.bank(m + 1)[:], ACT.Copy).then_inc(work.done[(m + 1) % BANKS], 1)
                if not post:
                    k = DC * hn_no[stage]
                    for c in range(DC):
                        scalar.wait_ge(v_made, k + c + 1)
                        nc.scalar.activation(hn[:, 0, c, :], tmp[:, c % 4, :], ACT.Copy).then_inc(hi_made, 1)

            def even_in():
                u, g, m = base["even_in"]
                for j in range(4):
                    n = g + 3 * j
                    stream.wait_full(scalar, n)
                    if j >= 2:
                        stream.wait_done(scalar, n - 5)
                    nc.scalar.activation(tmp[:, j % 2, :], stream.bank(n)[:], ACT.Copy).then_inc(stream.done[n % BANKS], 1)
                for j in range(4):
                    n = g + 12 + j
                    stream.wait_full(scalar, n)
                    nc.scalar.activation(u_g[:, j, :], stream.bank(n)[:], ACT.Gelu_apprx_tanh).then_inc(stream.done[n % BANKS], 1)
                for t in range(NT):
                    n = g + 16 + t
                    stream.wait_full(scalar, n)
                    nc.scalar.activation(v_t[:, t, :], stream.bank(n)[:], ACT.Gelu_apprx_tanh).then_inc(stream.done[n % BANKS], 1)
                for t in range(NT):
                    stream.wait_done(scalar, g + 16 + t)
                    if t >= 2:
                        scalar.wait_ge(v_square, t - 1)
                    nc.scalar.activation(v_sq[:, t % 2, :], v_t[:, t, :], ACT.Square).then_inc(v_gelu, 1)
                scalar.preload_act_table_set(LNEXP)
                rsqrt_guess(32)

            def ffn(stage):
                g = base[stage][1]
                scalar.preload_act_table_set("silu_and_others")
                with scalar.Fori(0, 2 * FC // 4) as i:
                    for j in (0, 2):
                        scalar.wait_ge(stream.full[(g + j) % BANKS], i + (g + j) // BANKS + 1)
                        scalar.wait_ge(stream.done[(g + j + 1) % BANKS], i + (g + j + 1) // BANKS)
                        nc.scalar.activation(tmp[:, j // 2, :], stream.bank(g + j)[:], ACT.Silu).then_inc(
                            stream.done[(g + j) % BANKS], 1)

            def ple(stage):
                g = base[stage][1]
                for c in range(DC):
                    n = g + 2 * c
                    stream.wait_full(scalar, n)
                    if c >= 2:
                        stream.wait_done(scalar, n - 3)
                    nc.scalar.activation(tmp[:, c % 2, :], stream.bank(n)[:], ACT.Sigmoid).then_inc(stream.done[n % BANKS], 1)

            def odd_in():
                g, m = base["odd_in"][1:]
                for c in range(5):
                    stream.wait_full(scalar, g + c)
                    nc.scalar.activation(lat_sq[:, c, :], stream.bank(g + c)[:], ACT.Square).then_inc(lat_squared, 1)
                for c in range(2):
                    n = g + 5 + c
                    stream.wait_full(scalar, n)
                    nc.scalar.activation(mq[:, c, :], stream.bank(n)[:], ACT.Copy, scale=64 ** -0.5).then_inc(stream.done[n % BANKS], 1)
                for c in range(2):
                    n = g + 7 + c
                    stream.wait_full(scalar, n)
                    nc.scalar.activation(mk[:, c, :], stream.bank(n)[:], ACT.Copy).then_inc(stream.done[n % BANKS], 1)
                for t in range(NT):
                    n = g + 9 + t
                    stream.wait_full(scalar, n)
                    nc.scalar.activation(mv[:, t, :], stream.bank(n)[:], ACT.Copy).then_inc(stream.done[n % BANKS], 1)
                for t in range(NT):
                    n = g + 13 + t
                    stream.wait_full(scalar, n)
                    nc.scalar.activation(mo[:, t, :], stream.bank(n)[:], ACT.Sigmoid).then_inc(stream.done[n % BANKS], 1)

            def mlstm():
                scalar.preload_act_table_set(LNEXP)
                scalar.wait_ge(gates_ready, 1)
                steps.did(nc.scalar.activation(gl[:, 0, :], gl[:, 3, :], ACT.Abs))
                steps.settle()
                steps.did(nc.scalar.activation(gl[:, 1, :], gl[:, 0, :], ACT.Exp, scale=-1.0))
                steps.settle()
                nc.scalar.activation(gl[:, 2, :], gl[:, 1, :], ACT.Ln, bias=1.0).then_inc(log_ready, 1)
                for n in range(MLSTM_BLOCKS + 1):
                    if n < MLSTM_BLOCKS:
                        head, i = divmod(n, NT)
                        m = MW["decay", n]
                        scalar.wait_ge(m_ready, n + 1)
                        nc.scalar.activation(exp_m[:, n:n + 1], neg_m[:, n:n + 1], ACT.Exp).then_inc(exp_m_ready, 1)
                        nc.scalar.activation(dec[:, n % 2, 0:(i + 1) * P], work.bank(m)[:, 0:(i + 1) * P], ACT.Exp,
                                             bias=neg_m[:, n:n + 1]).then_inc(work.done[m % BANKS], 1)
                    if n:
                        head, i = divmod(n - 1, NT)
                        m = MW["turned", n - 1]
                        work.wait_full(scalar, m)
                        nc.scalar.activation(sT[:, (n - 1) % 2, 0:(i + 1) * P], work.bank(m)[:, 0:(i + 1) * P],
                                             ACT.Copy).then_inc(work.done[m % BANKS], 1)
                        m = MW["out", n - 1]
                        work.wait_full(scalar, m)
                        scalar.wait_ge(rden_ready, n)
                        nc.scalar.activation(hv[:, i, head * P:(head + 1) * P], work.bank(m)[:, 0:P], ACT.Copy,
                                             scale=rden[:, n - 1:n]).then_inc(work.done[m % BANKS], 1)
                work.wait_done(scalar, MW["out", MLSTM_BLOCKS - 1])
                for t in range(NT):
                    nc.scalar.activation(hv_sq[:, t, :], hv[:, t, :], ACT.Square).then_inc(hv_squared, 1)
                rsqrt_guess(16)

            def mla_up():
                g = base["mla_up"][1]
                rsqrt_guess(8)
                scalar.wait_ge(lat_rs_ready, 1)
                for n in range(16):
                    half, t = divmod(n % 8, 4)
                    kv = n // 8
                    w = (384, 512)[kv]
                    stream.wait_full(scalar, g + n)
                    nc.scalar.activation((q_t, kv_t)[kv][:, t, half * w:half * w + w], stream.bank(g + n)[:, 0:w], ACT.Copy,
                                         scale=lat_rs[:, NT * kv + t:NT * kv + t + 1]).then_inc(stream.done[(g + n) % BANKS], 1)
                for n in range(8):
                    t, kv = n % 4, n // 4
                    stream.wait_done(scalar, g + 8 * kv + 4 + t)
                    stream.wait_done(scalar, g + 8 * kv + t)
                    if n >= 2:
                        scalar.wait_ge(summed, n - 1)
                    w = (768, 1024)[kv]
                    nc.scalar.activation(qk_sq[:, n % 2, 0:w], (q_t, kv_t)[kv][:, t, :], ACT.Square).then_inc(squared, 1)
                    if n == 3:
                        rsqrt_guess(64)
                rsqrt_guess(36)

            def mla():
                for n in range(MLA_BLOCKS + 1):
                    if n < MLA_BLOCKS:
                        head, i = divmod(n, NT)
                        m = AW["scores", n]
                        scalar.wait_ge(m_ready, MLSTM_BLOCKS + n + 1)
                        if n >= 2:
                            work.wait_full(scalar, AW["turned", n - 2])
                        nc.scalar.activation(prob[:, n % 2, 0:(i + 1) * P], work.bank(m)[:, 0:(i + 1) * P], ACT.Exp,
                                             bias=neg_m[:, n:n + 1], accum_out=den[:, n:n + 1]).then_inc(work.done[m % BANKS], 1)
                    if n:
                        head, i = divmod(n - 1, NT)
                        m = AW["turned", n - 1]
                        work.wait_full(scalar, m)
                        if i == 0 and head >= 2:
                            work.wait_full(scalar, AW["out", head - 2])
                        nc.scalar.activation((probT, probT2)[head % 2][:, 0:i + 1, i * P:(i + 1) * P],
                                             work.bank(m)[:, 0:(i + 1) * P].rearrange("p (a b) -> p a b", b=P),
                                             ACT.Copy).then_inc(work.done[m % BANKS], 1)

            def gla_in():
                g, m = base["gla_in"][1:]

                def copy(dst, n, scale=1.0, func=ACT.Copy):
                    stream.wait_full(scalar, n)
                    nc.scalar.activation(dst, stream.bank(n)[:], func, scale=scale).then_inc(stream.done[n % BANKS], 1)

                work.wait_full(scalar, m)
                nc.scalar.activation(g_low, work.bank(m)[0:16, :], ACT.Copy).then_inc(work.done[m % BANKS], 1)
                for c in range(2):
                    copy(gq[:, c, :], g + c, 64 ** -0.5)
                for c in range(2):
                    work.wait_full(scalar, m + 1 + c)
                    nc.scalar.activation(logit[:, c, :], work.bank(m + 1 + c)[:], ACT.Identity, bias=col("gla_b", c)).then_inc(
                        work.done[(m + 1 + c) % BANKS], 1)
                for c in range(2):
                    work.wait_done(scalar, m + 1 + c)
                steps.did(nc.scalar.activation(log_p, logit, ACT.Abs))
                steps.settle()
                steps.did(nc.scalar.activation(log_p, log_p, ACT.Exp, scale=-1.0))
                steps.settle()
                nc.scalar.activation(log_p, log_p, ACT.Ln, bias=1.0).then_inc(logit_logged, 1)
                for c in range(2):
                    copy(gk[:, c, :], g + 2 + c)
                decays(1)
                for t in range(NT):
                    copy(gv[:, t, :], g + 4 + t)
                decays(2)
                scalar.preload_act_table_set("silu_and_others")
                for t in range(NT):
                    copy(gr[:, t, :], g + 8 + t, func=ACT.Silu)

            def decays(n):
                scalar.wait_ge(exponent_ready, n)
                nc.scalar.activation(pair[:, n % 2], pair[:, n % 2], ACT.Exp, scale=1.0 / 16).then_inc(decay_ready, 1)

            def gla():
                scalar.preload_act_table_set(LNEXP)
                for n in range(3, LEVELS):
                    decays(n)
                scalar.wait_ge(exponent_ready, LEVELS)
                for c in range(2):
                    for i in range(NT - 1):
                        nc.scalar.activation(kd[:, c, i * P:(i + 1) * P], cum[:, c, i * P:(i + 1) * P], ACT.Exp, scale=-1.0 / 16,
                                             bias=tot16[:, c, i:i + 1])
                    for slot, i in enumerate((1, 3, 2)):
                        nc.scalar.activation(qd[:, c, slot * P:(slot + 1) * P], cum[:, c, i * P:(i + 1) * P], ACT.Exp, scale=1.0 / 16)
                nc.scalar.activation(exp_tot[:], tot16[:], ACT.Exp).then_inc(far_exp, 1)
                for head in range(GLA_HEADS):
                    for part, lo, w in (("far_a", 0, 512), ("far_b", 512, 256)):
                        m = GW[part, head]
                        work.wait_full(scalar, m)
                        nc.scalar.activation(far[:, head, lo:lo + w], work.bank(m)[:, 0:w], ACT.Copy).then_inc(work.done[m % BANKS], 1)
                for i in range(NT):
                    m = GW["o", i]
                    work.wait_full(scalar, m)
                    nc.scalar.activation(go[:, i, :], work.bank(m)[:], ACT.Copy).then_inc(work.done[m % BANKS], 1)
                for i in range(NT):
                    work.wait_done(scalar, GW["o", i])
                    nc.scalar.activation(go_sq[:, i, :], go[:, i, :], ACT.Square).then_inc(go_squared, 1)
                rsqrt_guess(16)

            def swa():
                g = base["swa"][1]
                for c in range(6):
                    dst = (sqT[:, c, :] if c < 4 else skT[:, 0, :] if c == 4 else sv.rearrange("p a b -> p (a b)"))
                    stream.wait_full(scalar, g + c)
                    nc.scalar.activation(dst, stream.bank(g + c)[:], ACT.Copy, scale=64 ** -0.5 if c < 4 else 1.0).then_inc(
                        stream.done[(g + c) % BANKS], 1)
                for n in range(SWA_BLOCKS + 1):
                    if n < SWA_BLOCKS:
                        m = SW["scores", n]
                        scalar.wait_ge(m_ready, MLSTM_BLOCKS + MLA_BLOCKS + n + 1)
                        scalar.wait_ge(sink_ready, n + 2)
                        if n >= 2:
                            work.wait_full(scalar, SW["turned", n - 2])
                        nc.scalar.activation(sink_m[:, 2 * n:2 * n + 2], sink_m[:, 2 * n:2 * n + 2], ACT.Exp)
                        for s in range(2):
                            x = nc.scalar.activation(sprob[:, n % 2, 256 * s:256 * s + 256], work.bank(m)[:, 256 * s:256 * s + 256],
                                                     ACT.Exp, bias=neg_m[:, 2 * n + s:2 * n + s + 1],
                                                     accum_out=den[:, 2 * n + s:2 * n + s + 1])
                        x.then_inc(work.done[m % BANKS], 1)
                    if n:
                        j, b = divmod(n - 1, 4)
                        m = SW["turned", n - 1]
                        work.wait_full(scalar, m)
                        if j and b == 0:
                            work.wait_full(scalar, SW["out", j - 1])
                        i, e = 2 * (b // 2), b % 2
                        nc.scalar.activation(sprobT[:, i:i + 2, 256 * e:256 * e + 256],
                                             work.bank(m)[:].rearrange("p (a b) -> p a b", a=2), ACT.Copy).then_inc(work.done[m % BANKS], 1)

            def pool():
                g = base["pool"][1]
                scalar.wait_ge(pad_ready, 1)
                for c in range(4):
                    stream.wait_full(scalar, g + c)
                    nc.scalar.activation(pu[:, c, 16:16 + T], stream.bank(g + c)[:], ACT.Copy).then_inc(stream.done[(g + c) % BANKS], 1)

            def merge():
                g = base["merge"][1]
                for n in range(3 * DC):
                    o = g + 2 * n
                    stream.wait_full(scalar, o)
                    if n == 0:
                        scalar.wait_ge(branch_ready, 4)
                    if n >= 2:
                        stream.wait_done(scalar, o - 3)
                    nc.scalar.activation(tmp[:, n % 2, :], stream.bank(o)[:], ACT.Sigmoid).then_inc(stream.done[o % BANKS], 1)

            def convffn():
                g = base["convffn"][1]
                scalar.preload_act_table_set("gelu_apprx_tanh_and_others")

                def body(i, first):
                    for j in range(4):
                        b, gate = j // 2, j % 2 == 0
                        c = 2 * i + b + (0 if gate else FC)
                        scalar.wait_ge(stream.full[(g + j) % BANKS], i + (g + j) // BANKS + 1)
                        if not first:
                            scalar.wait_ge(act_ready, FC * FFN_NO["convffn"] + 2 * (i - 1) + b + 1)
                        nc.scalar.activation(tmp[:, j, :].unsqueeze(1), stream.bank(g + j)[:].unsqueeze(1), ACT.Identity,
                                             scale=cols[:, bass.ds(c + COLS["cw2"], 1)],
                                             bias=cols[:, bass.ds(c + COLS["cb"], 1)]).then_inc(conv_started, 1)
                        if not gate:
                            scalar.wait_ge(stream.done[(g + j - 1) % BANKS], i + (g + j - 1) // BANKS + 1)
                            nc.scalar.activation(tmp[:, j - 1, :], tmp[:, j - 1, :], ACT.Gelu_apprx_tanh).then_inc(gelu_ready, 1)

                body(0, True)
                with scalar.Fori(1, 2 * FC // 4) as i:
                    body(i, False)

            scalar.dma_start(w_small[:], a["w_small"]).then_inc(tables_loaded, 16)
            scalar.dma_start(w_low[:], a["w_low"]).then_inc(tables_loaded, 16)
            scalar.dma_start(w_gate_up[:], a["w_gate_up"]).then_inc(tables_loaded, 16)
            scalar.dma_start(pos_i[:], a["positions"]).then_inc(tables_loaded, 16)
            scalar.dma_start(cols[:], a["cols"]).then_inc(tables_loaded, 16)
            scalar.dma_start(rows[:], a["rows"].partition_broadcast(P)).then_inc(tables_loaded, 16)
            scalar.dma_start(ws, a["w_s"]).then_inc(tables_loaded, 16)
            scalar.dma_start(b_row, a["b_s"]).then_inc(tables_loaded, 16)
            scalar.preload_act_table_set("silu_and_others")
            scalar.wait_ge(angle_ready, 1)
            nc.scalar.activation(cos_sin[:], angle[:, 3:5, :], ACT.Sin).then_inc(turned_ready, 1)
            norm("norm_mix0")
            even_in()
            if on("norm_ffn0"): norm("norm_ffn0")
            if on("ffn0"): ffn("ffn0")
            if on("norm_ple0"): norm("norm_ple0")
            if on("ple0"): ple("ple0")
            if on("norm_mix1"): norm("norm_mix1")
            if on("odd_in"): odd_in()
            if on("mlstm"): mlstm()
            if on("mla_up"): mla_up()
            if on("mla"): mla()
            if on("norm_ffn1"): norm("norm_ffn1")
            if on("ffn1"): ffn("ffn1")
            if on("norm_ple1"): norm("norm_ple1")
            if on("ple1"): ple("ple1")
            if on("norm_mix2"): norm("norm_mix2")
            if on("gla_in"): gla_in()
            if on("gla"): gla()
            if on("swa"): swa()
            if on("pool"): pool()
            if on("merge"): merge()
            if on("norm_post"): norm("norm_post")
            if on("norm_ffn2"): norm("norm_ffn2")
            if on("convffn"): convffn()
            if on("norm_last"): norm("norm_last")

        @block.vector
        def _(dve):
            steps = Steps(dve, dve_steps)
            calls = [0]

            def rsqrt(n):
                calls[0] += 1
                dve.wait_ge(rs_guessed, calls[0])
                steps.did(nc.vector.tensor_tensor(rt[:, 0, 0:n], rs0[:, 0:n], rs0[:, 0:n], ALU.mult))
                steps.settle()
                steps.did(nc.vector.scalar_tensor_tensor(rt[:, 1, 0:n], rt[:, 0, 0:n], -0.5, ms[:, 0:n], ALU.mult, ALU.mult))
                steps.settle()
                nc.vector.scalar_tensor_tensor(rstd[:, 0:n], rt[:, 1, 0:n], 1.5, rs0[:, 0:n], ALU.add, ALU.mult).then_inc(rstd_ready, 1)

            def keep_halves(to, v):
                steps.did(nc.vector.tensor_copy(to[0], v))
                steps.settle()
                return nc.vector.tensor_tensor(to[1], v, to[0].bitcast(F32), ALU.subtract)

            def norm(stage, gain):
                m, k = base[stage][2], norm_no[stage]
                work.wait_full(dve, m)
                nc.vector.tensor_copy(stat[:, 0:NT], work.bank(m)[:, 0:NT]).then_inc(work.done[m % BANKS], 1)
                work.wait_done(dve, m)
                nc.vector.tensor_scalar(ms[:, 0:NT], stat[:, 0:NT], 1.0 / D, EPS, ALU.mult, ALU.add).then_inc(ms_ready, 1)
                rsqrt(NT)
                work.wait_done(dve, m + 1)
                if k == 0:
                    dve.wait_ge(tables_loaded, 16 * N_TABLES)
                if stage in ("norm_post", "norm_last"):
                    for c in range(DC):
                        steps.did(nc.vector.scalar_tensor_tensor(tmp[:, c % 4, :], o_buf[:, c, :], col(gain, c), rstd_rows[:],
                                                                 ALU.mult, ALU.mult))
                        steps.settle()
                        nc.vector.tensor_tensor(h[:, c, :], h[:, c, :], tmp[:, c % 4, :], ALU.add).then_inc(h_updated, 1)
                    dve.wait_ge(h_updated, DC * (1 if stage == "norm_post" else 2))
                    return
                k = DC * hn_no[stage]
                for c in range(DC + 1):
                    if c < DC:
                        if c >= 4:
                            dve.wait_ge(hn_ready, k + c - 3)
                        nc.vector.scalar_tensor_tensor(tmp[:, c % 4, :], h[:, c, :], col(gain, c), rstd_rows[:], ALU.mult,
                                                       ALU.mult).then_inc(v_made, 1)
                    if c:
                        dve.wait_ge(hi_made, k + c)
                        nc.vector.tensor_tensor(hn[:, 1, c - 1, :], tmp[:, (c - 1) % 4, :], hn[:, 0, c - 1, :].bitcast(F32),
                                                ALU.subtract).then_inc(hn_ready, 1)
                dve.wait_ge(hn_ready, k + DC)

            def even_in():
                u, g, m = base["even_in"]
                for e in range(2):
                    steps.did(nc.vector.memset(z_pad[:, e, 0:2], 0.0))
                for j in range(4):
                    n, z, cv = g + 3 * j, z_pad[:, j % 2, :], conv[:, j % 2, :]
                    stream.wait_full(dve, n + 1)
                    stream.wait_done(dve, n)
                    if j >= 2:
                        stream.wait_done(dve, n - 4)
                    steps.settle()
                    nc.vector.tensor_tensor(z[:, 2:2 + T], stream.bank(n + 1)[:], tmp[:, j % 2, :], ALU.mult).then_inc(
                        stream.done[(n + 1) % BANKS], 1)
                    stream.wait_done(dve, n + 1)
                    steps.settle()
                    steps.did(nc.vector.tensor_scalar(cv, z[:, 2:2 + T], col("w_conv", 8 + j), None, ALU.mult))
                    for w in (1, 0):
                        steps.settle()
                        steps.did(nc.vector.scalar_tensor_tensor(cv, z[:, w:w + T], col("w_conv", 4 * w + j), cv, ALU.mult, ALU.add))
                    stream.wait_full(dve, n + 2)
                    steps.settle()
                    v = tmp[:, 2 + j % 2, :]
                    nc.vector.tensor_tensor(v, stream.bank(n + 2)[:], cv, ALU.mult).then_inc(stream.done[(n + 2) % BANKS], 1)
                    stream.wait_done(dve, n + 2)
                    keep_halves((y[:, 0, j, :], y[:, 1, j, :]), v).then_inc(y_ready, 1)
                    dve.wait_ge(y_ready, j + 1)
                for t in range(NT):
                    dve.wait_ge(v_gelu, t + 1)
                    nc.vector.tensor_reduce(stat[:, 16 + 8 * t:24 + 8 * t], v_sq[:, t % 2, :].rearrange("p (a b) -> p a b", a=8),
                                            AX_X, ALU.add).then_inc(v_square, 1)
                dve.wait_ge(v_square, NT)
                nc.vector.tensor_scalar(ms[:, 0:32], stat[:, 16:48], 1.0 / 64, EPS, ALU.mult, ALU.add).then_inc(ms_ready, 1)
                rsqrt(32)
                dve.wait_ge(rstd_ready, calls[0])
                for t in range(NT):
                    vt = v_t[:, t, :].rearrange("p (a b) -> p a b", a=8)
                    steps.did(nc.vector.tensor_tensor(vt, vt, rstd[:, 8 * t:8 * t + 8].unsqueeze(2).to_broadcast([P, 8, 64]), ALU.mult))
                    steps.settle()
                    nc.vector.tensor_tensor(v_t[:, t, :], v_t[:, t, :], row("g_v", 0, 512), ALU.mult).then_inc(v_ready, 1)
                for hp in range(4):
                    work.wait_full(dve, m + hp)
                    stream.wait_done(dve, g + 12 + hp)
                    v = tmp[:, 2 + hp % 2, :]
                    nc.vector.tensor_tensor(v, work.bank(m + hp)[:], u_g[:, hp, :], ALU.mult).then_inc(work.done[(m + hp) % BANKS], 1)
                    work.wait_done(dve, m + hp)
                    keep_halves((y[:, 0, 4 + hp, :], y[:, 1, 4 + hp, :]), v).then_inc(y_ready, 1)
                    dve.wait_ge(y_ready, 5 + hp)

            def add_outs(g, n):
                for c in range(n):
                    stream.wait_full(dve, g + c)
                    nc.vector.tensor_tensor(h[:, c, :], stream.bank(g + c)[:], h[:, c, :], ALU.add).then_inc(
                        stream.done[(g + c) % BANKS], 1)

            def ffn(stage):
                g = base[stage][1]
                with dve.Fori(0, 2 * FC // 4) as i:
                    for j in (1, 3):
                        dve.wait_ge(stream.full[(g + j) % BANKS], i + (g + j) // BANKS + 1)
                        dve.wait_ge(stream.done[(g + j - 1) % BANKS], i + (g + j - 1) // BANKS + 1)
                        v = tmp[:, 2 + j // 2, :]
                        nc.vector.tensor_tensor(v, stream.bank(g + j)[:], tmp[:, j // 2, :], ALU.mult).then_inc(
                            stream.done[(g + j) % BANKS], 1)
                        dve.wait_ge(stream.done[(g + j) % BANKS], i + (g + j) // BANKS + 1)
                        act_halves(stage, v, i, j // 2)
                steps.n += FC
                add_outs(g + 2 * FC, DC)

            def act_halves(stage, v, i, b):
                hi, lo = (act[:, p, bass.ds(2 * i + b, 1), :] for p in range(2))
                nc.vector.tensor_copy(hi, v.unsqueeze(1)).then_inc(dve_steps, 1)
                dve.wait_ge(dve_steps, steps.n + 2 * i + b + 1)
                nc.vector.tensor_tensor(lo, v.unsqueeze(1), hi.bitcast(F32), ALU.subtract).then_inc(act_ready, 1)
                dve.wait_ge(act_ready, FC * FFN_NO[stage] + 2 * i + b + 1)

            def ple(stage):
                g = base[stage][1]
                dve.wait_ge(p_loaded, 16 * (1 + int(stage[-1])))
                keep_halves((p_in[:, 0], p_in[:, 1]), p_raw).then_inc(p_split, 1)
                for c in range(DC):
                    n = g + 2 * c + 1
                    stream.wait_full(dve, n)
                    stream.wait_done(dve, n - 1)
                    if c >= 2:
                        stream.wait_done(dve, n - 4)
                    steps.did(nc.vector.tensor_tensor(tmp[:, 2 + c % 2, :], stream.bank(n)[:], tmp[:, c % 2, :], ALU.mult))
                    steps.settle()
                    nc.vector.tensor_tensor(h[:, c, :], tmp[:, 2 + c % 2, :], h[:, c, :], ALU.add).then_inc(
                        stream.done[n % BANKS], 1)

            def rope_angles():
                dve.wait_ge(tables_loaded, 16 * N_TABLES)
                dve.wait_ge(freq_ready, 1)
                ang, turns, off = angle[:, 0, :], angle[:, 1, :], angle[:, 2, :]
                a3 = ang.rearrange("p (a b) -> p a b", a=NT)
                steps.did(nc.vector.tensor_copy(stat[:, 60:64], pos_i[:]))
                steps.settle()
                steps.did(nc.vector.tensor_copy(a3, inv_freq[:].unsqueeze(1).to_broadcast([P, NT, 16])))
                steps.settle()
                steps.did(nc.vector.tensor_tensor(a3, a3, stat[:, 60:64].unsqueeze(2).to_broadcast([P, NT, 16]), ALU.mult))
                for j, (quarter, shift) in enumerate(((0.25, PI / 2), (0.0, 0.0))):
                    r = angle[:, 3 + j, :]
                    steps.settle()
                    steps.did(nc.vector.tensor_scalar(off, ang, 1.0 / TWO_PI, quarter, ALU.mult, ALU.add))
                    steps.settle()
                    steps.did(nc.vector.tensor_scalar(turns, off, ROUND, ROUND, ALU.add, ALU.subtract))
                    steps.settle()
                    steps.did(nc.vector.tensor_copy(r, ang))
                    for part in TURN_PARTS:
                        steps.settle()
                        steps.did(nc.vector.scalar_tensor_tensor(r, turns, -part, r, ALU.mult, ALU.add))
                    steps.settle()
                    steps.did(nc.vector.tensor_scalar(r, r, shift, 3.1415925, ALU.add, ALU.min))
                    steps.settle()
                    if j == 0:
                        steps.did(nc.vector.tensor_scalar(r, r, -3.1415925, None, ALU.max))
                    else:
                        nc.vector.tensor_scalar(r, r, -3.1415925, None, ALU.max).then_inc(angle_ready, 1)

            def odd_in():
                g, m = base["odd_in"][1:]
                for c in range(5):
                    stream.wait_full(dve, g + c)
                    dve.wait_ge(lat_squared, c + 1)
                    nc.vector.tensor_scalar(tmp[:, c % 4, :], stream.bank(g + c)[:], col("g_qa", c), None, ALU.mult).then_inc(
                        stream.done[(g + c) % BANKS], 1)
                    stream.wait_done(dve, g + c)
                    keep_halves((lat[:, 0, c, :], lat[:, 1, c, :]), tmp[:, c % 4, :]).then_inc(lat_ready, 1)
                    dve.wait_ge(lat_ready, c + 1)
                for t in range(NT):
                    stream.wait_done(dve, g + 13 + t)
                    steps.did(nc.vector.tensor_tensor(mo[:, t, :], mo[:, t, :], row("g_mh", 0, 512), ALU.mult))
                work.wait_full(dve, m)
                small = work.bank(m)[:, 0:160].rearrange("p (a b) -> p a b", a=NT)
                steps.did(nc.vector.tensor_copy(k_pe[:], small[:, :, 0:32]))
                nc.vector.tensor_tensor(gates[:], small[:, :, 32:40], row("b_gate", 0, 8).unsqueeze(1).to_broadcast([P, NT, 8]),
                                        ALU.add).then_inc(work.done[m % BANKS], 1)
                work.wait_full(dve, m + 1)
                nc.vector.tensor_copy(lat_ss[:], work.bank(m + 1)[:, 0:8]).then_inc(work.done[(m + 1) % BANKS], 1)

            def mlstm():
                work.wait_done(dve, base["odd_in"][2])
                f = gl[:, 3, :].rearrange("p (a b) -> p a b", a=NT)
                nc.vector.tensor_copy(f, gates[:, :, 4:8]).then_inc(gates_ready, 1)
                dve.wait_ge(log_ready, 1)
                nc.vector.scalar_tensor_tensor(lf[:], f, 0.0, gl[:, 2, :].rearrange("p (a b) -> p a b", a=NT), ALU.min,
                                               ALU.subtract).then_inc(lf_ready, 1)
                dve.wait_ge(lf_ready, 1)
                work.wait_full(dve, base["odd_in"][2] + 1)
                for n in range(MLSTM_BLOCKS):
                    head, k = divmod(n, NT)
                    steps.did(nc.vector.tensor_scalar(rdiag[:, n, :], ident[:], gates[:, k, head:head + 1], None, ALU.mult))
                    steps.settle()
                    nc.vector.scalar_tensor_tensor(rdiag[:, n, :], below[:], lf[:, k, head:head + 1], rdiag[:, n, :], ALU.mult,
                                                   ALU.add).then_inc(rdiag_ready, 1)
                m = MW["sums", 0]
                work.wait_full(dve, m)
                nc.vector.tensor_scalar(neg_sum[:], work.bank(m)[:, 0:16], -1.0, None, ALU.mult).then_inc(work.done[m % BANKS], 1)
                work.wait_done(dve, m)
                for n in range(MLSTM_BLOCKS):
                    head, i = divmod(n, NT)
                    m = MW["decay", n]
                    work.wait_full(dve, m)
                    steps.did(nc.vector.tensor_reduce(neg_m[:, n:n + 1], work.bank(m)[:, 0:(i + 1) * P], AX_X, ALU.max, negate=True))
                    steps.settle()
                    nc.vector.tensor_tensor(neg_m[:, n:n + 1], neg_m[:, n:n + 1], neg_sum[:, 4 * i + head:4 * i + head + 1],
                                            ALU.min).then_inc(m_ready, 1)
                    work.wait_done(dve, m)
                    m = MW["scores", n]
                    work.wait_full(dve, m)
                    w = dec[:, n % 2, 0:(i + 1) * P]
                    nc.vector.scalar_tensor_tensor(w, work.bank(m)[:, 0:(i + 1) * P], 1.0, w, ALU.mult, ALU.mult,
                                                   accum_out=den[:, n:n + 1]).then_inc(work.done[m % BANKS], 1)
                    work.wait_done(dve, m)
                    dve.wait_ge(exp_m_ready, n + 1)
                    steps.did(nc.vector.scalar_tensor_tensor(den[:, n:n + 1], den[:, n:n + 1], -1.0, den[:, n:n + 1], ALU.mult, ALU.max))
                    steps.settle()
                    steps.did(nc.vector.tensor_tensor(den[:, n:n + 1], den[:, n:n + 1], exp_m[:, n:n + 1], ALU.max))
                    steps.settle()
                    nc.vector.reciprocal(rden[:, n:n + 1], den[:, n:n + 1]).then_inc(rden_ready, 1)
                for t in range(NT):
                    dve.wait_ge(hv_squared, t + 1)
                    steps.did(nc.vector.tensor_reduce(stat[:, 4 * t:4 * t + 4], hv_sq[:, t, :].rearrange("p (a b) -> p a b", a=4),
                                                      AX_X, ALU.add))
                steps.settle()
                nc.vector.tensor_scalar(ms[:, 0:16], stat[:, 0:16], 1.0 / P, EPS, ALU.mult, ALU.add).then_inc(ms_ready, 1)
                rsqrt(16)
                dve.wait_ge(rstd_ready, calls[0])
                for t in range(NT):
                    v = hv[:, t, :].rearrange("p (a b) -> p a b", a=4)
                    steps.did(nc.vector.tensor_tensor(v, v, rstd[:, 4 * t:4 * t + 4].unsqueeze(2).to_broadcast([P, 4, P]), ALU.mult))
                    steps.settle()
                    nc.vector.tensor_tensor(hv[:, t, :], hv[:, t, :], mo[:, t, :], ALU.mult).then_inc(hv_ready, 1)
                for head in range(MLSTM_HEADS):
                    bank_halves(y[:, :, 4 + head, :], MW["y", head], slice(0, P))

            def bank_halves(to, m, at):
                work.wait_full(dve, m)
                steps.did(nc.vector.tensor_copy(to[at, 0], work.bank(m)[at, :]))
                steps.settle()
                nc.vector.tensor_tensor(to[at, 1], work.bank(m)[at, :], to[at, 0].bitcast(F32), ALU.subtract).then_inc(
                    work.done[m % BANKS], 1)

            def mla_up():
                work.wait_done(dve, base["odd_in"][2] + 1)
                steps.did(nc.vector.tensor_scalar(ms[:, 0:4], lat_ss[:, 0:4], 1.0 / 384, EPS, ALU.mult, ALU.add))
                nc.vector.tensor_scalar(ms[:, 4:8], lat_ss[:, 4:8], 1.0 / 256, EPS, ALU.mult, ALU.add).then_inc(ms_ready, 1)
                rsqrt(8)
                dve.wait_ge(rstd_ready, calls[0])
                nc.vector.tensor_copy(lat_rs[:], rstd[:, 0:8]).then_inc(lat_rs_ready, 1)
                steps.did(nc.vector.tensor_scalar(row("g_q", 0, 96), row("g_q", 0, 96), 96 ** -0.5, None, ALU.mult))
                st = stat[:].rearrange("p (a b) -> p a b", a=NT)
                for t in range(NT):
                    dve.wait_ge(squared, t + 1)
                    s3 = qk_sq[:, t % 2, 0:768].rearrange("p (a b) -> p a b", a=8)
                    steps.did(nc.vector.tensor_reduce(st[:, t, 0:8], s3[:, :, 0:64], AX_X, ALU.add))
                    nc.vector.tensor_reduce(st[:, t, 8:16], s3[:, :, 64:96], AX_X, ALU.add).then_inc(summed, 1)
                dve.wait_ge(summed, NT)
                m3 = ms[:].rearrange("p (a b) -> p a b", a=NT)
                steps.did(nc.vector.tensor_scalar(m3[:, :, 0:8], st[:, :, 0:8], 1.0 / 64, EPS, ALU.mult, ALU.add))
                nc.vector.tensor_scalar(m3[:, :, 8:16], st[:, :, 8:16], 1.0 / 32, EPS, ALU.mult, ALU.add).then_inc(ms_ready, 1)
                rsqrt(64)
                dve.wait_ge(rstd_ready, calls[0])
                r3 = rstd[:].rearrange("p (a b) -> p a b", a=NT)
                for t in range(NT):
                    q3 = q_t[:, t, :].rearrange("p (a b) -> p a b", a=8)
                    steps.did(nc.vector.tensor_tensor(q3[:, :, 0:64], q3[:, :, 0:64],
                                                      r3[:, t, 0:8].unsqueeze(2).to_broadcast([P, 8, 64]), ALU.mult))
                    steps.did(nc.vector.tensor_tensor(q3[:, :, 64:96], q3[:, :, 64:96],
                                                      r3[:, t, 8:16].unsqueeze(2).to_broadcast([P, 8, 32]), ALU.mult))
                    steps.settle()
                    steps.did(nc.vector.tensor_tensor(q3, q3, row("g_q", 0, 96).unsqueeze(1).to_broadcast([P, 8, 96]), ALU.mult))
                for t in range(NT):
                    dve.wait_ge(squared, NT + t + 1)
                    s3 = qk_sq[:, t % 2, :].rearrange("p (a b) -> p a b", a=8)
                    nc.vector.tensor_reduce(stat[:, 8 * t:8 * t + 8], s3[:, :, 0:64], AX_X, ALU.add).then_inc(summed, 1)
                steps.did(nc.vector.tensor_tensor(angle[:, 0:2, :].rearrange("p a (b c) -> p (a b) c", c=32), k_pe[:], k_pe[:], ALU.mult))
                steps.settle()
                steps.did(nc.vector.tensor_reduce(stat[:, 32:36], angle[:, 0:2, :].rearrange("p a (b c) -> p (a b) c", c=32), AX_X, ALU.add))
                steps.settle()
                steps.did(nc.vector.tensor_scalar(ms[:, 0:32], stat[:, 0:32], 1.0 / 64, EPS, ALU.mult, ALU.add))
                nc.vector.tensor_scalar(ms[:, 32:36], stat[:, 32:36], 1.0 / 32, EPS, ALU.mult, ALU.add).then_inc(ms_ready, 1)
                rsqrt(36)
                dve.wait_ge(rstd_ready, calls[0])
                k4 = k_t.rearrange("p t (a b) -> p t a b", a=8)
                for t in range(NT):
                    k3, kv3 = k4[:, t], kv_t[:, t, :].rearrange("p (a b) -> p a b", a=8)
                    steps.did(nc.vector.tensor_tensor(k3[:, :, 0:64], kv3[:, :, 0:64],
                                                      rstd[:, 8 * t:8 * t + 8].unsqueeze(2).to_broadcast([P, 8, 64]), ALU.mult))
                    steps.settle()
                    steps.did(nc.vector.tensor_tensor(k3[:, :, 0:64], k3[:, :, 0:64],
                                                      row("g_k", 0, 64).unsqueeze(1).to_broadcast([P, 8, 64]), ALU.mult))
                steps.did(nc.vector.tensor_tensor(k_pe[:], k_pe[:], rstd[:, 32:36].unsqueeze(2).to_broadcast([P, NT, 32]), ALU.mult))
                steps.settle()
                steps.did(nc.vector.tensor_tensor(k_pe[:], k_pe[:], row("g_k", 64, 32).unsqueeze(1).to_broadcast([P, NT, 32]), ALU.mult))
                dve.wait_ge(turned_ready, 1)
                cos, sin = (cos_sin[:, j, :].rearrange("p (a b) -> p a b", a=NT) for j in range(2))

                def turn(x1, x2, c, s, t4):
                    for j, (x, f) in enumerate(((x1, c), (x2, s), (x2, c), (x1, s))):
                        steps.settle()
                        steps.did(nc.vector.tensor_tensor(t4[j], x, f, ALU.mult))
                    steps.settle()
                    steps.did(nc.vector.tensor_tensor(x1, t4[0], t4[1], ALU.subtract))
                    steps.did(nc.vector.tensor_tensor(x2, t4[2], t4[3], ALU.add))

                dve.wait_ge(squared, 2 * NT)
                q4 = q_t.rearrange("p t (a b) -> p t a b", a=8)
                wide = [P, NT, 8, 16]
                turn(q4[:, :, :, 64:80], q4[:, :, :, 80:96], cos.unsqueeze(2).to_broadcast(wide), sin.unsqueeze(2).to_broadcast(wide),
                     [turn_tmp[:, j, :].rearrange("p (t a b) -> p t a b", t=NT, a=8) for j in range(4)])
                turn(k_pe[:, :, 0:16], k_pe[:, :, 16:32], cos, sin,
                     [turn_tmp[:, j, 0:64].rearrange("p (t b) -> p t b", t=NT) for j in range(4)])
                for t in range(NT):
                    steps.settle()
                    steps.did(nc.vector.tensor_copy(k4[:, t, :, 64:96], k_pe[:, t, :].unsqueeze(1).to_broadcast([P, 8, 32])))
                steps.settle()
                nc.vector.tensor_copy(stat[:, 0:1], k_pe[:, 0, 0:1]).then_inc(qk_ready, 1)

            def mla():
                def take_turned(name, dst, head):
                    m = AW[name, head]
                    work.wait_full(dve, m)
                    nc.vector.tensor_copy(dst[0:96, head % 2, :], work.bank(m)[0:96, :]).then_inc(work.done[m % BANKS], 1)

                take_turned("q", qT, 0)
                take_turned("k", kT, 0)
                for n in range(MLA_BLOCKS + 1):
                    if n < MLA_BLOCKS:
                        head, i = divmod(n, NT)
                        m = AW["scores", n]
                        work.wait_full(dve, m)
                        nc.vector.tensor_reduce(neg_m[:, n:n + 1], work.bank(m)[:, 0:(i + 1) * P], AX_X, ALU.max,
                                                negate=True).then_inc(m_ready, 1)
                        work.wait_done(dve, m)
                        steps.did(nc.vector.reciprocal(rden[:, n:n + 1], den[:, n:n + 1]))
                        steps.settle()
                        p = prob[:, n % 2, 0:(i + 1) * P]
                        nc.vector.tensor_scalar(p, p, rden[:, n:n + 1], None, ALU.mult).then_inc(prob_ready, 1)
                    if n and n % NT == 0:
                        head = n // NT - 1
                        m, q = AW["out", head], 64 * (head % 2)
                        bank_halves(y[:, :, head // 2, :], m, slice(q, q + 64))
                    if n % NT == 1 and n // NT + 1 < MLA_HEADS:
                        take_turned("q", qT, n // NT + 1)
                        take_turned("k", kT, n // NT + 1)

            def exponents(n):
                s = 1 << (n - 1)
                c4 = cum.rearrange("p c (n two s) -> p (c n) two s", two=2, s=s)
                e4 = pair[:, n % 2].rearrange("p c (n two s) -> p (c n) two s", two=2, s=s)
                left, right = c4[:, :, 0, :], c4[:, :, 1, :]
                mid = c4[:, :, 0, s - 1:s].to_broadcast([P, T // s, s])
                steps.did(nc.vector.tensor_tensor(e4[:, :, 0, :], mid, left, ALU.subtract))
                nc.vector.tensor_tensor(e4[:, :, 1, :], right, mid, ALU.subtract).then_inc(exponent_ready, 1)

            def pairs_of(n):
                s = 1 << (n - 1)
                cut = lambda x, half: x.rearrange("p c (n two s) -> p (c n) two s", two=2, s=s)[:, :, half, :]
                e = pair[:, n % 2]
                dve.wait_ge(decay_ready, n)
                steps.did(nc.vector.tensor_tensor(cut(e, 0), cut(e, 0), cut(gk, 0), ALU.mult))
                nc.vector.tensor_tensor(cut(e, 1), cut(e, 1), cut(gq, 1), ALU.mult).then_inc(pair_ready, 1)

            def take_level(n):
                for q in range(NT):
                    m = GW["level", n, q]
                    work.wait_full(dve, m)
                    acc = near[:, 2 * (q // 2):2 * (q // 2) + 2, :].rearrange("p t (c r b) -> p (t c) r b", c=2, r=2)[:, :, q % 2, :]
                    o = work.bank(m)[:].rearrange("p (a b) -> p a b", a=4)
                    if n == 0:
                        x = nc.vector.tensor_tensor(acc, o, ident[:].unsqueeze(1).to_broadcast([P, 4, P]), ALU.mult)
                    else:
                        work.wait_done(dve, GW["level", n - 1, q])
                        x = nc.vector.copy_predicated(
                            acc, level_mask[:, n - 1, :].bitcast(U32).unsqueeze(1).to_broadcast([P, 4, P]), o)
                    x.then_inc(work.done[m % BANKS], 1)

            def gla():
                g, m = base["gla_in"][1:]
                dve.wait_ge(logit_logged, 1)
                dve.wait_ge(masks_ready, N_MASKS)
                steps.did(nc.vector.scalar_tensor_tensor(logit, logit, 0.0, log_p, ALU.min, ALU.subtract))
                steps.settle()
                for c in range(2):
                    for i in range(NT):
                        tile = slice(i * P, (i + 1) * P)
                        steps.did(nc.vector.tensor_tensor_scan(cum[:, c, tile], ones[:], logit[:, c, tile], 0.0, ALU.mult, ALU.add))
                steps.settle()
                for c in range(2):
                    steps.did(nc.vector.tensor_scalar(tot16[:, c, :], cum[:, c, :].rearrange("p (a b) -> p a b", b=P)[:, :, P - 1],
                                                      1.0 / 16, None, ALU.mult))
                for c in range(4):
                    stream.wait_done(dve, g + c)
                exponents(1)
                pairs_of(1)
                exponents(2)
                take_level(0)
                pairs_of(2)
                for n in range(3, LEVELS):
                    take_level(n - 2)
                    exponents(n)
                    if n == 3:
                        for t in range(NT):
                            stream.wait_done(dve, g + 8 + t)
                            steps.did(nc.vector.tensor_tensor(gr[:, t, :], gr[:, t, :], row("gla_norm", 0, 512), ALU.mult))
                    pairs_of(n)
                steps.settle()
                nc.vector.tensor_copy(stat[:, 0:1], tot16[:, 0, 0:1]).then_inc(exponent_ready, 1)
                take_level(LEVELS - 2)
                dve.wait_ge(far_exp, 1)
                for c in range(2):
                    steps.did(nc.vector.tensor_tensor(kd[:, c, 0:3 * P], kd[:, c, 0:3 * P], gk[:, c, 0:3 * P], ALU.mult))
                    for slot, i in enumerate((1, 3, 2)):
                        v = qd[:, c, slot * P:(slot + 1) * P]
                        steps.did(nc.vector.tensor_tensor(v, v, gq[:, c, i * P:(i + 1) * P], ALU.mult))
                    steps.settle()
                    steps.did(nc.vector.tensor_scalar(kd[:, c, 3 * P:4 * P], kd[:, c, 0:P], exp_tot[:, c, 1:2], None, ALU.mult))
                    x = nc.vector.tensor_scalar(qd[:, c, 3 * P:4 * P], qd[:, c, P:2 * P], exp_tot[:, c, 2:3], None, ALU.mult)
                    if c == 0:
                        steps.did(x)
                    else:
                        x.then_inc(far_ready, 1)
                take_level(LEVELS - 1)
                for i in range(NT):
                    work.wait_done(dve, GW["level", LEVELS - 1, i])
                for i in range(NT):
                    nc.vector.tensor_copy(stat[:, 60 + i:61 + i], near[:, i, 0:1]).then_inc(near_ready, 1)
                for t in range(NT):
                    dve.wait_ge(go_squared, t + 1)
                    steps.did(nc.vector.tensor_reduce(stat[:, 4 * t:4 * t + 4], go_sq[:, t, :].rearrange("p (a b) -> p a b", a=4),
                                                      AX_X, ALU.add))
                steps.settle()
                nc.vector.tensor_scalar(ms[:, 0:16], stat[:, 0:16], 1.0 / P, EPS, ALU.mult, ALU.add).then_inc(ms_ready, 1)
                rsqrt(16)
                dve.wait_ge(rstd_ready, calls[0])
                for t in range(NT):
                    v = go[:, t, :].rearrange("p (a b) -> p a b", a=4)
                    steps.did(nc.vector.tensor_tensor(v, v, rstd[:, 4 * t:4 * t + 4].unsqueeze(2).to_broadcast([P, 4, P]), ALU.mult))
                    steps.settle()
                    nc.vector.tensor_tensor(go[:, t, :], go[:, t, :], gr[:, t, :], ALU.mult).then_inc(go_ready, 1)
                for head in range(GLA_HEADS):
                    bank_halves(branch[0][:, :, head, :], GW["y", head], slice(0, P))

            def swa():
                nc.vector.tensor_scalar(neg_sink[:], row("sinks", 0, 8), -1.0, None, ALU.mult).then_inc(sink_ready, 1)
                dve.wait_ge(sink_ready, 1)
                for n in range(SWA_BLOCKS + 1):
                    if n < SWA_BLOCKS:
                        m = SW["scores", n]
                        two = slice(2 * n, 2 * n + 2)
                        q_head = 4 * (n % 2) + n // 4
                        own = lambda x: x[:, q_head:q_head + 1].to_broadcast([P, 2])
                        work.wait_full(dve, m)
                        steps.did(nc.vector.tensor_reduce(neg_m[:, two], work.bank(m)[:].rearrange("p (s b) -> p s b", s=2),
                                                          AX_X, ALU.max, negate=True))
                        steps.settle()
                        nc.vector.tensor_tensor(neg_m[:, two], neg_m[:, two], own(neg_sink), ALU.min).then_inc(m_ready, 1)
                        dve.wait_ge(m_ready, MLSTM_BLOCKS + MLA_BLOCKS + n + 1)
                        nc.vector.tensor_tensor(sink_m[:, two], neg_m[:, two], own(row("sinks", 0, 8)), ALU.add).then_inc(sink_ready, 1)
                        work.wait_done(dve, m)
                        steps.did(nc.vector.tensor_tensor(den[:, two], den[:, two], sink_m[:, two], ALU.add))
                        steps.settle()
                        steps.did(nc.vector.reciprocal(rden[:, two], den[:, two]))
                        steps.settle()
                        for s in range(2):
                            p = sprob[:, n % 2, 256 * s:256 * s + 256]
                            x = nc.vector.tensor_scalar(p, p, rden[:, 2 * n + s:2 * n + s + 1], None, ALU.mult)
                            if s == 0:
                                steps.did(x)
                        x.then_inc(sprob_ready, 1)
                    if n and n % NT == 0:
                        j = n // NT - 1
                        bank_halves(branch[1][:, :, j, :], SW["out", j], slice(0, P))

            def pool():
                g = base["pool"][1]
                nc.vector.memset(pu[:, :, 0:16], 0.0).then_inc(pad_ready, 1)
                dve.wait_ge(pad_ready, 1)
                dve.wait_ge(freq_ready, 2)
                for c in range(4):
                    stream.wait_done(dve, g + c)
                    src = pu[:, c, :]
                    for r in range(c + 1):
                        k, lo = 1 << r, (2 << r) - 1
                        dst = psum_a[:, r % 2, :]
                        steps.did(nc.vector.tensor_tensor(dst[:, lo:16 + T], src[:, lo:16 + T], src[:, lo - k:16 + T - k], ALU.add))
                        steps.settle()
                        src = dst
                    w = 2 << c
                    steps.did(nc.vector.tensor_tensor(stat[:, 0:w], src[:, 16:16 + w], inv_count[:, 0:w], ALU.mult))
                    v = tmp[:, c, :]
                    steps.did(nc.vector.scalar_tensor_tensor(v[:, w:T], src[:, 16 + w:16 + T], 1.0 / w, pu[:, c, 16 + w:16 + T],
                                                             ALU.mult, ALU.subtract))
                    steps.settle()
                    steps.did(nc.vector.tensor_tensor(v[:, 0:w], stat[:, 0:w], pu[:, c, 16:16 + w], ALU.subtract))
                    steps.settle()
                    keep_halves((pd[:, 0, c, :], pd[:, 1, c, :]), v).then_inc(pd_ready, 1)
                    dve.wait_ge(pd_ready, c + 1)
                for c in range(4):
                    n = g + 4 + c
                    stream.wait_full(dve, n)
                    nc.vector.tensor_scalar(tmp[:, c, :], stream.bank(n)[:], col("pool_scale", c), None, ALU.mult).then_inc(
                        stream.done[n % BANKS], 1)
                    stream.wait_done(dve, n)
                    keep_halves((branch[2][:, 0, c, :], branch[2][:, 1, c, :]), tmp[:, c, :]).then_inc(branch_ready, 1)
                dve.wait_ge(branch_ready, 4)

            def merge():
                g = base["merge"][1]
                for n in range(3 * DC):
                    c, b = divmod(n, 3)
                    o = g + 2 * n + 1
                    stream.wait_full(dve, o)
                    stream.wait_done(dve, o - 1)
                    nc.vector.tensor_tensor(tmp[:, 3 if b == 0 else 2, :], stream.bank(o)[:], tmp[:, n % 2, :], ALU.mult).then_inc(
                        stream.done[o % BANKS], 1)
                    stream.wait_done(dve, o)
                    if b:
                        steps.did(nc.vector.tensor_tensor(tmp[:, 3, :], tmp[:, 3, :], tmp[:, 2, :], ALU.add))
                        steps.settle()
                    if b == 2:
                        keep_halves((merged[:, 0, c, :], merged[:, 1, c, :]), tmp[:, 3, :]).then_inc(y_ready, 1)
                        dve.wait_ge(y_ready, DC + c + 1)

            def convffn():
                g = base["convffn"][1]

                def body(i):
                    for j in range(4):
                        b, gate = j // 2, j % 2 == 0
                        c = 2 * i + b + (0 if gate else FC)
                        dve.wait_ge(conv_started, 4 * i + j + 1)
                        o = stream.bank(g + j)
                        nc.vector.scalar_tensor_tensor(tmp[:, j, 1:T], o[:, 0:T - 1], cols[:, bass.ds(c + COLS["cw1"], 1)],
                                                       tmp[:, j, 1:T], ALU.mult, ALU.add).then_inc(dve_steps, 1)
                        dve.wait_ge(dve_steps, steps.n + 6 * i + j + (j > 1) + 1)
                        nc.vector.scalar_tensor_tensor(tmp[:, j, 2:T], o[:, 0:T - 2], cols[:, bass.ds(c + COLS["cw0"], 1)],
                                                       tmp[:, j, 2:T], ALU.mult, ALU.add).then_inc(stream.done[(g + j) % BANKS], 1)
                        if not gate:
                            dve.wait_ge(gelu_ready, 2 * i + b + 1)
                            dve.wait_ge(stream.done[(g + j) % BANKS], i + (g + j) // BANKS + 1)
                            v = tmp[:, j, :]
                            nc.vector.tensor_tensor(v, v, tmp[:, j - 1, :], ALU.mult).then_inc(conv_product, 1)
                            dve.wait_ge(conv_product, 2 * i + b + 1)
                            hi, lo = (act[:, p, bass.ds(2 * i + b, 1), :] for p in range(2))
                            nc.vector.tensor_copy(hi, v.unsqueeze(1)).then_inc(dve_steps, 1)
                            dve.wait_ge(dve_steps, steps.n + 6 * i + 3 * b + 3)
                            nc.vector.tensor_tensor(lo, v.unsqueeze(1), hi.bitcast(F32), ALU.subtract).then_inc(act_ready, 1)

                with dve.Fori(0, 2 * FC // 4) as i:
                    body(i)
                steps.n += 3 * FC

            rope_angles()
            norm("norm_mix0", "g_mix0")
            even_in()
            add_outs(base["even_out"][1], DC)
            if on("norm_ffn0"): norm("norm_ffn0", "g_ffn0")
            if on("ffn0"): ffn("ffn0")
            if on("norm_ple0"): norm("norm_ple0", "g_ple0")
            if on("ple0"): ple("ple0")
            if on("norm_mix1"): norm("norm_mix1", "g_mix1")
            if on("odd_in"): odd_in()
            if on("mlstm"): mlstm()
            if on("mla_up"): mla_up()
            if on("mla"): mla()
            if on("odd_out"): add_outs(base["odd_out"][1], DC)
            if on("norm_ffn1"): norm("norm_ffn1", "g_ffn1")
            if on("ffn1"): ffn("ffn1")
            if on("norm_ple1"): norm("norm_ple1", "g_ple1")
            if on("ple1"): ple("ple1")
            if on("norm_mix2"): norm("norm_mix2", "mix_pre")
            if on("gla"): gla()
            if on("swa"): swa()
            if on("pool"): pool()
            if on("merge"): merge()
            if on("norm_post"): norm("norm_post", "mix_post")
            if on("norm_ffn2"): norm("norm_ffn2", "ffn_pre")
            if on("convffn"): convffn()
            if on("norm_last"): norm("norm_last", "ffn_post")


def feature_units(w):
    k, n = w.shape
    return w.reshape(k // P, P, n // P, P).transpose(2, 1, 0, 3).reshape(n // P, P, k)


def token_units(w):
    return w.reshape(4, 2, P, 512).transpose(0, 2, 1, 3).reshape(4, P, 1024)


def down_units(w):
    return w.reshape(2, 11, P, DC, P).transpose(3, 0, 2, 1, 4).reshape(2 * DC, P, 11 * P)


def pairs(gate, up):
    import numpy as np
    return np.stack([feature_units(gate), feature_units(up)], 1).reshape(2 * FC, P, D)


def chunks(v):
    return v.reshape(-1, P).T


def tokens_first(x):
    return x.reshape(T, -1, P).transpose(2, 1, 0)


def lay_out(i):
    import numpy as np
    o = {}
    o["x"] = tokens_first(i["x"][0])
    o["p0"] = tokens_first(i["p"][0, 0])
    c = {"g_mix0": i["g_mix"][0], "g_ffn0": i["g_ffn"][0], "g_ple0": i["g_ple"][0],
         "g_mix1": i["g_mix"][1], "g_ffn1": i["g_ffn"][1], "g_ple1": i["g_ple"][1],
         "mix_pre": i["norm_mix_pre_2"], "mix_post": i["norm_mix_post_2"],
         "ffn_pre": i["norm_ffn_pre_2"], "ffn_post": i["norm_ffn_post_2"],
         "w_conv": i["ev_w_conv"], "g_qa": i["od_g_qa"], "g_kva": i["od_g_kva"], "gla_b": i["gla_b_gate_2"],
         "pool_scale": i["pool_scale_2"], "cw0": i["ffn_conv_w_2"][0, 0], "cw1": i["ffn_conv_w_2"][0, 1],
         "cw2": i["ffn_conv_w_2"][0, 2], "cb": i["ffn_conv_b_2"]}
    o["cols"] = np.concatenate([chunks(c[n]) for n in COLS], 1)
    r = {"g_v": i["ev_g_v"], "g_q": i["od_g_q"], "g_k": i["od_g_k"], "b_gate": i["od_b_gate"], "g_mh": i["od_g_mh"],
         "gla_norm": i["gla_norm_2"], "sinks": i["swa_sinks_2"]}
    o["rows"] = np.concatenate([r[n].reshape(-1) for n in ROWS])
    o["w_s"] = i["ev_w_s"][0].transpose(2, 0, 1)
    o["b_s"] = i["ev_b_s"]
    w = i["ev_w_in"][0]
    fu = feature_units(w[:, :2048]).reshape(4, 4, P, D)
    o["w_even"] = np.concatenate([fu[[1, 2, 0]].transpose(1, 0, 2, 3).reshape(12, P, D), fu[3], token_units(w[:, 2048:])])
    o["w_even_out"] = feature_units(i["ev_w_out"][0])
    for l in range(2):
        o[f"w_up{l}"] = pairs(i["w_gate"][l], i["w_up"][l])
        o[f"w_down{l}"] = down_units(i["w_down"][l])
        o[f"w_ple{l}"] = np.concatenate([feature_units(i["w_ple_gate"][l]), feature_units(i["w_ple_proj"][l])], 2)
    o["p1"] = tokens_first(i["p"][1, 0])
    w = i["od_w_in"][0]
    at = np.cumsum([0, 384, 256, 32, 256, 256, 512, 512, 8])
    q_lat, kv_lat, k_pe, mq, mk, mv, mo, gates = (w[:, x:y] for x, y in zip(at[:-1], at[1:]))
    o["w_odd"] = np.concatenate([feature_units(v) for v in (q_lat, kv_lat, mq, mk)] + [token_units(v) for v in (mv, mo)])
    o["w_small"] = np.concatenate([k_pe, gates], 1).reshape(DC, P, 40).transpose(1, 0, 2)
    o["positions"] = i["positions"].reshape(NT, P).T
    o["w_q_up"] = i["od_w_q_up"][0].reshape(3, P, 2, 384).transpose(2, 1, 0, 3).reshape(2, P, 1152)
    o["w_kv_up"] = i["od_w_kv_up"][0].reshape(2, P, 2, 512).transpose(2, 1, 0, 3).reshape(2, P, 1024)
    o["w_odd_out"] = feature_units(i["od_w_out"][0])
    w = i["w_in_2"][0]
    at = np.cumsum([0, 256, 256, 512, 16, 512, 512, 128, 128, 512, 3072])
    g_q, g_k, g_v, low, g_r, s_q, s_k, s_v, p_u, gate = (w[:, x:y] for x, y in zip(at[:-1], at[1:]))
    o["w_gla"] = np.concatenate([feature_units(g_q), feature_units(g_k), token_units(g_v), token_units(g_r)])
    o["w_low"] = low.reshape(DC, P, 16).transpose(1, 0, 2)
    o["w_gate_up"] = i["gla_w_gate_up_2"][0]
    s_q = s_q.reshape(D, 2, 4, 64).transpose(0, 2, 1, 3).reshape(D, 512)
    o["w_swa"] = np.concatenate([feature_units(s_q), feature_units(s_k), feature_units(s_v)])
    o["w_pool"] = feature_units(p_u)
    o["w_group"] = i["pool_w_2"][0].transpose(1, 0, 2).reshape(1, P, 512)
    swa = i["w_branch_swa_2"][0].reshape(2, 4, 64, D).transpose(1, 0, 2, 3).reshape(512, D)
    o["w_merge"] = np.stack([np.concatenate([feature_units(gate[:, D * b:D * b + D]), feature_units(v)], 2)
                             for b, v in enumerate((i["w_branch_gla_2"][0], swa, i["w_branch_pool_2"][0]))], 1).reshape(3 * DC, P, 12 * P)
    o["w_block_out"] = feature_units(i["w_out_2"][0])
    w = i["ffn_w_up_2"][0]
    o["w_up2"] = pairs(w[:, :FF], w[:, FF:])
    o["w_down2"] = down_units(i["ffn_w_down_2"][0])
    return o


def kernel(**inputs):
    import numpy as np
    import concourse.bacc as bacc
    from concourse.bass_utils import run_bass_kernel_spmd

    nc = bacc.Bacc("TRN2", target_bir_lowering=False, num_devices=1)
    arrays, aps = {}, {}
    for name, v in lay_out({k: np.asarray(v) for k, v in inputs.items()}).items():
        arrays[f"in_{name}"] = np.ascontiguousarray(v)
        aps[name] = nc.dram_tensor(f"in_{name}", v.shape, mybir.dt.from_np(v.dtype), kind="ExternalInput").ap()
    out = nc.dram_tensor("out_dram", (P, DC, T), F32, kind="ExternalOutput").ap()
    build(nc, aps, out)
    r = run_bass_kernel_spmd(nc, [arrays], core_ids=[0])
    return r.results[0]["out_dram"].transpose(2, 1, 0).reshape(1, T, D)
```

```python
from contextlib import ExitStack

import concourse.bass as bass
from concourse import mybir

F32 = mybir.dt.float32
F32R = mybir.dt.float32r
I32 = mybir.dt.int32
BF16 = mybir.dt.bfloat16
U32 = mybir.dt.uint32
ALU = mybir.AluOpType
ACT = mybir.ActivationFunctionType
AX_X = mybir.AxisListType.X

P = 128
T = 512
NT = T // P
D = 1024
DC = D // P
EPS = 1e-6
NEG = -1e30
FF = 2816
FC = FF // P
SLOTS = 2
SLOT = 12 * P
BANKS = 4
X_PARTS = 4
LNEXP = "natural_log_exp_and_others"
FFN_UNITS = 2 * FC + 2 * DC
FFN_OUTS = 2 * FC + DC

STAGES = [
    ("norm_mix0", 0, 0, 2),
    ("even_in", 20, 20, 4),
    ("even_out", 8, 8, 0),
    ("norm_ffn0", 0, 0, 2),
    ("ffn0", FFN_UNITS, FFN_OUTS, 0),
    ("norm_ple0", 0, 0, 2),
    ("ple0", 8, 16, 0),
    ("norm_mix1", 0, 0, 2),
    ("odd_in", 17, 17, 2),
    ("mla_up", 4, 16, 0),
    ("mlstm", 0, 0, 65),
    ("mla", 0, 0, 92),
    ("odd_out", 8, 8, 0),
    ("norm_ffn1", 0, 0, 2),
    ("ffn1", FFN_UNITS, FFN_OUTS, 0),
    ("norm_ple1", 0, 0, 2),
    ("ple1", 8, 16, 0),
    ("norm_mix2", 0, 0, 2),
    ("gla_in", 13, 13, 2),
    ("gla", 0, 0, 48),
    ("swa", 6, 6, 36),
    ("pool", 5, 8, 0),
    ("merge", 24, 48, 0),
    ("block_out", 8, 8, 0),
    ("norm_post", 0, 0, 2),
    ("norm_ffn2", 0, 0, 2),
    ("convffn", FFN_UNITS, FFN_OUTS, 0),
    ("norm_last", 0, 0, 2),
]

COLS = {}
COLS_N = 0
for _name, _n in (
    ("g_mix0", 8), ("g_ffn0", 8), ("g_ple0", 8), ("g_mix1", 8), ("g_ffn1", 8), ("g_ple1", 8),
    ("mix_pre", 8), ("mix_post", 8), ("ffn_pre", 8), ("ffn_post", 8),
    ("w_conv", 12), ("g_qa", 3), ("g_kva", 2), ("gla_b", 2), ("pool_scale", 4),
    ("cw0", 44), ("cw1", 44), ("cw2", 44), ("cb", 44),
):
    COLS[_name] = COLS_N
    COLS_N += _n

ROWS = {}
ROWS_N = 0
for _name, _n in (("g_v", 512), ("g_q", 96), ("g_k", 96), ("b_gate", 8), ("g_mh", 512), ("gla_norm", 512), ("sinks", 8)):
    ROWS[_name] = ROWS_N
    ROWS_N += _n


def stage_bases():
    u = g = m = 0
    base = {}
    for name, units, outs, works in STAGES:
        base[name] = (u, g, m)
        u, g, m = u + units, g + outs, m + works
    return base, u


class Turns:

    def __init__(self, banks, full, done):
        self.banks, self.full, self.done = banks, full, done

    def bank(self, n):
        return self.banks[n % BANKS]

    def wait_full(self, eng, n, more=0):
        eng.wait_ge(self.full[n % BANKS], more + n // BANKS + 1)

    def wait_done(self, eng, n, more=0):
        eng.wait_ge(self.done[n % BANKS], more + n // BANKS + 1)

    def wait_free(self, eng, n, more=0):
        if n >= BANKS:
            eng.wait_ge(self.done[n % BANKS], more + n // BANKS)


class Steps:

    def __init__(self, eng, sem):
        self.eng, self.sem, self.n = eng, sem, 0

    def did(self, ins):
        ins.then_inc(self.sem, 1)
        self.n = self.n + 1

    def settle(self):
        self.eng.wait_ge(self.sem, self.n)


RSQRTS = {"norm_mix0": 1, "norm_ffn0": 3, "norm_ple0": 4, "norm_mix1": 5, "norm_ffn1": 10, "norm_ple1": 11,
          "norm_mix2": 12, "norm_post": 14, "norm_ffn2": 15, "norm_last": 16}
FFN_NO = {"ffn0": 0, "ffn1": 1, "convffn": 2}
MLSTM_HEADS = 4
HV_BLOCK = 9
MLSTM_BLOCKS = MLSTM_HEADS * NT
MLA_HEADS = 8
GLA_HEADS = 4
LEVELS = 8
SWA_PAIRS = 4
SWA_BLOCKS = SWA_PAIRS * NT
MLA_BLOCKS = MLA_HEADS * NT
PI = 3.141592653589793
TWO_PI = 2 * PI
ROUND = 12582912.0
TURN_PARTS = (6.28125, 0.0019350051879882812, 3.0199159795074593e-07)


def ffn_units(up, down):
    return [("out", up, i) for i in range(2 * FC)] + [(("half", "out")[i % 2], down, i) for i in range(2 * DC)]


def fm(array, n, at=0):
    return [("out", array, at + i) for i in range(n)]


def tm(array, at=0):
    return [(("part", "part", "part", "tokens")[i], array, at + i) for i in range(4)]


UNITS = {
    "even_in": fm("w_even", 16) + tm("w_even", 16),
    "even_out": fm("w_even_out", 8),
    "ffn0": ffn_units("w_up0", "w_down0"),
    "ple0": [("two", "w_ple0", i) for i in range(8)],
    "odd_in": fm("w_odd", 9) + tm("w_odd", 9) + tm("w_odd", 13),
    "mla_up": [("tokens", "w_q_up", 0), ("tokens", "w_q_up", 1), ("tokens", "w_kv_up", 0), ("tokens", "w_kv_up", 1)],
    "odd_out": fm("w_odd_out", 8),
    "ffn1": ffn_units("w_up1", "w_down1"),
    "ple1": [("two", "w_ple1", i) for i in range(8)],
    "gla_in": fm("w_gla", 5) + tm("w_gla", 5) + tm("w_gla", 9),
    "swa": fm("w_swa", 6),
    "pool": fm("w_pool", 4) + [("four", "w_group", 0)],
    "merge": [("two", "w_merge", i) for i in range(24)],
    "block_out": fm("w_block_out", 8),
    "convffn": ffn_units("w_up2", "w_down2"),
}
AFTER_NORM = {"even_in": "norm_mix0", "ffn0": "norm_ffn0", "ple0": "norm_ple0", "odd_in": "norm_mix1",
              "ffn1": "norm_ffn1", "ple1": "norm_ple1", "gla_in": "norm_mix2", "convffn": "norm_ffn2"}
BEFORE = {"norm_ffn0": "even_out", "norm_ple0": "ffn0", "norm_mix1": "ple0", "norm_ffn1": "odd_out",
          "norm_ple1": "ffn1", "norm_mix2": "ple1", "norm_post": "block_out", "norm_last": "convffn"}


def gla_order():
    return ([("level", n, i) for n in range(LEVELS) for i in range(NT)]
            + [(part, head) for head in range(GLA_HEADS) for part in ("far_a", "far_b")]
            + [("o", i) for i in range(NT)] + [("y", head) for head in range(GLA_HEADS)])


def swa_order():
    order = []
    for n in range(SWA_BLOCKS + 2):
        if n < SWA_BLOCKS:
            order.append(("scores", n))
        if n >= 2:
            order.append(("turned", n - 2))
        if n > NT and n % NT == 1:
            order.append(("out", n // NT - 1))
    return order


def mlstm_order():
    order = [("sums", 0), ("decay", 0)]
    for n in range(MLSTM_BLOCKS + 2):
        if n + 1 < MLSTM_BLOCKS:
            order.append(("decay", n + 1))
        if n < MLSTM_BLOCKS:
            order.append(("scores", n))
        if 1 <= n <= MLSTM_BLOCKS:
            order.append(("turned", n - 1))
        if n >= 2:
            order.append(("out", n - 2))
    return order


def mla_order():
    order = [("q", 0), ("k", 0)]
    for n in range(MLA_BLOCKS + 2):
        if n < MLA_BLOCKS:
            order.append(("scores", n))
        if n >= 2:
            order.append(("turned", n - 2))
        if n > NT and n % NT == 1:
            order.append(("out", n // NT - 1))
        if n % NT == 1 and n // NT + 1 < MLA_HEADS:
            order += [("q", n // NT + 1), ("k", n // NT + 1)]
        if n == HV_BLOCK:
            order += [("y", head) for head in range(MLSTM_HEADS)]
    return order


def build(nc, a, out):
    base, n_units = stage_bases()

    with ExitStack() as ctx:
        def sb(name, shape, dt=F32):
            return ctx.enter_context(nc.sbuf_tensor("s_" + name, shape, dt))

        def sem(name):
            return ctx.enter_context(nc.semaphore(name))

        def sems(name, n):
            return [sem(f"{name}{i}") for i in range(n)]

        h = sb("h", [P, DC, T])
        ring = sb("ring", [P, SLOTS, SLOT])
        split_ring = sb("split_ring", [P, SLOTS, 2, SLOT], F32R)
        arena_at = nc.sbuf_base
        arena = sb("arena", [P, 2 * DC * T + 2 * FC * T])
        tmp = sb("tmp", [P, 4, T])
        cols = sb("cols", [P, COLS_N])
        rows = sb("rows", [P, ROWS_N])
        zero = sb("zero", [P, 1])
        ident = sb("ident", [P, P])
        ones = sb("ones", [P, P])
        upto = sb("upto", [P, P])
        below = sb("below", [P, P])
        ident_b = sb("ident_b", [P, P], BF16)
        neg_after = sb("neg_after", [P, P], BF16)
        neg_until = sb("neg_until", [P, P], BF16)
        ms = sb("ms", [P, 64])
        ln_ms = sb("ln_ms", [P, 64])
        rs0 = sb("rs0", [P, 64])
        rt = sb("rt", [P, 2, 64])
        rstd = sb("rstd", [P, 64])
        stat = sb("stat", [P, 64])

        def region(at, *shape):
            n = 1
            for s in shape:
                n *= s
            v = arena[:, at:at + n]
            if len(shape) == 2:
                v = v.rearrange("p (a b) -> p a b", a=shape[0])
            if len(shape) == 3:
                v = v.rearrange("p (a b c) -> p a b c", a=shape[0], b=shape[1])
            return v, at + n

        def halves_of(name, at, n):
            v = nc.alloc_sbuf_tensor_at("s_" + name, [P, 2, n, T], F32R, offset=arena_at + 4 * at)
            return v[:], at + 2 * n * T

        hn, A = halves_of("hn", 0, DC)
        act, _ = halves_of("act", A, FC)
        y, Y_END = halves_of("y", A, DC)
        sq_hn, at = region(0, DC, T)
        o_buf, _ = region(at, DC, T)
        sq_rest, _ = region(A, DC, T)
        p_raw, at = region(Y_END + 4096, 2, T)
        p_in, _ = halves_of("p_in", at, 2)

        ws, at = region(Y_END, 8, P)
        z_pad, at = region(at, 2, 2 + T)
        conv, at = region(at, 2, T)
        u_g, at = region(at, 4, T)
        v_t, at = region(at, NT, 512)
        v_sq, at = region(at, 2, 512)
        b_row = arena[0:1, at:at + 8 * P].rearrange("p (a b) -> p a b", a=8)
        lat_q, at = halves_of("lat_q", Y_END, 3)
        lat_kv, LAT_END = halves_of("lat_kv", at, 2)
        mq, at = region(LAT_END, 2, T)
        mk, at = region(at, 2, T)
        mv, at = region(at, NT, 512)
        mo, at = region(at, NT, 512)
        lat_sq, _ = region(at, 5, T)
        rdiag, end = region(0, MLSTM_BLOCKS, P)
        dec, end = region(end, 3, T)
        sT, end = region(end, 2, T)
        hv, end = region(end, NT, 512)
        hv_sq, _ = region(A, NT, 512)
        assert end <= A
        q_t, at = region(at, NT, 768)
        k_t, at = region(Y_END, NT, 768)
        qk_sq, _ = region(at, 2, 1024)
        turn_tmp, _ = region(at, 4, T)
        v_m = tmp
        qT, at = region(LAT_END, 2, T)
        kT, at = region(at, 2, T)
        prob, at = region(at, 3, T)
        probT, at = region(0, 4, T)
        probT2, at = region(at, 4, T)

        def lat(c, p):
            return lat_q[:, p, c, :] if c < 3 else lat_kv[:, p, c - 3, :]

        branch = []
        at = A
        for b in range(3):
            v, at = halves_of(f"branch{b}", at, 4)
            branch.append(v)
        BRANCH_END = at
        gq, at = region(A, 2, T)
        gk, at = region(at, 2, T)
        cum, at = region(at, 2, T)
        kd, at = region(at, 2, T)
        gv, at = region(at, NT, 512)
        gr, at = region(at, NT, 512)
        pair, at = region(at, 2, 2, T)
        near, at = region(at, NT, 512)
        far, at = region(at, GLA_HEADS, 768)
        qd, at = region(at, 2, T)
        go, at = region(at, NT, 512)
        go_sq = pair.rearrange("p a b c -> p (a b) c")
        logit = near[:, 0:2, :]
        log_p = near[:, 2:4, :]
        pu, at = region(BRANCH_END + 7 * T + 2 * (16 + T), 4, 16 + T)
        sqT, at = region(at, 4, T)
        skT, at = region(at, 1, T)
        sv, at = region(at, NT, P)
        sprob, at = region(BRANCH_END, 3, T)
        sprobT, at = region(at, NT, T)
        psum_a, _ = region(at, 2, 16 + T)
        pd, _ = halves_of("pd", BRANCH_END, 4)
        merged, at = halves_of("merged", BRANCH_END, DC)
        g_low = tmp[0:16, 3, :]
        w_gate_up = sb("w_gate_up", [16, 256])
        level_mask = sb("level_mask", [P, LEVELS - 1, P])
        tot16 = sb("tot16", [P, 2, NT])
        exp_tot = sb("exp_tot", [P, 2, NT])
        neg_sink = sb("neg_sink", [P, 8])
        sink_m = sb("sink_m", [P, 32])
        inv_count = sb("inv_count", [P, 16])
        GW = {k: base["gla"][2] + i for i, k in enumerate(gla_order())}
        SW = {k: base["swa"][2] + i for i, k in enumerate(swa_order())}
        w_small = sb("w_small", [P, DC, 40])
        gates = sb("gates", [P, NT, 8])
        k_pe = sb("k_pe", [P, NT, 32])
        lat_ss = sb("lat_ss", [P, 8])
        lat_rs = sb("lat_rs", [P, 8])
        pos_i = sb("pos_i", [P, NT], I32)
        inv_freq = sb("inv_freq", [P, 16])
        angle = sb("angle", [P, 5, NT * 16])
        cos_sin = sb("cos_sin", [P, 2, NT * 16])
        lf = sb("lf", [P, NT, 4])
        gl = sb("gl", [P, 4, 16])
        neg_sum = sb("neg_sum", [P, 16])
        neg_m = sb("neg_m", [P, 32])
        exp_m = sb("exp_m", [P, 16])
        den = sb("den", [P, 32])
        rden = sb("rden", [P, 32])
        MW = {k: base["mlstm"][2] + i for i, k in enumerate(mlstm_order())}
        AW = {k: base["mla"][2] + i for i, k in enumerate(mla_order())}
        N_TABLES = 6
        N_MASKS = 1 + 3 * (LEVELS - 1)
        N_CONSTS = 14

        def col(name, c=0, n=1):
            return cols[:, COLS[name] + c:COLS[name] + c + n]

        def row(name, at, n):
            return rows[:, ROWS[name] + at:ROWS[name] + at + n]

        stream = Turns([ctx.enter_context(nc.psum_tensor(f"stream_bank{i}", [P, 512], F32)) for i in range(BANKS)],
                       sems("stream_full", BANKS), sems("stream_done", BANKS))
        work = Turns([ctx.enter_context(nc.psum_tensor(f"work_bank{i}", [P, 512], F32)) for i in range(BANKS)],
                     sems("work_full", BANKS), sems("work_done", BANKS))
        slot_loaded = sems("slot_loaded", SLOTS)
        x_loaded = sems("x_loaded", X_PARTS)
        cols_loaded = sem("cols_loaded")
        tables_loaded = sem("tables_loaded")
        p_loaded = sem("p_loaded")
        consts_ready = sem("consts_ready")
        sq_ready = sem("sq_ready")
        ms_ready = sem("ms_ready")
        rs_guessed = sem("rs_guessed")
        rstd_ready = sem("rstd_ready")
        hn_ready = sems("hn_ready", 2)
        k_units = sem("k_units")
        down_half = sem("down_half")
        act_steps = sem("act_steps")
        dve_steps = sem("dve_steps")
        out_stored = sem("out_stored")
        v_gelu = sem("v_gelu")
        v_square = sem("v_square")
        v_ready = sem("v_ready")
        lat_squared = sem("lat_squared")
        gates_ready = sem("gates_ready")
        log_ready = sem("log_ready")
        lf_ready = sem("lf_ready")
        rdiag_ready = sem("rdiag_ready")
        m_ready = sem("m_ready")
        exp_m_ready = sem("exp_m_ready")
        rden_ready = sem("rden_ready")
        hv_squared = sem("hv_squared")
        hv_ready = sem("hv_ready")
        lat_rs_ready = sem("lat_rs_ready")
        squared = sem("squared")
        summed = sem("summed")
        qk_ready = sem("qk_ready")
        prob_ready = sem("prob_ready")
        angle_ready = sem("angle_ready")
        turned_ready = sem("turned_ready")
        freq_ready = sem("freq_ready")
        logit_logged = sem("logit_logged")
        exponent_ready = sem("exponent_ready")
        decay_ready = sem("decay_ready")
        pair_ready = sem("pair_ready")
        near_ready = sem("near_ready")
        masks_ready = sem("masks_ready")
        far_exp = sem("far_exp")
        far_ready = sem("far_ready")
        go_squared = sem("go_squared")
        go_ready = sem("go_ready")
        sink_ready = sem("sink_ready")
        sprob_ready = sem("sprob_ready")
        pad_ready = sem("pad_ready")
        pd_ready = sem("pd_ready")
        h_updated = sem("h_updated")
        conv_started = sem("conv_started")
        gelu_ready = sem("gelu_ready")
        act_ready = sem("act_ready")
        split_ready = sems("split_ready", SLOTS)
        w_high = sem("w_high")
        conv_product = sem("conv_product")
        v_made = sem("v_made")
        hi_made = sem("hi_made")
        y_ready = sem("y_ready")
        lat_ready = sem("lat_ready")
        branch_ready = sem("branch_ready")
        p_split = sem("p_split")

        norm_no = {n: i for i, n in enumerate(s[0] for s in STAGES if s[0].startswith("norm"))}
        hn_no = {n: i for i, n in enumerate(n for n in norm_no if n not in ("norm_post", "norm_last"))}

        def h_out(stage, c):
            g = base[stage][1]
            if "ffn" in stage:
                return g + 2 * FC + c
            return g + (2 * c + 1 if stage.startswith("ple") else c)

        def wait_hn_chunk(eng, norm, c):
            eng.wait_ge(hn_ready[c % 2], DC // 2 * norm + c // 2 + 1)

        def squares_of(stage):
            return sq_rest if stage in ("norm_mix0", "norm_mix1", "norm_mix2") else sq_hn

        def h_ready(eng, norm, c):
            if norm == "norm_ffn2":
                eng.wait_ge(h_updated, c + 1)
            elif norm == "norm_mix0":
                eng.wait_ge(x_loaded[c * X_PARTS // DC], 16)
            else:
                stream.wait_done(eng, h_out(BEFORE[norm], c))

        freed, weights = [], []
        quarters = firsts = 0
        for name, units, _, _ in STAGES:
            g = base[name][1]
            for kind, array, i in UNITS.get(name, []):
                weights.append((array, i))
                if kind == "part":
                    quarters += 1
                    freed.append((k_units, quarters))
                    continue
                if kind == "half":
                    firsts += 1
                    freed.append((down_half, firsts))
                    continue
                g += {"out": 1, "two": 2, "tokens": NT, "four": 4}[kind]
                freed.append((stream.full[(g - 1) % BANKS], (g - 1) // BANKS + 1))
        assert len(weights) == n_units, (len(weights), n_units)

        def wait_unit(eng, u, more=0):
            eng.wait_ge(split_ready[u % SLOTS], more + u // SLOTS + 1)

        block = ctx.enter_context(nc.Block())

        @block.sync
        def _(sp):
            for q in range(X_PARTS):
                cut = slice(q * DC // X_PARTS, (q + 1) * DC // X_PARTS)
                sp.dma_start(h[:, cut, :], a["x"][:, cut, :]).then_inc(x_loaded[q], 16)
            for name, units, _, _ in STAGES:
                u0 = base[name][0]
                u = u0
                while u < u0 + units:
                    array, i = weights[u]
                    n = a[array].shape[2]
                    if u - u0 == SLOTS and FFN_UNITS == units:
                        with sp.Fori(1, 2 * FC // SLOTS) as r:
                            for j in range(SLOTS):
                                sp.wait_ge(split_ready[(u + j) % SLOTS], r + (u0 + j) // SLOTS)
                                sp.dma_start(ring[:, (u + j) % SLOTS, 0:n].unsqueeze(1),
                                             a[array][bass.ds(SLOTS * r + j, 1)].rearrange("a p n -> p a n")).then_inc(
                                    slot_loaded[(u + j) % SLOTS], 16)
                        u = u0 + 2 * FC
                        continue
                    if u >= SLOTS:
                        sp.wait_ge(split_ready[u % SLOTS], u // SLOTS)
                    sp.dma_start(ring[:, u % SLOTS, 0:n], a[array][i]).then_inc(slot_loaded[u % SLOTS], 16)
                    u += 1
            for c in range(DC):
                sp.wait_ge(h_updated, DC + c + 1)
                sp.dma_start(out[:, c, :], h[:, c, :]).then_inc(out_stored, 16)
            sp.wait_ge(turned_ready, 1)
            sp.wait_ge(out_stored, 16 * DC)

        @block.gpsimd
        def _(pool):
            def split(u, n, r=0, more=None, free=None):
                s = u % SLOTS
                pool.wait_ge(slot_loaded[s], 16 * (r + u // SLOTS + 1))
                if free is not None:
                    pool.wait_ge(*free)
                hi = split_ring[:, s, 0, 0:n]
                nc.gpsimd.tensor_tensor(hi, ring[:, s, 0:n], zero[:].to_broadcast([P, n]), ALU.add).then_inc(w_high, 1)
                pool.wait_ge(w_high, (u if more is None else more) + 1)
                nc.gpsimd.tensor_tensor(split_ring[:, s, 1, 0:n], ring[:, s, 0:n], hi.bitcast(F32), ALU.subtract).then_inc(
                    split_ready[s], 1)

            def hn_low(no):
                for c in range(1, DC, 2):
                    pool.wait_ge(hi_made, DC * no + c + 1)
                    nc.gpsimd.tensor_tensor(hn[:, 1, c, :], tmp[:, c % 4, :], hn[:, 0, c, :].bitcast(F32),
                                            ALU.subtract).then_inc(hn_ready[1], 1)

            def split_stage(name, skip=0):
                u0, g, _ = base[name]
                units = dict((s[0], s[1]) for s in STAGES)[name]
                u = u0 + skip
                while u < u0 + units:
                    if u - u0 == SLOTS and name in AFTER_NORM:
                        hn_low(hn_no[AFTER_NORM[name]])
                    if u - u0 == 4 and units == FFN_UNITS:
                        with pool.Fori(1, 2 * FC // 4) as i:
                            for j in range(4):
                                q = g + j - SLOTS
                                split(u0 + j, D, r=(4 // SLOTS) * i, more=u0 + j + 4 * i, free=(stream.full[q % BANKS], i + q // BANKS + 1))
                        u = u0 + 2 * FC
                        continue
                    split(u, a[weights[u][0]].shape[2], free=freed[u - SLOTS] if u >= SLOTS else None)
                    u += 1

            steps = Steps(pool, consts_ready)
            nc.gpsimd.memset(zero[:], 0.0)
            steps.did(nc.gpsimd.memset(ident[:], 0.0))
            steps.did(nc.gpsimd.memset(ones[:], 1.0))
            steps.settle()
            steps.did(nc.gpsimd.affine_select(out=ident[:], in_=ident[:], compare_op=ALU.not_equal, fill=1.0, base=0,
                                              pattern=[[-1, P]], channel_multiplier=1))
            for u in range(SLOTS):
                split(u, D)
            split_stage("even_in", skip=SLOTS)
            pool.wait_ge(tables_loaded, 16 * N_TABLES)
            steps.did(nc.gpsimd.affine_select(out=ws, in_=ws, compare_op=ALU.is_ge, fill=0.0, base=0,
                                              pattern=[[0, 8], [1, P]], channel_multiplier=-1))
            for t, v in ((upto, 1.0), (below, 1.0), (ident_b, 0.0), (neg_after, 0.0), (neg_until, 0.0)):
                steps.did(nc.gpsimd.memset(t[:], v))
            steps.settle()
            for t, op, fill, at, step, mult in (
                (ident_b, ALU.not_equal, 1.0, 0, -1, 1), (upto, ALU.is_ge, 0.0, 0, 1, -1), (below, ALU.is_ge, 0.0, -1, -1, 1),
                (neg_after, ALU.is_ge, NEG, 0, -1, 1), (neg_until, ALU.is_ge, NEG, -1, 1, -1),
            ):
                steps.did(nc.gpsimd.affine_select(out=t[:], in_=t[:], compare_op=op, fill=fill, base=at,
                                                  pattern=[[step, P]], channel_multiplier=mult))
            for j in range(16):
                last = nc.gpsimd.memset(inv_freq[:, j:j + 1], float(10000.0 ** (-j / 16)))
            last.then_inc(freq_ready, 1)
            for j in range(16):
                last = nc.gpsimd.memset(inv_count[:, j:j + 1], 1.0 / (j + 1))
            last.then_inc(freq_ready, 1)
            split_stage("even_out")
            masks = Steps(pool, masks_ready)
            masks.did(nc.gpsimd.memset(level_mask[:], 0.0))
            for n in range(1, LEVELS):
                s = 1 << (n - 1)
                v = level_mask[:, n - 1, :].rearrange("p (n two s) -> p n two s", two=2, s=s)[:, :, 1, :]
                masks.settle()
                masks.did(nc.gpsimd.memset(v, 1.0))
                masks.settle()
                masks.did(nc.gpsimd.affine_select(out=v, in_=v, compare_op=ALU.is_ge, fill=0.0, base=0,
                                                  pattern=[[-2 * s, P // (2 * s)], [0, s]], channel_multiplier=1))
                masks.settle()
                masks.did(nc.gpsimd.affine_select(out=v, in_=v, compare_op=ALU.is_ge, fill=0.0, base=s - 1,
                                                  pattern=[[2 * s, P // (2 * s)], [0, s]], channel_multiplier=-1))
            for name, units, _, _ in STAGES:
                if units and name not in ("even_in", "even_out"):
                    split_stage(name)

        @block.tensor
        def _(pe):
            def norm(stage):
                k, m = norm_no[stage], base[stage][2]
                squares = squares_of(stage)
                work.wait_free(pe, m)
                for c in range(DC):
                    pe.wait_ge(sq_ready, DC * k + c + 1)
                    for t in range(NT):
                        mm = nc.tensor.matmul(work.bank(m)[:, t:t + 1], squares[:, c, t * P:(t + 1) * P], ones[:, 0:1],
                                              start=(c == 0 and t == 0), stop=(c == DC - 1), skip_group_check=True)
                mm.then_inc(work.full[m % BANKS], 1)
                work.wait_free(pe, m + 1)
                pe.wait_ge(rstd_ready, RSQRTS[stage])
                for t in range(NT):
                    mm = nc.tensor.matmul(work.bank(m + 1)[:, t * P:(t + 1) * P],
                                          rstd[:, t:t + 1].to_broadcast([P, P]), ident[:], start=True, stop=True)
                mm.then_inc(work.full[(m + 1) % BANKS], 1)

            def product(o, w, x, start, stop):
                nc.tensor.matmul(o, w(0), x(0), start=start, stop=False)
                nc.tensor.matmul(o, w(0), x(1), start=False, stop=False)
                return nc.tensor.matmul(o, w(1), x(0), start=False, stop=stop)

            def feature_out(u, g, x, k_tiles, at=0, more_u=0, more_g=0, wait_x=None, signal=True, start=True, stop=True, k0=0):
                wait_unit(pe, u, more_u)
                for k in range(k_tiles):
                    if wait_x is not None:
                        wait_x(k)
                    mm = product(stream.bank(g)[:], lambda p: split_ring[:, u % SLOTS, p, at + k * P:at + (k + 1) * P],
                                 lambda p: x(k0 + k, p), start and k == 0, stop and k == k_tiles - 1)
                return mm

            def hn_in(k, p):
                return hn[:, p, k, :]

            def y_in(k, p):
                return y[:, p, k, :]

            def token_outs(u, g, x, per_unit):
                for t in range(NT):
                    stream.wait_free(pe, g + t)
                for i in range(4):
                    wait_unit(pe, u + i)
                    for k in range(2):
                        for t in range(NT):
                            mm = product(stream.bank(g + t)[:], lambda p: x(2 * i + k, p)[:, t * P:(t + 1) * P],
                                         lambda p: split_ring[:, (u + i) % SLOTS, p, k * 512:(k + 1) * 512],
                                         i == 0 and k == 0, i == 3 and k == 1)
                            if i == 3 and k == 1:
                                mm.then_inc(stream.full[(g + t) % BANKS], 1)
                    if i < 3:
                        mm.then_inc(k_units, 1)

            def hn_wait(stage):
                return lambda k: wait_hn_chunk(pe, hn_no[stage], k)

            def simple_outs(u, g, n, x, wait_x):
                for i in range(n):
                    stream.wait_free(pe, g + i)
                    feature_out(u + i, g + i, x, DC, wait_x=wait_x if i == 0 else None).then_inc(
                        stream.full[(g + i) % BANKS], 1)

            def even_in():
                u, g, m = base["even_in"]
                simple_outs(u, g, 16, hn_in, hn_wait("norm_mix0"))
                token_outs(u + 16, g + 16, hn_in, 2)
                pe.wait_ge(consts_ready, 4)
                pe.wait_ge(tables_loaded, 16 * N_TABLES)
                for hp in range(4):
                    work.wait_free(pe, m + hp)
                    for n in range(NT):
                        if hp == 0:
                            pe.wait_ge(v_ready, n + 1)
                        for e in range(2):
                            head = 2 * hp + e
                            o = work.bank(m + hp)[64 * e:64 * e + 64, n * P:(n + 1) * P]
                            nc.tensor.matmul(o, v_t[:, n, head * 64:head * 64 + 64], ws[:, head, :], start=True, stop=False)
                            mm = nc.tensor.matmul(o, ones[0:1, 0:64], b_row[0:1, head, :], start=False, stop=True)
                    mm.then_inc(work.full[(m + hp) % BANKS], 1)

            def ffn(stage, norm_stage):
                u, g, _ = base[stage]
                wait_hn = hn_wait(norm_stage)

                def up(i, first):
                    for j in range(4):
                        pe.wait_ge(stream.done[(g + j) % BANKS], i + (g + j) // BANKS)
                        feature_out(u + j, g + j, hn_in, DC, more_u=i * (4 // SLOTS),
                                    wait_x=wait_hn if first and j == 0 else None).then_inc(stream.full[(g + j) % BANKS], 1)

                up(0, True)
                with pe.Fori(1, 2 * FC // 4) as i:
                    up(i, False)
                u, g2 = u + 2 * FC, g + 2 * FC

                def act_wait(k):
                    pe.wait_ge(act_ready, FC * FFN_NO[stage] + k + 1)

                def down(i, first):
                    for j in range(4):
                        pe.wait_ge(stream.done[(g2 + j) % BANKS], i + (g2 + j) // BANKS)
                        for half in range(2):
                            ux = u + 2 * j + half
                            wait_unit(pe, ux, 8 // SLOTS * i)
                            for k in range(11):
                                if first and j == 0:
                                    act_wait(11 * half + k)
                                mm = product(stream.bank(g2 + j)[:], lambda p: split_ring[:, ux % SLOTS, p, k * P:(k + 1) * P],
                                             lambda p: act[:, p, 11 * half + k, :], half == 0 and k == 0, half == 1 and k == 10)
                            mm.then_inc(stream.full[(g2 + j) % BANKS] if half else down_half, 1)

                down(0, True)
                down(1, False)

            def ple(stage, norm_stage, layer):
                u, g, _ = base[stage]
                wait_hn = hn_wait(norm_stage)
                for c in range(DC):
                    stream.wait_free(pe, g + 2 * c)
                    feature_out(u + c, g + 2 * c, hn_in, DC, wait_x=wait_hn if c == 0 else None).then_inc(
                        stream.full[(g + 2 * c) % BANKS], 1)
                    stream.wait_free(pe, g + 2 * c + 1)
                    if c == 0:
                        pe.wait_ge(p_split, layer + 1)
                    for k in range(2):
                        mm = product(stream.bank(g + 2 * c + 1)[:],
                                     lambda p: split_ring[:, (u + c) % SLOTS, p, (8 + k) * P:(9 + k) * P],
                                     lambda p: p_in[:, p, k, :], k == 0, k == 1)
                    mm.then_inc(stream.full[(g + 2 * c + 1) % BANKS], 1)

            def odd_in():
                u, g, m = base["odd_in"]
                simple_outs(u, g, 9, hn_in, hn_wait("norm_mix1"))
                token_outs(u + 9, g + 9, hn_in, 2)
                work.wait_free(pe, m + 1)
                pe.wait_ge(lat_squared, 5)
                for t in range(NT):
                    for c in range(5):
                        o = t + (NT if c >= 3 else 0)
                        mm = nc.tensor.matmul(work.bank(m + 1)[:, o:o + 1], lat_sq[:, c, t * P:(t + 1) * P], ones[:, 0:1],
                                              start=c in (0, 3), stop=c in (2, 4))
                mm.then_inc(work.full[(m + 1) % BANKS], 1)
                token_outs(u + 13, g + 13, hn_in, 2)
                work.wait_free(pe, m)
                for t in range(NT):
                    for k in range(2 * DC):
                        mm = nc.tensor.matmul(work.bank(m)[:, 40 * t:40 * t + 40], hn[:, k % 2, k // 2, t * P:(t + 1) * P].bitcast(F32),
                                              w_small[:, k // 2, :], start=(k == 0), stop=(k == 2 * DC - 1))
                mm.then_inc(work.full[m % BANKS], 1)

            def mlstm():
                pe.wait_ge(consts_ready, N_CONSTS)
                m = MW["sums", 0]
                work.wait_free(pe, m)
                pe.wait_ge(lf_ready, 1)
                for i in range(NT):
                    for k in range(i + 1):
                        mm = nc.tensor.matmul(work.bank(m)[:, 4 * i:4 * i + 4], (upto if k == i else ones)[:], lf[:, k, :],
                                              start=(k == 0), stop=(k == i))
                mm.then_inc(work.full[m % BANKS], 1)
                def decay(n):
                    head, i = divmod(n, NT)
                    m = MW["decay", n]
                    work.wait_free(pe, m)
                    pe.wait_ge(rdiag_ready, n + 1)
                    o = work.bank(m)
                    for k in range(i, -1, -1):
                        lhs = (upto if k == i else ones)[:]
                        nc.tensor.matmul(o[:, k * P:(k + 1) * P], lhs, rdiag[:, head * NT + k, :], start=(k == i), stop=(k < i),
                                         skip_group_check=True)
                        if k:
                            nc.tensor.matmul(o[:, 0:k * P], lhs, lf[:, k, head:head + 1].to_broadcast([P, k * P]),
                                             start=False, stop=False, skip_group_check=True)
                    nc.tensor.matmul(o[:, i * P:(i + 1) * P], ident_b[:], neg_after[:], start=False, stop=True,
                                     skip_group_check=True).then_inc(work.full[m % BANKS], 1)

                decay(0)
                for n in range(MLSTM_BLOCKS + 2):
                    if n + 1 < MLSTM_BLOCKS:
                        decay(n + 1)
                    if n < MLSTM_BLOCKS:
                        head, i = divmod(n, NT)
                        m = MW["scores", n]
                        work.wait_free(pe, m)
                        if n == 0:
                            for j in range(4):
                                stream.wait_done(pe, base["odd_in"][1] + 5 + j)
                        q = 64 * (head % 2)
                        nc.tensor.matmul(work.bank(m)[:, 0:(i + 1) * P], mq[q:q + 64, head // 2, i * P:(i + 1) * P],
                                         mk[q:q + 64, head // 2, 0:(i + 1) * P], start=True, stop=True).then_inc(
                            work.full[m % BANKS], 1)
                    if 1 <= n <= MLSTM_BLOCKS:
                        n1 = n - 1
                        head, i = divmod(n1, NT)
                        m = MW["turned", n1]
                        work.wait_free(pe, m)
                        work.wait_done(pe, MW["scores", n1])
                        for j in range(i + 1):
                            mm = nc.tensor.transpose(work.bank(m)[:, j * P:(j + 1) * P], dec[:, n1 % 3, j * P:(j + 1) * P], ident[:])
                        mm.then_inc(work.full[m % BANKS], 1)
                    if n >= 2:
                        n1 = n - 2
                        head, i = divmod(n1, NT)
                        m = MW["out", n1]
                        work.wait_free(pe, m)
                        work.wait_done(pe, MW["turned", n1])
                        if n1 == 0:
                            for j in range(NT):
                                stream.wait_done(pe, base["odd_in"][1] + 9 + j)
                        for j in range(i + 1):
                            mm = nc.tensor.matmul(work.bank(m)[:, 0:P], sT[:, n1 % 2, j * P:(j + 1) * P],
                                                  mv[:, j, head * P:(head + 1) * P], start=(j == 0), stop=(j == i))
                        mm.then_inc(work.full[m % BANKS], 1)

            def mla_up():
                u, g, _ = base["mla_up"]
                pe.wait_ge(lat_ready, 5)
                for n in range(4 * NT):
                    part, t = divmod(n, NT)
                    k0, k_tiles, w = ((0, 3, 384), (3, 2, 512))[part // 2]
                    if t == 0:
                        wait_unit(pe, u + part)
                    stream.wait_free(pe, g + n)
                    for k in range(k_tiles):
                        mm = product(stream.bank(g + n)[:, 0:w], lambda p: lat(k0 + k, p)[:, t * P:(t + 1) * P],
                                     lambda p: split_ring[:, (u + part) % SLOTS, p, k * w:(k + 1) * w], k == 0, k == k_tiles - 1)
                    mm.then_inc(stream.full[(g + n) % BANKS], 1)

            def mla():
                def turn(name, src, head):
                    m = AW[name, head]
                    work.wait_free(pe, m)
                    for t in range(NT):
                        mm = nc.tensor.transpose(work.bank(m)[0:96, t * P:(t + 1) * P], src[:, t, head * 96:head * 96 + 96], ident[:])
                    mm.then_inc(work.full[m % BANKS], 1)

                pe.wait_ge(qk_ready, 1)
                turn("q", q_t, 0)
                turn("k", k_t, 0)
                for n in range(MLA_BLOCKS + 2):
                    if n < MLA_BLOCKS:
                        head, i = divmod(n, NT)
                        m = AW["scores", n]
                        work.wait_free(pe, m)
                        if i == 0:
                            work.wait_done(pe, AW["q", head])
                            work.wait_done(pe, AW["k", head])
                        nc.tensor.matmul(work.bank(m)[:, 0:(i + 1) * P], qT[0:96, head % 2, i * P:(i + 1) * P],
                                         kT[0:96, head % 2, 0:(i + 1) * P], start=True, stop=True, skip_group_check=True)
                        nc.tensor.matmul(work.bank(m)[:, i * P:(i + 1) * P], ident_b[:], neg_after[:], start=False, stop=True,
                                         skip_group_check=True).then_inc(work.full[m % BANKS], 1)
                    if n >= 2:
                        head, i = divmod(n - 2, NT)
                        m = AW["turned", n - 2]
                        work.wait_free(pe, m)
                        pe.wait_ge(prob_ready, n - 1)
                        for j in range(i + 1):
                            mm = nc.tensor.transpose(work.bank(m)[:, j * P:(j + 1) * P], prob[:, (n - 2) % 3, j * P:(j + 1) * P], ident[:])
                        mm.then_inc(work.full[m % BANKS], 1)
                    if n > NT and n % NT == 1:
                        head = n // NT - 1
                        m = AW["out", head]
                        work.wait_free(pe, m)
                        work.wait_done(pe, AW["turned", n - 2])
                        q = 64 * (head % 2)
                        pt = (probT, probT2)[head % 2]
                        for j in range(NT):
                            mm = nc.tensor.matmul(work.bank(m)[q:q + 64, j * P:T], v_m[:, j, head * 64:head * 64 + 64],
                                                  pt[:, j, j * P:T], start=(j == 0), stop=True, skip_group_check=True)
                        mm.then_inc(work.full[m % BANKS], 1)
                    if n % NT == 1 and n // NT + 1 < MLA_HEADS:
                        turn("q", q_t, n // NT + 1)
                        turn("k", k_t, n // NT + 1)
                    if n == HV_BLOCK:
                        for head in range(MLSTM_HEADS):
                            m = AW["y", head]
                            work.wait_free(pe, m)
                            pe.wait_ge(hv_ready, NT)
                            for t in range(NT):
                                mm = nc.tensor.transpose(work.bank(m)[:, t * P:(t + 1) * P], hv[:, t, head * P:(head + 1) * P], ident[:])
                            mm.then_inc(work.full[m % BANKS], 1)

            def odd_out():
                u, g, _ = base["odd_out"]
                for head in range(MLSTM_HEADS):
                    work.wait_done(pe, AW["y", head])
                for head in range(MLA_HEADS):
                    work.wait_done(pe, AW["out", head])
                simple_outs(u, g, 8, y_in, None)

            def gla_in():
                u, g, m = base["gla_in"]
                simple_outs(u, g, 3, hn_in, hn_wait("norm_mix2"))
                stream.wait_done(pe, g)
                for c in range(2):
                    work.wait_free(pe, m + c)
                    nc.tensor.matmul(work.bank(m + c)[:], w_gate_up[:, c * P:(c + 1) * P], g_low, start=True,
                                     stop=True).then_inc(work.full[(m + c) % BANKS], 1)
                simple_outs(u + 3, g + 3, 2, hn_in, None)
                token_outs(u + 5, g + 5, hn_in, 2)
                token_outs(u + 9, g + 9, hn_in, 2)

            def gla():
                g = base["gla_in"][1] + 1
                for n in range(4):
                    stream.wait_done(pe, g + n)
                for n in range(LEVELS):
                    if n:
                        pe.wait_ge(pair_ready, n)
                    for q in range(NT):
                        m, r = GW["level", n, q], 64 * (q % 2)
                        work.wait_free(pe, m)
                        for o in range(4):
                            i, c = 2 * (q // 2) + o // 2, o % 2
                            cut = (slice(r, r + 64), c, slice(i * P, (i + 1) * P))
                            lhs, rhs = (pair[cut[0], n % 2, c, cut[2]],) * 2 if n else (gk[cut], gq[cut])
                            mm = nc.tensor.matmul(work.bank(m)[:, o * P:(o + 1) * P], lhs, rhs, start=True, stop=True)
                        mm.then_inc(work.full[m % BANKS], 1)
                    if n in (3, 5):
                        swa_in((n - 3) // 2)
                swa_in(2)
                swa_in(3)
                pe.wait_ge(far_ready, 1)
                for head in range(GLA_HEADS):
                    r, c = 64 * (head % 2), head // 2
                    k = lambda n: kd[r:r + 64, c, n * P:(n + 1) * P]
                    q = lambda n, w: qd[r:r + 64, c, n * P:(n + w) * P]
                    m = GW["far_a", head]
                    work.wait_free(pe, m)
                    for o, w, lhs, rhs in ((0, 1, k(0), q(0, 1)), (1, 2, k(3), q(2, 2)), (3, 1, k(2), q(1, 1))):
                        mm = nc.tensor.matmul(work.bank(m)[:, o * P:(o + w) * P], lhs, rhs, start=True, stop=True)
                    mm.then_inc(work.full[m % BANKS], 1)
                    m = GW["far_b", head]
                    work.wait_free(pe, m)
                    nc.tensor.matmul(work.bank(m)[:, 0:2 * P], k(1), q(2, 2), start=True, stop=True).then_inc(work.full[m % BANKS], 1)
                for n in range(4, 8):
                    stream.wait_done(pe, g + n)
                where = {(0, 1): 0, (0, 2): 1, (0, 3): 2, (2, 3): 3, (1, 2): 4, (1, 3): 5}
                pe.wait_ge(near_ready, NT)
                for head in range(GLA_HEADS):
                    work.wait_done(pe, GW["far_b", head])
                    work.wait_done(pe, GW["far_a", head])
                for i in range(NT):
                    m = GW["o", i]
                    work.wait_free(pe, m)
                    for head in range(GLA_HEADS):
                        for j in range(i + 1):
                            w = near[:, i, head * P:(head + 1) * P] if j == i else far[:, head, where[j, i] * P:(where[j, i] + 1) * P]
                            mm = nc.tensor.matmul(work.bank(m)[:, head * P:(head + 1) * P], w, gv[:, j, head * P:(head + 1) * P],
                                                  start=(j == 0), stop=(j == i))
                    mm.then_inc(work.full[m % BANKS], 1)
                swa_in(4)
                swa_in(5)
                pe.wait_ge(go_ready, NT)
                for head in range(GLA_HEADS):
                    m = GW["y", head]
                    work.wait_free(pe, m)
                    for t in range(NT):
                        mm = nc.tensor.transpose(work.bank(m)[:, t * P:(t + 1) * P], go[:, t, head * P:(head + 1) * P], ident[:])
                    mm.then_inc(work.full[m % BANKS], 1)

            def swa_in(n):
                u, g, _ = base["swa"]
                if n < 5:
                    simple_outs(u + n, g + n, 1, hn_in, None)
                    return
                stream.wait_free(pe, g + 5)
                wait_unit(pe, u + 5)
                for t in range(NT):
                    for k in range(DC):
                        mm = product(stream.bank(g + 5)[:, t * P:(t + 1) * P], lambda p: hn[:, p, k, t * P:(t + 1) * P],
                                     lambda p: split_ring[:, (u + 5) % SLOTS, p, k * P:(k + 1) * P], k == 0, k == DC - 1)
                mm.then_inc(stream.full[(g + 5) % BANKS], 1)

            def swa():
                g = base["swa"][1]
                for n in range(6):
                    stream.wait_done(pe, g + n)
                for n in range(SWA_BLOCKS + 2):
                    if n % 4 == 1 and n < SWA_BLOCKS:
                        simple_outs(base["pool"][0] + n // 4, base["pool"][1] + n // 4, 1, hn_in, None)
                    if n < SWA_BLOCKS:
                        m, r = SW["scores", n], 64 * (n % 2)
                        work.wait_free(pe, m)
                        for s in range(2):
                            i, at = 2 * (n // 2 % 2) + s, 256 * s
                            w = 256 if i else P
                            if i == 0:
                                nc.tensor.matmul(work.bank(m)[:, 0:P], ident_b[:], neg_until[:, 0:1].to_broadcast([P, P]),
                                                 start=True, stop=True, skip_group_check=True)
                            nc.tensor.matmul(work.bank(m)[:, at + 256 - w:at + 256], sqT[r:r + 64, n // 4, i * P:(i + 1) * P],
                                             skT[r:r + 64, 0, (i + 1) * P - w:(i + 1) * P], start=True, stop=True, skip_group_check=True)
                            if i:
                                nc.tensor.matmul(work.bank(m)[:, at:at + P], ident_b[:], neg_until[:], start=False, stop=True,
                                                 skip_group_check=True)
                            mm = nc.tensor.matmul(work.bank(m)[:, at + P:at + 2 * P], ident_b[:], neg_after[:], start=False,
                                                  stop=True, skip_group_check=True)
                        mm.then_inc(work.full[m % BANKS], 1)
                    if n >= 2:
                        m = SW["turned", n - 2]
                        work.wait_free(pe, m)
                        pe.wait_ge(sprob_ready, n - 1)
                        for o in range(4):
                            mm = nc.tensor.transpose(work.bank(m)[:, o * P:(o + 1) * P], sprob[:, (n - 2) % 3, o * P:(o + 1) * P],
                                                     ident[:])
                        mm.then_inc(work.full[m % BANKS], 1)
                    if n > NT and n % NT == 1:
                        j = n // NT - 1
                        m = SW["out", j]
                        work.wait_free(pe, m)
                        work.wait_done(pe, SW["turned", n - 2])
                        for i in range(NT):
                            for e in range(2):
                                for b in range(0 if i else 1, 2):
                                    mm = nc.tensor.matmul(work.bank(m)[64 * e:64 * e + 64, i * P:(i + 1) * P],
                                                          sv[:, i - 1 + b, 64 * e:64 * e + 64],
                                                          sprobT[:, i, (2 * e + b) * P:(2 * e + b + 1) * P],
                                                          start=(b == 1 or i > 0) and (b == 0 or i == 0), stop=(b == 1))
                        mm.then_inc(work.full[m % BANKS], 1)

            def pool():
                u, g, _ = base["pool"]
                wait_unit(pe, u + 4)
                for c in range(4):
                    stream.wait_free(pe, g + 4 + c)
                    pe.wait_ge(pd_ready, c + 1)
                    product(stream.bank(g + 4 + c)[:], lambda p: split_ring[:, (u + 4) % SLOTS, p, c * P:(c + 1) * P],
                            lambda p: pd[:, p, c, :], True, True).then_inc(stream.full[(g + 4 + c) % BANKS], 1)

            def merge():
                u, g, _ = base["merge"]
                for n in range(3 * DC):
                    b = n % 3
                    stream.wait_free(pe, g + 2 * n)
                    feature_out(u + n, g + 2 * n, hn_in, DC).then_inc(stream.full[(g + 2 * n) % BANKS], 1)
                    stream.wait_free(pe, g + 2 * n + 1)
                    if n < 3:
                        for c in range(4):
                            if n == 2:
                                pe.wait_ge(branch_ready, c + 1)
                            else:
                                work.wait_done(pe, (SW["out", c] if n else GW["y", c]))
                    for k in range(4):
                        mm = product(stream.bank(g + 2 * n + 1)[:], lambda p: split_ring[:, (u + n) % SLOTS, p, (8 + k) * P:(9 + k) * P],
                                     lambda p: branch[b][:, p, k, :], k == 0, k == 3)
                    mm.then_inc(stream.full[(g + 2 * n + 1) % BANKS], 1)

            def block_out():
                u, g, _ = base["block_out"]
                simple_outs(u, g, 8, lambda k, p: merged[:, p, k, :], lambda k: pe.wait_ge(y_ready, DC + k + 1))

            pe.wait_ge(consts_ready, 3)
            norm("norm_mix0")
            even_in()
            u, g, _ = base["even_out"]
            simple_outs(u, g, 8, y_in, lambda k: pe.wait_ge(y_ready, k + 1))
            norm("norm_ffn0")
            ffn("ffn0", "norm_ffn0")
            norm("norm_ple0")
            ple("ple0", "norm_ple0", 0)
            norm("norm_mix1")
            odd_in()
            mla_up()
            mlstm()
            mla()
            odd_out()
            norm("norm_ffn1")
            ffn("ffn1", "norm_ffn1")
            norm("norm_ple1")
            ple("ple1", "norm_ple1", 1)
            norm("norm_mix2")
            gla_in()
            gla()
            swa()
            pool()
            merge()
            block_out()
            norm("norm_post")
            norm("norm_ffn2")
            ffn("convffn", "norm_ffn2")
            norm("norm_last")

        @block.scalar
        def _(scalar):
            steps = Steps(scalar, act_steps)
            calls = [0]

            def rsqrt_guess(n):
                calls[0] += 1
                scalar.wait_ge(ms_ready, calls[0])
                steps.did(nc.scalar.activation(ln_ms[:, 0:n], ms[:, 0:n], ACT.Ln))
                steps.settle()
                nc.scalar.activation(rs0[:, 0:n], ln_ms[:, 0:n], ACT.Exp, scale=-0.5).then_inc(rs_guessed, 1)

            def norm(stage, src=None, ready=None):
                m = base[stage][2]
                scalar.preload_act_table_set(LNEXP)
                post = stage in ("norm_post", "norm_last")
                for c in range(DC):
                    if post:
                        n = h_out(BEFORE[stage], c)
                        stream.wait_full(scalar, n)
                        nc.scalar.activation(o_buf[:, c, :], stream.bank(n)[:], ACT.Copy).then_inc(stream.done[n % BANKS], 1)
                for c in range(DC):
                    h_ready(scalar, stage, c)
                    nc.scalar.activation(squares_of(stage)[:, c, :], (o_buf if post else h)[:, c, :],
                                         ACT.Square).then_inc(sq_ready, 1)
                if stage.startswith("norm_ple"):
                    scalar.dma_start(p_raw, a["p" + stage[-1]]).then_inc(p_loaded, 16)
                if stage == "norm_mix0":
                    for to, name in ((w_small[:], "w_small"), (w_gate_up[:], "w_gate_up"), (pos_i[:], "positions"), (ws, "w_s"),
                                     (b_row, "b_s")):
                        scalar.dma_start(to, a[name]).then_inc(tables_loaded, 16)
                    scalar.dma_start(rows[:], a["rows"].partition_broadcast(P)).then_inc(tables_loaded, 16)
                rsqrt_guess(NT)
                if not post:
                    k = DC * hn_no[stage]
                    for c in range(DC):
                        scalar.wait_ge(v_made, k + c + 1)
                        nc.scalar.activation(hn[:, 0, c, :], tmp[:, c % 4, :], ACT.Copy).then_inc(hi_made, 1)

            def even_in():
                u, g, m = base["even_in"]
                for j in range(4):
                    n = g + 3 * j
                    stream.wait_full(scalar, n)
                    if j >= 2:
                        stream.wait_done(scalar, n - 5)
                    nc.scalar.activation(tmp[:, j % 2, :], stream.bank(n)[:], ACT.Copy).then_inc(stream.done[n % BANKS], 1)
                for j in range(4):
                    n = g + 12 + j
                    stream.wait_full(scalar, n)
                    nc.scalar.activation(u_g[:, j, :], stream.bank(n)[:], ACT.Gelu_apprx_tanh).then_inc(stream.done[n % BANKS], 1)
                for t in range(NT):
                    n = g + 16 + t
                    stream.wait_full(scalar, n)
                    nc.scalar.activation(v_t[:, t, :], stream.bank(n)[:], ACT.Gelu_apprx_tanh).then_inc(stream.done[n % BANKS], 1)
                for t in range(NT):
                    stream.wait_done(scalar, g + 16 + t)
                    if t >= 2:
                        scalar.wait_ge(v_square, t - 1)
                    nc.scalar.activation(v_sq[:, t % 2, :], v_t[:, t, :], ACT.Square).then_inc(v_gelu, 1)
                scalar.preload_act_table_set(LNEXP)
                rsqrt_guess(32)

            def ffn(stage):
                g = base[stage][1]
                scalar.preload_act_table_set("silu_and_others")
                if stage == "ffn0":
                    scalar.wait_ge(angle_ready, 1)
                    nc.scalar.activation(cos_sin[:], angle[:, 3:5, :], ACT.Sin).then_inc(turned_ready, 1)
                with scalar.Fori(0, 2 * FC // 4) as i:
                    for j in (0, 2):
                        scalar.wait_ge(stream.full[(g + j) % BANKS], i + (g + j) // BANKS + 1)
                        scalar.wait_ge(stream.done[(g + j + 1) % BANKS], i + (g + j + 1) // BANKS)
                        nc.scalar.activation(tmp[:, j // 2, :], stream.bank(g + j)[:], ACT.Silu).then_inc(
                            stream.done[(g + j) % BANKS], 1)

            def ple(stage):
                g = base[stage][1]
                for c in range(DC):
                    n = g + 2 * c
                    stream.wait_full(scalar, n)
                    if c >= 2:
                        stream.wait_done(scalar, n - 3)
                    nc.scalar.activation(tmp[:, c % 2, :], stream.bank(n)[:], ACT.Sigmoid).then_inc(stream.done[n % BANKS], 1)

            def odd_in():
                g, m = base["odd_in"][1:]
                for c in range(5):
                    stream.wait_full(scalar, g + c)
                    nc.scalar.activation(lat_sq[:, c, :], stream.bank(g + c)[:], ACT.Square).then_inc(lat_squared, 1)
                for c in range(2):
                    n = g + 5 + c
                    stream.wait_full(scalar, n)
                    nc.scalar.activation(mq[:, c, :], stream.bank(n)[:], ACT.Copy, scale=64 ** -0.5).then_inc(stream.done[n % BANKS], 1)
                for c in range(2):
                    n = g + 7 + c
                    stream.wait_full(scalar, n)
                    nc.scalar.activation(mk[:, c, :], stream.bank(n)[:], ACT.Copy).then_inc(stream.done[n % BANKS], 1)
                for t in range(NT):
                    n = g + 9 + t
                    stream.wait_full(scalar, n)
                    nc.scalar.activation(mv[:, t, :], stream.bank(n)[:], ACT.Copy).then_inc(stream.done[n % BANKS], 1)
                rsqrt_guess(8)
                for t in range(NT):
                    n = g + 13 + t
                    stream.wait_full(scalar, n)
                    nc.scalar.activation(mo[:, t, :], stream.bank(n)[:], ACT.Sigmoid).then_inc(stream.done[n % BANKS], 1)

            def mlstm():
                scalar.preload_act_table_set(LNEXP)
                scalar.wait_ge(gates_ready, 1)
                steps.did(nc.scalar.activation(gl[:, 0, :], gl[:, 3, :], ACT.Abs))
                steps.settle()
                steps.did(nc.scalar.activation(gl[:, 1, :], gl[:, 0, :], ACT.Exp, scale=-1.0))
                steps.settle()
                nc.scalar.activation(gl[:, 2, :], gl[:, 1, :], ACT.Ln, bias=1.0).then_inc(log_ready, 1)
                mla_up()
                for n in range(MLSTM_BLOCKS + 3):
                    if n < MLSTM_BLOCKS:
                        head, i = divmod(n, NT)
                        m = MW["decay", n]
                        scalar.wait_ge(m_ready, n + 1)
                        nc.scalar.activation(exp_m[:, n:n + 1], neg_m[:, n:n + 1], ACT.Exp).then_inc(exp_m_ready, 1)
                        if n >= 3:
                            work.wait_full(scalar, MW["turned", n - 3])
                        nc.scalar.activation(dec[:, n % 3, 0:(i + 1) * P], work.bank(m)[:, 0:(i + 1) * P], ACT.Exp,
                                             bias=neg_m[:, n:n + 1]).then_inc(work.done[m % BANKS], 1)
                        if n < 4:
                            qk_square(n)
                        if n in (5, 11):
                            rsqrt_guess(64 if n == 5 else 36)
                        if 6 <= n < 10:
                            qk_square(n - 2)
                    if 2 <= n <= MLSTM_BLOCKS + 1:
                        head, i = divmod(n - 2, NT)
                        m = MW["turned", n - 2]
                        work.wait_full(scalar, m)
                        nc.scalar.activation(sT[:, n % 2, 0:(i + 1) * P], work.bank(m)[:, 0:(i + 1) * P],
                                             ACT.Copy).then_inc(work.done[m % BANKS], 1)
                    if n >= 3:
                        head, i = divmod(n - 3, NT)
                        m = MW["out", n - 3]
                        work.wait_full(scalar, m)
                        scalar.wait_ge(rden_ready, n - 2)
                        nc.scalar.activation(hv[:, i, head * P:(head + 1) * P], work.bank(m)[:, 0:P], ACT.Copy,
                                             scale=rden[:, n - 3:n - 2]).then_inc(work.done[m % BANKS], 1)

            def mla_up():
                g = base["mla_up"][1]
                scalar.wait_ge(lat_rs_ready, 1)
                heads = lambda v: v.rearrange("p (a b) -> p a b", a=4)
                for n in range(16):
                    kv, (half, t) = n // 8, divmod(n % 8, 4)
                    stream.wait_full(scalar, g + n)
                    o, rs = stream.bank(g + n), lat_rs[:, NT * kv + t:NT * kv + t + 1]
                    if kv:
                        nc.scalar.activation(heads(k_t[:, t, half * 384:half * 384 + 384])[:, :, 0:64], heads(o[:])[:, :, 0:64],
                                             ACT.Copy, scale=rs)
                        x = nc.scalar.activation(heads(v_m[:, t, half * 256:half * 256 + 256]), heads(o[:])[:, :, 64:128],
                                                 ACT.Copy, scale=rs)
                    else:
                        x = nc.scalar.activation(q_t[:, t, half * 384:half * 384 + 384], o[:, 0:384], ACT.Copy, scale=rs)
                    x.then_inc(stream.done[(g + n) % BANKS], 1)

            def qk_square(n):
                g = base["mla_up"][1]
                t, kv = n % 4, n // 4
                stream.wait_done(scalar, g + 8 * kv + 4 + t)
                stream.wait_done(scalar, g + 8 * kv + t)
                if n >= 2:
                    scalar.wait_ge(summed, n - 1)
                if kv:
                    x = nc.scalar.activation(qk_sq[:, n % 2, 0:512].rearrange("p (a b) -> p a b", a=8),
                                             k_t[:, t, :].rearrange("p (a b) -> p a b", a=8)[:, :, 0:64], ACT.Square)
                else:
                    x = nc.scalar.activation(qk_sq[:, n % 2, 0:768], q_t[:, t, :], ACT.Square)
                x.then_inc(squared, 1)

            def mla():
                for n in range(MLA_BLOCKS + 2):
                    if n < MLA_BLOCKS:
                        head, i = divmod(n, NT)
                        m = AW["scores", n]
                        scalar.wait_ge(m_ready, MLSTM_BLOCKS + n + 1)
                        if n >= 3:
                            work.wait_full(scalar, AW["turned", n - 3])
                        nc.scalar.activation(prob[:, n % 3, 0:(i + 1) * P], work.bank(m)[:, 0:(i + 1) * P], ACT.Exp,
                                             bias=neg_m[:, n:n + 1], accum_out=den[:, n:n + 1]).then_inc(work.done[m % BANKS], 1)
                        if n == 0:
                            work.wait_done(scalar, MW["out", MLSTM_BLOCKS - 1])
                        if n < NT:
                            nc.scalar.activation(hv_sq[:, n, :], hv[:, n, :], ACT.Square).then_inc(hv_squared, 1)
                        if n == NT + 1:
                            rsqrt_guess(16)
                    if n >= 2:
                        head, i = divmod(n - 2, NT)
                        m = AW["turned", n - 2]
                        work.wait_full(scalar, m)
                        if i == 0 and head >= 2:
                            work.wait_full(scalar, AW["out", head - 2])
                        nc.scalar.activation((probT, probT2)[head % 2][:, 0:i + 1, i * P:(i + 1) * P],
                                             work.bank(m)[:, 0:(i + 1) * P].rearrange("p (a b) -> p a b", b=P),
                                             ACT.Copy).then_inc(work.done[m % BANKS], 1)

            def gla_in():
                g, m = base["gla_in"][1:]

                def copy(dst, n, scale=1.0, func=ACT.Copy):
                    stream.wait_full(scalar, n)
                    nc.scalar.activation(dst, stream.bank(n)[:], func, scale=scale).then_inc(stream.done[n % BANKS], 1)

                stream.wait_full(scalar, g)
                nc.scalar.activation(g_low, stream.bank(g)[0:16, :], ACT.Copy).then_inc(stream.done[g % BANKS], 1)
                g = g + 1
                for c in range(2):
                    copy(gq[:, c, :], g + c, 64 ** -0.5)
                for c in range(2):
                    work.wait_full(scalar, m + c)
                    nc.scalar.activation(logit[:, c, :], work.bank(m + c)[:], ACT.Identity, bias=col("gla_b", c)).then_inc(
                        work.done[(m + c) % BANKS], 1)
                for c in range(2):
                    work.wait_done(scalar, m + c)
                steps.did(nc.scalar.activation(log_p, logit, ACT.Abs))
                steps.settle()
                steps.did(nc.scalar.activation(log_p, log_p, ACT.Exp, scale=-1.0))
                steps.settle()
                nc.scalar.activation(log_p, log_p, ACT.Ln, bias=1.0).then_inc(logit_logged, 1)
                for c in range(2):
                    copy(gk[:, c, :], g + 2 + c)
                decays(1)
                for t in range(NT):
                    copy(gv[:, t, :], g + 4 + t)
                decays(2)
                scalar.preload_act_table_set("silu_and_others")
                for t in range(NT):
                    copy(gr[:, t, :], g + 8 + t, func=ACT.Silu)

            def decays(n):
                scalar.wait_ge(exponent_ready, n)
                nc.scalar.activation(pair[:, n % 2], pair[:, n % 2], ACT.Exp, scale=1.0 / 16).then_inc(decay_ready, 1)

            def swa_in(c):
                g = base["swa"][1]
                dst = (sqT[:, c, :] if c < 4 else skT[:, 0, :] if c == 4 else sv.rearrange("p a b -> p (a b)"))
                stream.wait_full(scalar, g + c)
                nc.scalar.activation(dst, stream.bank(g + c)[:], ACT.Copy, scale=64 ** -0.5 if c < 4 else 1.0).then_inc(
                    stream.done[(g + c) % BANKS], 1)

            def gla():
                scalar.preload_act_table_set(LNEXP)
                for n in range(3, LEVELS):
                    decays(n)
                    if n in (5, 7):
                        swa_in((n - 5) // 2)
                scalar.wait_ge(exponent_ready, LEVELS)
                for c in range(2):
                    for i in range(NT - 1):
                        nc.scalar.activation(kd[:, c, i * P:(i + 1) * P], cum[:, c, i * P:(i + 1) * P], ACT.Exp, scale=-1.0 / 16,
                                             bias=tot16[:, c, i:i + 1])
                    for slot, i in enumerate((1, 3, 2)):
                        nc.scalar.activation(qd[:, c, slot * P:(slot + 1) * P], cum[:, c, i * P:(i + 1) * P], ACT.Exp, scale=1.0 / 16)
                nc.scalar.activation(exp_tot[:], tot16[:], ACT.Exp).then_inc(far_exp, 1)
                swa_in(2)
                swa_in(3)
                for head in range(GLA_HEADS):
                    for part, lo, w in (("far_a", 0, 512), ("far_b", 512, 256)):
                        m = GW[part, head]
                        work.wait_full(scalar, m)
                        nc.scalar.activation(far[:, head, lo:lo + w], work.bank(m)[:, 0:w], ACT.Copy).then_inc(work.done[m % BANKS], 1)
                for i in range(NT):
                    m = GW["o", i]
                    work.wait_full(scalar, m)
                    nc.scalar.activation(go[:, i, :], work.bank(m)[:], ACT.Copy).then_inc(work.done[m % BANKS], 1)
                for i in range(NT):
                    work.wait_done(scalar, GW["o", i])
                    nc.scalar.activation(go_sq[:, i, :], go[:, i, :], ACT.Square).then_inc(go_squared, 1)
                rsqrt_guess(16)
                swa_in(4)
                swa_in(5)

            def swa():
                for n in range(SWA_BLOCKS + 2):
                    if n % 4 == 2:
                        c = n // 4
                        scalar.wait_ge(pad_ready, 1)
                        g = base["pool"][1]
                        stream.wait_full(scalar, g + c)
                        nc.scalar.activation(pu[:, c, 16:16 + T], stream.bank(g + c)[:], ACT.Copy).then_inc(
                            stream.done[(g + c) % BANKS], 1)
                    if n < SWA_BLOCKS:
                        m = SW["scores", n]
                        scalar.wait_ge(m_ready, MLSTM_BLOCKS + MLA_BLOCKS + n + 1)
                        scalar.wait_ge(sink_ready, n + 2)
                        if n >= 3:
                            work.wait_full(scalar, SW["turned", n - 3])
                        nc.scalar.activation(sink_m[:, 2 * n:2 * n + 2], sink_m[:, 2 * n:2 * n + 2], ACT.Exp)
                        for s in range(2):
                            x = nc.scalar.activation(sprob[:, n % 3, 256 * s:256 * s + 256], work.bank(m)[:, 256 * s:256 * s + 256],
                                                     ACT.Exp, bias=neg_m[:, 2 * n + s:2 * n + s + 1],
                                                     accum_out=den[:, 2 * n + s:2 * n + s + 1])
                        x.then_inc(work.done[m % BANKS], 1)
                    if n >= 2:
                        j, b = divmod(n - 2, 4)
                        m = SW["turned", n - 2]
                        work.wait_full(scalar, m)
                        if j and b == 0:
                            work.wait_full(scalar, SW["out", j - 1])
                        i, e = 2 * (b // 2), b % 2
                        nc.scalar.activation(sprobT[:, i:i + 2, 256 * e:256 * e + 256],
                                             work.bank(m)[:].rearrange("p (a b) -> p a b", a=2), ACT.Copy).then_inc(work.done[m % BANKS], 1)


            def merge():
                g = base["merge"][1]
                for n in range(3 * DC):
                    o = g + 2 * n
                    stream.wait_full(scalar, o)
                    if n == 0:
                        scalar.wait_ge(branch_ready, 4)
                    if n >= 2:
                        stream.wait_done(scalar, o - 3)
                    nc.scalar.activation(tmp[:, n % 2, :], stream.bank(o)[:], ACT.Sigmoid).then_inc(stream.done[o % BANKS], 1)

            def convffn():
                g = base["convffn"][1]
                scalar.preload_act_table_set("gelu_apprx_tanh_and_others")

                def body(i, first):
                    for j in range(4):
                        b, gate = j // 2, j % 2 == 0
                        c = 2 * i + b + (0 if gate else FC)
                        scalar.wait_ge(stream.full[(g + j) % BANKS], i + (g + j) // BANKS + 1)
                        if not first:
                            scalar.wait_ge(act_ready, FC * FFN_NO["convffn"] + 2 * (i - 1) + b + 1)
                        nc.scalar.activation(tmp[:, j, :].unsqueeze(1), stream.bank(g + j)[:].unsqueeze(1), ACT.Identity,
                                             scale=cols[:, bass.ds(c + COLS["cw2"], 1)],
                                             bias=cols[:, bass.ds(c + COLS["cb"], 1)]).then_inc(conv_started, 1)
                        if not gate:
                            scalar.wait_ge(stream.done[(g + j - 1) % BANKS], i + (g + j - 1) // BANKS + 1)
                            nc.scalar.activation(tmp[:, j - 1, :], tmp[:, j - 1, :], ACT.Gelu_apprx_tanh).then_inc(gelu_ready, 1)

                body(0, True)
                with scalar.Fori(1, 2 * FC // 4) as i:
                    body(i, False)

            scalar.dma_start(cols[:], a["cols"]).then_inc(cols_loaded, 16)
            norm("norm_mix0")
            even_in()
            norm("norm_ffn0")
            ffn("ffn0")
            norm("norm_ple0")
            ple("ple0")
            norm("norm_mix1")
            odd_in()
            mlstm()
            mla()
            norm("norm_ffn1")
            ffn("ffn1")
            norm("norm_ple1")
            ple("ple1")
            norm("norm_mix2")
            gla_in()
            gla()
            swa()
            merge()
            norm("norm_post")
            norm("norm_ffn2")
            convffn()
            norm("norm_last")

        @block.vector
        def _(dve):
            steps = Steps(dve, dve_steps)
            calls = [0]

            def rsqrt(n):
                calls[0] += 1
                dve.wait_ge(rs_guessed, calls[0])
                steps.did(nc.vector.tensor_tensor(rt[:, 0, 0:n], rs0[:, 0:n], rs0[:, 0:n], ALU.mult))
                steps.settle()
                steps.did(nc.vector.scalar_tensor_tensor(rt[:, 1, 0:n], rt[:, 0, 0:n], -0.5, ms[:, 0:n], ALU.mult, ALU.mult))
                steps.settle()
                nc.vector.scalar_tensor_tensor(rstd[:, 0:n], rt[:, 1, 0:n], 1.5, rs0[:, 0:n], ALU.add, ALU.mult).then_inc(rstd_ready, 1)

            def keep_halves(to, v):
                steps.did(nc.vector.tensor_copy(to[0], v))
                steps.settle()
                return nc.vector.tensor_tensor(to[1], v, to[0].bitcast(F32), ALU.subtract)

            def norm(stage, gain):
                m, k = base[stage][2], norm_no[stage]
                work.wait_full(dve, m)
                nc.vector.tensor_copy(stat[:, 0:NT], work.bank(m)[:, 0:NT]).then_inc(work.done[m % BANKS], 1)
                work.wait_done(dve, m)
                nc.vector.tensor_scalar(ms[:, 0:NT], stat[:, 0:NT], 1.0 / D, EPS, ALU.mult, ALU.add).then_inc(ms_ready, 1)
                rsqrt(NT)
                work.wait_full(dve, m + 1)
                rstd_rows = work.bank(m + 1)
                if k == 0:
                    dve.wait_ge(cols_loaded, 16)
                if stage in ("norm_post", "norm_last"):
                    for c in range(DC):
                        x = nc.vector.scalar_tensor_tensor(tmp[:, c % 4, :], o_buf[:, c, :], col(gain, c), rstd_rows[:],
                                                           ALU.mult, ALU.mult)
                        if c < DC - 1:
                            steps.did(x)
                            steps.settle()
                        else:
                            x.then_inc(work.done[(m + 1) % BANKS], 1)
                            work.wait_done(dve, m + 1)
                        nc.vector.tensor_tensor(h[:, c, :], h[:, c, :], tmp[:, c % 4, :], ALU.add).then_inc(h_updated, 1)
                    dve.wait_ge(h_updated, DC * (1 if stage == "norm_post" else 2))
                    return
                no = hn_no[stage]
                for c in range(DC + 1):
                    if c < DC:
                        if c >= 4:
                            wait_hn_chunk(dve, no, c - 4)
                        nc.vector.scalar_tensor_tensor(tmp[:, c % 4, :], h[:, c, :], col(gain, c), rstd_rows[:], ALU.mult,
                                                       ALU.mult).then_inc(v_made, 1)
                    if c == DC:
                        nc.vector.tensor_copy(stat[:, 0:1], rstd_rows[:, 0:1]).then_inc(work.done[(m + 1) % BANKS], 1)
                        work.wait_done(dve, m + 1)
                    if c % 2:
                        dve.wait_ge(hi_made, DC * no + c)
                        nc.vector.tensor_tensor(hn[:, 1, c - 1, :], tmp[:, (c - 1) % 4, :], hn[:, 0, c - 1, :].bitcast(F32),
                                                ALU.subtract).then_inc(hn_ready[0], 1)
                for c in (DC - 2, DC - 1):
                    wait_hn_chunk(dve, no, c)

            def even_in():
                u, g, m = base["even_in"]
                for e in range(2):
                    steps.did(nc.vector.memset(z_pad[:, e, 0:2], 0.0))
                for j in range(4):
                    n, z, cv = g + 3 * j, z_pad[:, j % 2, :], conv[:, j % 2, :]
                    stream.wait_full(dve, n + 1)
                    stream.wait_done(dve, n)
                    if j >= 2:
                        stream.wait_done(dve, n - 4)
                    steps.settle()
                    nc.vector.tensor_tensor(z[:, 2:2 + T], stream.bank(n + 1)[:], tmp[:, j % 2, :], ALU.mult).then_inc(
                        stream.done[(n + 1) % BANKS], 1)
                    stream.wait_done(dve, n + 1)
                    steps.settle()
                    steps.did(nc.vector.tensor_scalar(cv, z[:, 2:2 + T], col("w_conv", 8 + j), None, ALU.mult))
                    for w in (1, 0):
                        steps.settle()
                        steps.did(nc.vector.scalar_tensor_tensor(cv, z[:, w:w + T], col("w_conv", 4 * w + j), cv, ALU.mult, ALU.add))
                    stream.wait_full(dve, n + 2)
                    steps.settle()
                    v = tmp[:, 2 + j % 2, :]
                    nc.vector.tensor_tensor(v, stream.bank(n + 2)[:], cv, ALU.mult).then_inc(stream.done[(n + 2) % BANKS], 1)
                    stream.wait_done(dve, n + 2)
                    keep_halves((y[:, 0, j, :], y[:, 1, j, :]), v).then_inc(y_ready, 1)
                    dve.wait_ge(y_ready, j + 1)
                dve.wait_ge(tables_loaded, 16 * N_TABLES)
                for t in range(NT):
                    dve.wait_ge(v_gelu, t + 1)
                    nc.vector.tensor_reduce(stat[:, 16 + 8 * t:24 + 8 * t], v_sq[:, t % 2, :].rearrange("p (a b) -> p a b", a=8),
                                            AX_X, ALU.add).then_inc(v_square, 1)
                dve.wait_ge(v_square, NT)
                nc.vector.tensor_scalar(ms[:, 0:32], stat[:, 16:48], 1.0 / 64, EPS, ALU.mult, ALU.add).then_inc(ms_ready, 1)
                rsqrt(32)
                dve.wait_ge(rstd_ready, calls[0])
                for t in range(NT):
                    vt = v_t[:, t, :].rearrange("p (a b) -> p a b", a=8)
                    steps.did(nc.vector.tensor_tensor(vt, vt, rstd[:, 8 * t:8 * t + 8].unsqueeze(2).to_broadcast([P, 8, 64]), ALU.mult))
                    steps.settle()
                    nc.vector.tensor_tensor(v_t[:, t, :], v_t[:, t, :], row("g_v", 0, 512), ALU.mult).then_inc(v_ready, 1)
                for hp in range(4):
                    work.wait_full(dve, m + hp)
                    stream.wait_done(dve, g + 12 + hp)
                    v = tmp[:, 2 + hp % 2, :]
                    nc.vector.tensor_tensor(v, work.bank(m + hp)[:], u_g[:, hp, :], ALU.mult).then_inc(work.done[(m + hp) % BANKS], 1)
                    work.wait_done(dve, m + hp)
                    keep_halves((y[:, 0, 4 + hp, :], y[:, 1, 4 + hp, :]), v).then_inc(y_ready, 1)
                    dve.wait_ge(y_ready, 5 + hp)

            def add_outs(g, n):
                for c in range(n):
                    stream.wait_full(dve, g + c)
                    nc.vector.tensor_tensor(h[:, c, :], stream.bank(g + c)[:], h[:, c, :], ALU.add).then_inc(
                        stream.done[(g + c) % BANKS], 1)

            def ffn(stage):
                g = base[stage][1]
                with dve.Fori(0, 2 * FC // 4) as i:
                    for j in (1, 3):
                        dve.wait_ge(stream.full[(g + j) % BANKS], i + (g + j) // BANKS + 1)
                        dve.wait_ge(stream.done[(g + j - 1) % BANKS], i + (g + j - 1) // BANKS + 1)
                        v = tmp[:, 2 + j // 2, :]
                        nc.vector.tensor_tensor(v, stream.bank(g + j)[:], tmp[:, j // 2, :], ALU.mult).then_inc(
                            stream.done[(g + j) % BANKS], 1)
                        dve.wait_ge(stream.done[(g + j) % BANKS], i + (g + j) // BANKS + 1)
                        act_halves(stage, v, i, j // 2)
                steps.n += FC
                add_outs(g + 2 * FC, DC)

            def act_halves(stage, v, i, b):
                hi, lo = (act[:, p, bass.ds(2 * i + b, 1), :] for p in range(2))
                nc.vector.tensor_copy(hi, v.unsqueeze(1)).then_inc(dve_steps, 1)
                dve.wait_ge(dve_steps, steps.n + 2 * i + b + 1)
                nc.vector.tensor_tensor(lo, v.unsqueeze(1), hi.bitcast(F32), ALU.subtract).then_inc(act_ready, 1)
                dve.wait_ge(act_ready, FC * FFN_NO[stage] + 2 * i + b + 1)

            def ple(stage):
                g = base[stage][1]
                dve.wait_ge(p_loaded, 16 * (1 + int(stage[-1])))
                keep_halves((p_in[:, 0], p_in[:, 1]), p_raw).then_inc(p_split, 1)
                for c in range(DC):
                    n = g + 2 * c + 1
                    stream.wait_full(dve, n)
                    stream.wait_done(dve, n - 1)
                    if c >= 2:
                        stream.wait_done(dve, n - 4)
                    steps.did(nc.vector.tensor_tensor(tmp[:, 2 + c % 2, :], stream.bank(n)[:], tmp[:, c % 2, :], ALU.mult))
                    steps.settle()
                    nc.vector.tensor_tensor(h[:, c, :], tmp[:, 2 + c % 2, :], h[:, c, :], ALU.add).then_inc(
                        stream.done[n % BANKS], 1)

            def rope_angles():
                dve.wait_ge(tables_loaded, 16 * N_TABLES)
                dve.wait_ge(freq_ready, 1)
                ang, turns, off = angle[:, 0, :], angle[:, 1, :], angle[:, 2, :]
                a3 = ang.rearrange("p (a b) -> p a b", a=NT)
                steps.did(nc.vector.tensor_copy(stat[:, 60:64], pos_i[:]))
                steps.settle()
                steps.did(nc.vector.tensor_copy(a3, inv_freq[:].unsqueeze(1).to_broadcast([P, NT, 16])))
                steps.settle()
                steps.did(nc.vector.tensor_tensor(a3, a3, stat[:, 60:64].unsqueeze(2).to_broadcast([P, NT, 16]), ALU.mult))
                for j, (quarter, shift) in enumerate(((0.25, PI / 2), (0.0, 0.0))):
                    r = angle[:, 3 + j, :]
                    steps.settle()
                    steps.did(nc.vector.tensor_scalar(off, ang, 1.0 / TWO_PI, quarter, ALU.mult, ALU.add))
                    steps.settle()
                    steps.did(nc.vector.tensor_scalar(turns, off, ROUND, ROUND, ALU.add, ALU.subtract))
                    steps.settle()
                    steps.did(nc.vector.tensor_copy(r, ang))
                    for part in TURN_PARTS:
                        steps.settle()
                        steps.did(nc.vector.scalar_tensor_tensor(r, turns, -part, r, ALU.mult, ALU.add))
                    steps.settle()
                    steps.did(nc.vector.tensor_scalar(r, r, shift, 3.1415925, ALU.add, ALU.min))
                    steps.settle()
                    if j == 0:
                        steps.did(nc.vector.tensor_scalar(r, r, -3.1415925, None, ALU.max))
                    else:
                        nc.vector.tensor_scalar(r, r, -3.1415925, None, ALU.max).then_inc(angle_ready, 1)

            def odd_in():
                g, m = base["odd_in"][1:]
                for c in range(5):
                    stream.wait_full(dve, g + c)
                    dve.wait_ge(lat_squared, c + 1)
                    nc.vector.tensor_scalar(tmp[:, c % 4, :], stream.bank(g + c)[:], col("g_qa", c), None, ALU.mult).then_inc(
                        stream.done[(g + c) % BANKS], 1)
                    stream.wait_done(dve, g + c)
                    keep_halves((lat(c, 0), lat(c, 1)), tmp[:, c % 4, :]).then_inc(lat_ready, 1)
                    dve.wait_ge(lat_ready, c + 1)
                work.wait_full(dve, m + 1)
                nc.vector.tensor_copy(lat_ss[:], work.bank(m + 1)[:, 0:8]).then_inc(work.done[(m + 1) % BANKS], 1)
                work.wait_done(dve, m + 1)
                steps.did(nc.vector.tensor_scalar(ms[:, 0:4], lat_ss[:, 0:4], 1.0 / 384, EPS, ALU.mult, ALU.add))
                nc.vector.tensor_scalar(ms[:, 4:8], lat_ss[:, 4:8], 1.0 / 256, EPS, ALU.mult, ALU.add).then_inc(ms_ready, 1)
                rsqrt(8)
                dve.wait_ge(rstd_ready, calls[0])
                nc.vector.tensor_copy(lat_rs[:], rstd[:, 0:8]).then_inc(lat_rs_ready, 1)
                steps.did(nc.vector.tensor_scalar(row("g_q", 0, 96), row("g_q", 0, 96), 96 ** -0.5, None, ALU.mult))
                for t in range(NT):
                    stream.wait_done(dve, g + 13 + t)
                    steps.did(nc.vector.tensor_tensor(mo[:, t, :], mo[:, t, :], row("g_mh", 0, 512), ALU.mult))
                work.wait_full(dve, m)
                small = work.bank(m)[:, 0:160].rearrange("p (a b) -> p a b", a=NT)
                steps.did(nc.vector.tensor_copy(k_pe[:], small[:, :, 0:32]))
                nc.vector.tensor_tensor(gates[:], small[:, :, 32:40], row("b_gate", 0, 8).unsqueeze(1).to_broadcast([P, NT, 8]),
                                        ALU.add).then_inc(work.done[m % BANKS], 1)

            def mlstm():
                dve.wait_ge(consts_ready, N_CONSTS)
                work.wait_done(dve, base["odd_in"][2])
                f = gl[:, 3, :].rearrange("p (a b) -> p a b", a=NT)
                nc.vector.tensor_copy(f, gates[:, :, 4:8]).then_inc(gates_ready, 1)
                dve.wait_ge(log_ready, 1)
                nc.vector.scalar_tensor_tensor(lf[:], f, 0.0, gl[:, 2, :].rearrange("p (a b) -> p a b", a=NT), ALU.min,
                                               ALU.subtract).then_inc(lf_ready, 1)
                dve.wait_ge(lf_ready, 1)
                work.wait_full(dve, base["odd_in"][2] + 1)
                for n in range(MLSTM_BLOCKS):
                    head, k = divmod(n, NT)
                    steps.did(nc.vector.tensor_scalar(rdiag[:, n, :], ident[:], gates[:, k, head:head + 1], None, ALU.mult))
                    steps.settle()
                    nc.vector.scalar_tensor_tensor(rdiag[:, n, :], below[:], lf[:, k, head:head + 1], rdiag[:, n, :], ALU.mult,
                                                   ALU.add).then_inc(rdiag_ready, 1)
                m = MW["sums", 0]
                work.wait_full(dve, m)
                nc.vector.tensor_scalar(neg_sum[:], work.bank(m)[:, 0:16], -1.0, None, ALU.mult).then_inc(work.done[m % BANKS], 1)
                work.wait_done(dve, m)
                for n in range(MLSTM_BLOCKS + 1):
                    if n < MLSTM_BLOCKS:
                        head, i = divmod(n, NT)
                        m = MW["decay", n]
                        work.wait_full(dve, m)
                        steps.did(nc.vector.tensor_reduce(neg_m[:, n:n + 1], work.bank(m)[:, 0:(i + 1) * P], AX_X, ALU.max, negate=True))
                        steps.settle()
                        nc.vector.tensor_tensor(neg_m[:, n:n + 1], neg_m[:, n:n + 1], neg_sum[:, 4 * i + head:4 * i + head + 1],
                                                ALU.min).then_inc(m_ready, 1)
                        between(n)
                    if n:
                        n1 = n - 1
                        i = n1 % NT
                        work.wait_done(dve, MW["decay", n1])
                        m = MW["scores", n1]
                        work.wait_full(dve, m)
                        w = dec[:, n1 % 3, 0:(i + 1) * P]
                        nc.vector.scalar_tensor_tensor(w, work.bank(m)[:, 0:(i + 1) * P], 1.0, w, ALU.mult, ALU.mult,
                                                       accum_out=den[:, n1:n1 + 1]).then_inc(work.done[m % BANKS], 1)
                        work.wait_done(dve, m)
                        dve.wait_ge(exp_m_ready, n1 + 1)
                        steps.did(nc.vector.scalar_tensor_tensor(den[:, n1:n1 + 1], den[:, n1:n1 + 1], -1.0, den[:, n1:n1 + 1], ALU.mult, ALU.max))
                        steps.settle()
                        steps.did(nc.vector.tensor_tensor(den[:, n1:n1 + 1], den[:, n1:n1 + 1], exp_m[:, n1:n1 + 1], ALU.max))
                        steps.settle()
                        nc.vector.reciprocal(rden[:, n1:n1 + 1], den[:, n1:n1 + 1]).then_inc(rden_ready, 1)

            def hv_sums(t):
                dve.wait_ge(hv_squared, t + 1)
                steps.did(nc.vector.tensor_reduce(stat[:, 4 * t:4 * t + 4], hv_sq[:, t, :].rearrange("p (a b) -> p a b", a=4),
                                                  AX_X, ALU.add))
                if t == NT - 1:
                    steps.settle()
                    nc.vector.tensor_scalar(ms[:, 0:16], stat[:, 0:16], 1.0 / P, EPS, ALU.mult, ALU.add).then_inc(ms_ready, 1)

            def hv_scale(t):
                v = hv[:, t, :].rearrange("p (a b) -> p a b", a=4)
                steps.did(nc.vector.tensor_tensor(v, v, rstd[:, 4 * t:4 * t + 4].unsqueeze(2).to_broadcast([P, 4, P]), ALU.mult))
                steps.settle()
                nc.vector.tensor_tensor(hv[:, t, :], hv[:, t, :], mo[:, t, :], ALU.mult).then_inc(hv_ready, 1)

            def bank_halves(to, m, at):
                work.wait_full(dve, m)
                steps.did(nc.vector.tensor_copy(to[at, 0], work.bank(m)[at, :]))
                steps.settle()
                nc.vector.tensor_tensor(to[at, 1], work.bank(m)[at, :], to[at, 0].bitcast(F32), ALU.subtract).then_inc(
                    work.done[m % BANKS], 1)

            def between(n):
                if 1 <= n < 5:
                    q_sums(n - 1)
                if n == 6:
                    rsqrt(64)
                    dve.wait_ge(rstd_ready, calls[0])
                if 6 <= n < 10:
                    q_scale(n - 6)
                if 7 <= n < 11:
                    k_sums(n - 7)
                if n == 12:
                    rsqrt(36)
                    dve.wait_ge(rstd_ready, calls[0])
                if n == 11:
                    rotate_q()
                if 12 <= n:
                    k_scale(n - 12)
                if n == MLSTM_BLOCKS - 1:
                    rotate_k()

            def q_sums(t):
                st = stat[:].rearrange("p (a b) -> p a b", a=NT)
                dve.wait_ge(squared, t + 1)
                s3 = qk_sq[:, t % 2, 0:768].rearrange("p (a b) -> p a b", a=8)
                steps.did(nc.vector.tensor_reduce(st[:, t, 0:8], s3[:, :, 0:64], AX_X, ALU.add))
                nc.vector.tensor_reduce(st[:, t, 8:16], s3[:, :, 64:96], AX_X, ALU.add).then_inc(summed, 1)
                if t == NT - 1:
                    dve.wait_ge(summed, NT)
                    m3 = ms[:].rearrange("p (a b) -> p a b", a=NT)
                    steps.did(nc.vector.tensor_scalar(m3[:, :, 0:8], st[:, :, 0:8], 1.0 / 64, EPS, ALU.mult, ALU.add))
                    nc.vector.tensor_scalar(m3[:, :, 8:16], st[:, :, 8:16], 1.0 / 32, EPS, ALU.mult, ALU.add).then_inc(ms_ready, 1)

            def q_scale(t):
                r3 = rstd[:].rearrange("p (a b) -> p a b", a=NT)
                q3 = q_t[:, t, :].rearrange("p (a b) -> p a b", a=8)
                steps.did(nc.vector.tensor_tensor(q3[:, :, 0:64], q3[:, :, 0:64],
                                                  r3[:, t, 0:8].unsqueeze(2).to_broadcast([P, 8, 64]), ALU.mult))
                steps.did(nc.vector.tensor_tensor(q3[:, :, 64:96], q3[:, :, 64:96],
                                                  r3[:, t, 8:16].unsqueeze(2).to_broadcast([P, 8, 32]), ALU.mult))
                steps.settle()
                steps.did(nc.vector.tensor_tensor(q3, q3, row("g_q", 0, 96).unsqueeze(1).to_broadcast([P, 8, 96]), ALU.mult))

            def k_sums(t):
                dve.wait_ge(squared, NT + t + 1)
                s3 = qk_sq[:, t % 2, 0:512].rearrange("p (a b) -> p a b", a=8)
                nc.vector.tensor_reduce(stat[:, 8 * t:8 * t + 8], s3, AX_X, ALU.add).then_inc(summed, 1)
                if t == NT - 1:
                    pe2 = angle[:, 0:2, :].rearrange("p a (b c) -> p (a b) c", c=32)
                    steps.did(nc.vector.tensor_tensor(pe2, k_pe[:], k_pe[:], ALU.mult))
                    steps.settle()
                    steps.did(nc.vector.tensor_reduce(stat[:, 32:36], pe2, AX_X, ALU.add))
                    steps.settle()
                    dve.wait_ge(summed, 2 * NT)
                    steps.did(nc.vector.tensor_scalar(ms[:, 0:32], stat[:, 0:32], 1.0 / 64, EPS, ALU.mult, ALU.add))
                    nc.vector.tensor_scalar(ms[:, 32:36], stat[:, 32:36], 1.0 / 32, EPS, ALU.mult, ALU.add).then_inc(ms_ready, 1)

            def k_scale(t):
                k3 = k_t[:, t, :].rearrange("p (a b) -> p a b", a=8)
                steps.did(nc.vector.tensor_tensor(k3[:, :, 0:64], k3[:, :, 0:64],
                                                  rstd[:, 8 * t:8 * t + 8].unsqueeze(2).to_broadcast([P, 8, 64]), ALU.mult))
                steps.settle()
                steps.did(nc.vector.tensor_tensor(k3[:, :, 0:64], k3[:, :, 0:64],
                                                  row("g_k", 0, 64).unsqueeze(1).to_broadcast([P, 8, 64]), ALU.mult))

            def turn(x1, x2, c, s, t4):
                for j, (x, f) in enumerate(((x1, c), (x2, s), (x2, c), (x1, s))):
                    steps.settle()
                    steps.did(nc.vector.tensor_tensor(t4[j], x, f, ALU.mult))
                steps.settle()
                steps.did(nc.vector.tensor_tensor(x1, t4[0], t4[1], ALU.subtract))
                steps.did(nc.vector.tensor_tensor(x2, t4[2], t4[3], ALU.add))

            def rotate_q():
                dve.wait_ge(turned_ready, 1)
                dve.wait_ge(squared, 2 * NT)
                dve.wait_ge(summed, 2 * NT)
                cos, sin = (cos_sin[:, j, :].rearrange("p (a b) -> p a b", a=NT) for j in range(2))
                q4 = q_t.rearrange("p t (a b) -> p t a b", a=8)
                wide = [P, NT, 8, 16]
                turn(q4[:, :, :, 64:80], q4[:, :, :, 80:96], cos.unsqueeze(2).to_broadcast(wide), sin.unsqueeze(2).to_broadcast(wide),
                     [turn_tmp[:, j, :].rearrange("p (t a b) -> p t a b", t=NT, a=8) for j in range(4)])

            def rotate_k():
                cos, sin = (cos_sin[:, j, :].rearrange("p (a b) -> p a b", a=NT) for j in range(2))
                steps.did(nc.vector.tensor_tensor(k_pe[:], k_pe[:], rstd[:, 32:36].unsqueeze(2).to_broadcast([P, NT, 32]), ALU.mult))
                steps.settle()
                steps.did(nc.vector.tensor_tensor(k_pe[:], k_pe[:], row("g_k", 64, 32).unsqueeze(1).to_broadcast([P, NT, 32]), ALU.mult))
                turn(k_pe[:, :, 0:16], k_pe[:, :, 16:32], cos, sin,
                     [turn_tmp[:, j, 0:64].rearrange("p (t b) -> p t b", t=NT) for j in range(4)])
                k4 = k_t.rearrange("p t (a b) -> p t a b", a=8)
                steps.settle()
                for t in range(NT):
                    x = nc.vector.tensor_copy(k4[:, t, :, 64:96], k_pe[:, t, :].unsqueeze(1).to_broadcast([P, 8, 32]))
                    if t < NT - 1:
                        steps.did(x)
                x.then_inc(qk_ready, 1)

            def mla():
                def take_turned(name, dst, head):
                    m = AW[name, head]
                    work.wait_full(dve, m)
                    nc.vector.tensor_copy(dst[0:96, head % 2, :], work.bank(m)[0:96, :]).then_inc(work.done[m % BANKS], 1)

                take_turned("q", qT, 0)
                take_turned("k", kT, 0)
                for n in range(MLA_BLOCKS + 2):
                    if n < MLA_BLOCKS:
                        head, i = divmod(n, NT)
                        m = AW["scores", n]
                        work.wait_full(dve, m)
                        nc.vector.tensor_reduce(neg_m[:, n:n + 1], work.bank(m)[:, 0:(i + 1) * P], AX_X, ALU.max,
                                                negate=True).then_inc(m_ready, 1)
                        if 1 <= n <= NT:
                            hv_sums(n - 1)
                        if n == HV_BLOCK - 3:
                            rsqrt(16)
                            dve.wait_ge(rstd_ready, calls[0])
                        if HV_BLOCK - 3 <= n <= HV_BLOCK:
                            hv_scale(n - HV_BLOCK + 3)
                    if 1 <= n <= MLA_BLOCKS:
                        n1 = n - 1
                        work.wait_done(dve, AW["scores", n1])
                        steps.did(nc.vector.reciprocal(rden[:, n1:n1 + 1], den[:, n1:n1 + 1]))
                        steps.settle()
                        p = prob[:, n1 % 3, 0:(n1 % NT + 1) * P]
                        nc.vector.tensor_scalar(p, p, rden[:, n1:n1 + 1], None, ALU.mult).then_inc(prob_ready, 1)
                    if n > NT and n % NT == 1:
                        head = n // NT - 1
                        m, q = AW["out", head], 64 * (head % 2)
                        bank_halves(y[:, :, head // 2, :], m, slice(q, q + 64))
                    if n % NT == 1 and n // NT + 1 < MLA_HEADS:
                        take_turned("q", qT, n // NT + 1)
                        take_turned("k", kT, n // NT + 1)
                    if n == HV_BLOCK:
                        for head in range(MLSTM_HEADS):
                            bank_halves(y[:, :, 4 + head, :], AW["y", head], slice(0, P))

            def exponents(n):
                s = 1 << (n - 1)
                c4 = cum.rearrange("p c (n two s) -> p (c n) two s", two=2, s=s)
                e4 = pair[:, n % 2].rearrange("p c (n two s) -> p (c n) two s", two=2, s=s)
                left, right = c4[:, :, 0, :], c4[:, :, 1, :]
                mid = c4[:, :, 0, s - 1:s].to_broadcast([P, T // s, s])
                steps.did(nc.vector.tensor_tensor(e4[:, :, 0, :], mid, left, ALU.subtract))
                nc.vector.tensor_tensor(e4[:, :, 1, :], right, mid, ALU.subtract).then_inc(exponent_ready, 1)

            def pairs_of(n):
                s = 1 << (n - 1)
                cut = lambda x, half: x.rearrange("p c (n two s) -> p (c n) two s", two=2, s=s)[:, :, half, :]
                e = pair[:, n % 2]
                dve.wait_ge(decay_ready, n)
                steps.did(nc.vector.tensor_tensor(cut(e, 0), cut(e, 0), cut(gk, 0), ALU.mult))
                nc.vector.tensor_tensor(cut(e, 1), cut(e, 1), cut(gq, 1), ALU.mult).then_inc(pair_ready, 1)

            def take_level(n):
                for q in range(NT):
                    m = GW["level", n, q]
                    work.wait_full(dve, m)
                    acc = near[:, 2 * (q // 2):2 * (q // 2) + 2, :].rearrange("p t (c r b) -> p (t c) r b", c=2, r=2)[:, :, q % 2, :]
                    o = work.bank(m)[:].rearrange("p (a b) -> p a b", a=4)
                    if n == 0:
                        x = nc.vector.tensor_tensor(acc, o, ident[:].unsqueeze(1).to_broadcast([P, 4, P]), ALU.mult)
                    else:
                        work.wait_done(dve, GW["level", n - 1, q])
                        x = nc.vector.copy_predicated(
                            acc, level_mask[:, n - 1, :].bitcast(U32).unsqueeze(1).to_broadcast([P, 4, P]), o)
                    x.then_inc(work.done[m % BANKS], 1)

            def gla():
                g = base["gla_in"][1] + 1
                dve.wait_ge(logit_logged, 1)
                dve.wait_ge(masks_ready, N_MASKS)
                steps.did(nc.vector.scalar_tensor_tensor(logit, logit, 0.0, log_p, ALU.min, ALU.subtract))
                steps.settle()
                for c in range(2):
                    for i in range(NT):
                        tile = slice(i * P, (i + 1) * P)
                        steps.did(nc.vector.tensor_tensor_scan(cum[:, c, tile], ones[:], logit[:, c, tile], 0.0, ALU.mult, ALU.add))
                steps.settle()
                for c in range(2):
                    steps.did(nc.vector.tensor_scalar(tot16[:, c, :], cum[:, c, :].rearrange("p (a b) -> p a b", b=P)[:, :, P - 1],
                                                      1.0 / 16, None, ALU.mult))
                for c in range(4):
                    stream.wait_done(dve, g + c)
                exponents(1)
                pairs_of(1)
                exponents(2)
                take_level(0)
                pairs_of(2)
                for n in range(3, LEVELS):
                    take_level(n - 2)
                    exponents(n)
                    if n == 3:
                        for t in range(NT):
                            stream.wait_done(dve, g + 8 + t)
                            steps.did(nc.vector.tensor_tensor(gr[:, t, :], gr[:, t, :], row("gla_norm", 0, 512), ALU.mult))
                    pairs_of(n)
                steps.settle()
                nc.vector.tensor_copy(stat[:, 0:1], tot16[:, 0, 0:1]).then_inc(exponent_ready, 1)
                take_level(LEVELS - 2)
                dve.wait_ge(far_exp, 1)
                for c in range(2):
                    steps.did(nc.vector.tensor_tensor(kd[:, c, 0:3 * P], kd[:, c, 0:3 * P], gk[:, c, 0:3 * P], ALU.mult))
                    for slot, i in enumerate((1, 3, 2)):
                        v = qd[:, c, slot * P:(slot + 1) * P]
                        steps.did(nc.vector.tensor_tensor(v, v, gq[:, c, i * P:(i + 1) * P], ALU.mult))
                    steps.settle()
                    steps.did(nc.vector.tensor_scalar(kd[:, c, 3 * P:4 * P], kd[:, c, 0:P], exp_tot[:, c, 1:2], None, ALU.mult))
                    x = nc.vector.tensor_scalar(qd[:, c, 3 * P:4 * P], qd[:, c, P:2 * P], exp_tot[:, c, 2:3], None, ALU.mult)
                    if c == 0:
                        steps.did(x)
                    else:
                        x.then_inc(far_ready, 1)
                take_level(LEVELS - 1)
                for i in range(NT):
                    work.wait_done(dve, GW["level", LEVELS - 1, i])
                for i in range(NT):
                    nc.vector.tensor_copy(stat[:, 60 + i:61 + i], near[:, i, 0:1]).then_inc(near_ready, 1)
                for t in range(NT):
                    dve.wait_ge(go_squared, t + 1)
                    steps.did(nc.vector.tensor_reduce(stat[:, 4 * t:4 * t + 4], go_sq[:, t, :].rearrange("p (a b) -> p a b", a=4),
                                                      AX_X, ALU.add))
                steps.settle()
                nc.vector.tensor_scalar(ms[:, 0:16], stat[:, 0:16], 1.0 / P, EPS, ALU.mult, ALU.add).then_inc(ms_ready, 1)
                rsqrt(16)
                dve.wait_ge(rstd_ready, calls[0])
                for t in range(NT):
                    v = go[:, t, :].rearrange("p (a b) -> p a b", a=4)
                    steps.did(nc.vector.tensor_tensor(v, v, rstd[:, 4 * t:4 * t + 4].unsqueeze(2).to_broadcast([P, 4, P]), ALU.mult))
                    steps.settle()
                    nc.vector.tensor_tensor(go[:, t, :], go[:, t, :], gr[:, t, :], ALU.mult).then_inc(go_ready, 1)
                for head in range(GLA_HEADS):
                    bank_halves(branch[0][:, :, head, :], GW["y", head], slice(0, P))

            def pool_means(c):
                stream.wait_done(dve, base["pool"][1] + c)
                src = pu[:, c, :]
                for r in range(c + 1):
                    k, lo = 1 << r, (2 << r) - 1
                    dst = psum_a[:, r % 2, :]
                    steps.did(nc.vector.tensor_tensor(dst[:, lo:16 + T], src[:, lo:16 + T], src[:, lo - k:16 + T - k], ALU.add))
                    steps.settle()
                    src = dst
                w = 2 << c
                steps.did(nc.vector.tensor_tensor(stat[:, 0:w], src[:, 16:16 + w], inv_count[:, 0:w], ALU.mult))
                v = tmp[:, c, :]
                steps.did(nc.vector.scalar_tensor_tensor(v[:, w:T], src[:, 16 + w:16 + T], 1.0 / w, pu[:, c, 16 + w:16 + T],
                                                         ALU.mult, ALU.subtract))
                steps.settle()
                steps.did(nc.vector.tensor_tensor(v[:, 0:w], stat[:, 0:w], pu[:, c, 16:16 + w], ALU.subtract))
                steps.settle()

            def swa():
                dve.wait_ge(freq_ready, 2)
                nc.vector.memset(pu[:, :, 0:16], 0.0).then_inc(pad_ready, 1)
                nc.vector.tensor_scalar(neg_sink[:], row("sinks", 0, 8), -1.0, None, ALU.mult).then_inc(sink_ready, 1)
                dve.wait_ge(sink_ready, 1)
                for n in range(SWA_BLOCKS + 2):
                    if n < SWA_BLOCKS:
                        m = SW["scores", n]
                        two = slice(2 * n, 2 * n + 2)
                        q_head = 4 * (n % 2) + n // 4
                        own = lambda x: x[:, q_head:q_head + 1].to_broadcast([P, 2])
                        work.wait_full(dve, m)
                        steps.did(nc.vector.tensor_reduce(neg_m[:, two], work.bank(m)[:].rearrange("p (s b) -> p s b", s=2),
                                                          AX_X, ALU.max, negate=True))
                        steps.settle()
                        nc.vector.tensor_tensor(neg_m[:, two], neg_m[:, two], own(neg_sink), ALU.min).then_inc(m_ready, 1)
                        dve.wait_ge(m_ready, MLSTM_BLOCKS + MLA_BLOCKS + n + 1)
                        nc.vector.tensor_tensor(sink_m[:, two], neg_m[:, two], own(row("sinks", 0, 8)), ALU.add).then_inc(sink_ready, 1)
                    if 1 <= n <= SWA_BLOCKS:
                        n1 = n - 1
                        two = slice(2 * n1, 2 * n1 + 2)
                        work.wait_done(dve, SW["scores", n1])
                        steps.did(nc.vector.tensor_tensor(den[:, two], den[:, two], sink_m[:, two], ALU.add))
                        steps.settle()
                        steps.did(nc.vector.reciprocal(rden[:, two], den[:, two]))
                        steps.settle()
                        for s in range(2):
                            p = sprob[:, n1 % 3, 256 * s:256 * s + 256]
                            x = nc.vector.tensor_scalar(p, p, rden[:, 2 * n1 + s:2 * n1 + s + 1], None, ALU.mult)
                            if s == 0:
                                steps.did(x)
                        x.then_inc(sprob_ready, 1)
                    if n > NT and n % NT == 1:
                        j = n // NT - 1
                        bank_halves(branch[1][:, :, j, :], SW["out", j], slice(0, P))
                    if n % 4 == 3:
                        pool_means(n // 4)

            def pool():
                g = base["pool"][1]
                for c in range(4):
                    keep_halves((pd[:, 0, c, :], pd[:, 1, c, :]), tmp[:, c, :]).then_inc(pd_ready, 1)
                    dve.wait_ge(pd_ready, c + 1)
                for c in range(4):
                    n = g + 4 + c
                    stream.wait_full(dve, n)
                    nc.vector.tensor_scalar(tmp[:, c, :], stream.bank(n)[:], col("pool_scale", c), None, ALU.mult).then_inc(
                        stream.done[n % BANKS], 1)
                    stream.wait_done(dve, n)
                    keep_halves((branch[2][:, 0, c, :], branch[2][:, 1, c, :]), tmp[:, c, :]).then_inc(branch_ready, 1)
                dve.wait_ge(branch_ready, 4)

            def merge():
                g = base["merge"][1]
                for n in range(3 * DC):
                    c, b = divmod(n, 3)
                    o = g + 2 * n + 1
                    stream.wait_full(dve, o)
                    stream.wait_done(dve, o - 1)
                    nc.vector.tensor_tensor(tmp[:, 3 if b == 0 else 2, :], stream.bank(o)[:], tmp[:, n % 2, :], ALU.mult).then_inc(
                        stream.done[o % BANKS], 1)
                    stream.wait_done(dve, o)
                    if b:
                        steps.did(nc.vector.tensor_tensor(tmp[:, 3, :], tmp[:, 3, :], tmp[:, 2, :], ALU.add))
                        steps.settle()
                    if b == 2:
                        keep_halves((merged[:, 0, c, :], merged[:, 1, c, :]), tmp[:, 3, :]).then_inc(y_ready, 1)
                        dve.wait_ge(y_ready, DC + c + 1)

            def convffn():
                g = base["convffn"][1]

                def body(i):
                    for j in range(4):
                        b, gate = j // 2, j % 2 == 0
                        c = 2 * i + b + (0 if gate else FC)
                        dve.wait_ge(conv_started, 4 * i + j + 1)
                        o = stream.bank(g + j)
                        nc.vector.scalar_tensor_tensor(tmp[:, j, 1:T], o[:, 0:T - 1], cols[:, bass.ds(c + COLS["cw1"], 1)],
                                                       tmp[:, j, 1:T], ALU.mult, ALU.add).then_inc(dve_steps, 1)
                        dve.wait_ge(dve_steps, steps.n + 6 * i + j + (j > 1) + 1)
                        nc.vector.scalar_tensor_tensor(tmp[:, j, 2:T], o[:, 0:T - 2], cols[:, bass.ds(c + COLS["cw0"], 1)],
                                                       tmp[:, j, 2:T], ALU.mult, ALU.add).then_inc(stream.done[(g + j) % BANKS], 1)
                        if not gate:
                            dve.wait_ge(gelu_ready, 2 * i + b + 1)
                            dve.wait_ge(stream.done[(g + j) % BANKS], i + (g + j) // BANKS + 1)
                            v = tmp[:, j, :]
                            nc.vector.tensor_tensor(v, v, tmp[:, j - 1, :], ALU.mult).then_inc(conv_product, 1)
                            dve.wait_ge(conv_product, 2 * i + b + 1)
                            hi, lo = (act[:, p, bass.ds(2 * i + b, 1), :] for p in range(2))
                            nc.vector.tensor_copy(hi, v.unsqueeze(1)).then_inc(dve_steps, 1)
                            dve.wait_ge(dve_steps, steps.n + 6 * i + 3 * b + 3)
                            nc.vector.tensor_tensor(lo, v.unsqueeze(1), hi.bitcast(F32), ALU.subtract).then_inc(act_ready, 1)

                with dve.Fori(0, 2 * FC // 4) as i:
                    body(i)
                steps.n += 3 * FC

            norm("norm_mix0", "g_mix0")
            even_in()
            add_outs(base["even_out"][1], DC)
            norm("norm_ffn0", "g_ffn0")
            rope_angles()
            ffn("ffn0")
            norm("norm_ple0", "g_ple0")
            ple("ple0")
            norm("norm_mix1", "g_mix1")
            odd_in()
            mlstm()
            mla()
            add_outs(base["odd_out"][1], DC)
            norm("norm_ffn1", "g_ffn1")
            ffn("ffn1")
            norm("norm_ple1", "g_ple1")
            ple("ple1")
            norm("norm_mix2", "mix_pre")
            gla()
            swa()
            pool()
            merge()
            norm("norm_post", "mix_post")
            norm("norm_ffn2", "ffn_pre")
            convffn()
            norm("norm_last", "ffn_post")


def feature_units(w):
    k, n = w.shape
    return w.reshape(k // P, P, n // P, P).transpose(2, 1, 0, 3).reshape(n // P, P, k)


def token_units(w):
    return w.reshape(4, 2, P, 512).transpose(0, 2, 1, 3).reshape(4, P, 1024)


def down_units(w):
    return w.reshape(2, 11, P, DC, P).transpose(3, 0, 2, 1, 4).reshape(2 * DC, P, 11 * P)


def pairs(gate, up):
    import numpy as np
    return np.stack([feature_units(gate), feature_units(up)], 1).reshape(2 * FC, P, D)


def chunks(v):
    return v.reshape(-1, P).T


def tokens_first(x):
    return x.reshape(T, -1, P).transpose(2, 1, 0)


def lay_out(i):
    import numpy as np
    o = {}
    o["x"] = tokens_first(i["x"][0])
    o["p0"] = tokens_first(i["p"][0, 0])
    c = {"g_mix0": i["g_mix"][0], "g_ffn0": i["g_ffn"][0], "g_ple0": i["g_ple"][0],
         "g_mix1": i["g_mix"][1], "g_ffn1": i["g_ffn"][1], "g_ple1": i["g_ple"][1],
         "mix_pre": i["norm_mix_pre_2"], "mix_post": i["norm_mix_post_2"],
         "ffn_pre": i["norm_ffn_pre_2"], "ffn_post": i["norm_ffn_post_2"],
         "w_conv": i["ev_w_conv"], "g_qa": i["od_g_qa"], "g_kva": i["od_g_kva"], "gla_b": i["gla_b_gate_2"],
         "pool_scale": i["pool_scale_2"], "cw0": i["ffn_conv_w_2"][0, 0], "cw1": i["ffn_conv_w_2"][0, 1],
         "cw2": i["ffn_conv_w_2"][0, 2], "cb": i["ffn_conv_b_2"]}
    o["cols"] = np.concatenate([chunks(c[n]) for n in COLS], 1)
    r = {"g_v": i["ev_g_v"], "g_q": i["od_g_q"], "g_k": i["od_g_k"], "b_gate": i["od_b_gate"], "g_mh": i["od_g_mh"],
         "gla_norm": i["gla_norm_2"], "sinks": i["swa_sinks_2"]}
    o["rows"] = np.concatenate([r[n].reshape(-1) for n in ROWS])
    o["w_s"] = i["ev_w_s"][0].transpose(2, 0, 1)
    o["b_s"] = i["ev_b_s"]
    w = i["ev_w_in"][0]
    fu = feature_units(w[:, :2048]).reshape(4, 4, P, D)
    o["w_even"] = np.concatenate([fu[[1, 2, 0]].transpose(1, 0, 2, 3).reshape(12, P, D), fu[3], token_units(w[:, 2048:])])
    o["w_even_out"] = feature_units(i["ev_w_out"][0])
    for l in range(2):
        o[f"w_up{l}"] = pairs(i["w_gate"][l], i["w_up"][l])
        o[f"w_down{l}"] = down_units(i["w_down"][l])
        o[f"w_ple{l}"] = np.concatenate([feature_units(i["w_ple_gate"][l]), feature_units(i["w_ple_proj"][l])], 2)
    o["p1"] = tokens_first(i["p"][1, 0])
    w = i["od_w_in"][0]
    at = np.cumsum([0, 384, 256, 32, 256, 256, 512, 512, 8])
    q_lat, kv_lat, k_pe, mq, mk, mv, mo, gates = (w[:, x:y] for x, y in zip(at[:-1], at[1:]))
    o["w_odd"] = np.concatenate([feature_units(v) for v in (q_lat, kv_lat, mq, mk)] + [token_units(v) for v in (mv, mo)])
    o["w_small"] = np.concatenate([k_pe, gates], 1).reshape(DC, P, 40).transpose(1, 0, 2)
    o["positions"] = i["positions"].reshape(NT, P).T
    o["w_q_up"] = i["od_w_q_up"][0].reshape(3, P, 2, 384).transpose(2, 1, 0, 3).reshape(2, P, 1152)
    o["w_kv_up"] = i["od_w_kv_up"][0].reshape(2, P, 2, 512).transpose(2, 1, 0, 3).reshape(2, P, 1024)
    o["w_odd_out"] = feature_units(i["od_w_out"][0])
    w = i["w_in_2"][0]
    at = np.cumsum([0, 256, 256, 512, 16, 512, 512, 128, 128, 512, 3072])
    g_q, g_k, g_v, low, g_r, s_q, s_k, s_v, p_u, gate = (w[:, x:y] for x, y in zip(at[:-1], at[1:]))
    low = np.concatenate([low, np.zeros((D, P - 16), low.dtype)], 1)
    o["w_gla"] = np.concatenate([feature_units(low), feature_units(g_q), feature_units(g_k), token_units(g_v), token_units(g_r)])
    o["w_gate_up"] = i["gla_w_gate_up_2"][0]
    s_q = s_q.reshape(D, 2, 4, 64).transpose(0, 2, 1, 3).reshape(D, 512)
    o["w_swa"] = np.concatenate([feature_units(s_q), feature_units(s_k), feature_units(s_v)])
    o["w_pool"] = feature_units(p_u)
    o["w_group"] = i["pool_w_2"][0].transpose(1, 0, 2).reshape(1, P, 512)
    swa = i["w_branch_swa_2"][0].reshape(2, 4, 64, D).transpose(1, 0, 2, 3).reshape(512, D)
    o["w_merge"] = np.stack([np.concatenate([feature_units(gate[:, D * b:D * b + D]), feature_units(v)], 2)
                             for b, v in enumerate((i["w_branch_gla_2"][0], swa, i["w_branch_pool_2"][0]))], 1).reshape(3 * DC, P, 12 * P)
    o["w_block_out"] = feature_units(i["w_out_2"][0])
    w = i["ffn_w_up_2"][0]
    o["w_up2"] = pairs(w[:, :FF], w[:, FF:])
    o["w_down2"] = down_units(i["ffn_w_down_2"][0])
    return o


def kernel(**inputs):
    import numpy as np
    import concourse.bacc as bacc
    from concourse.bass_utils import run_bass_kernel_spmd

    nc = bacc.Bacc("TRN2", target_bir_lowering=False, num_devices=1)
    arrays, aps = {}, {}
    for name, v in lay_out({k: np.asarray(v) for k, v in inputs.items()}).items():
        arrays[f"in_{name}"] = np.ascontiguousarray(v)
        aps[name] = nc.dram_tensor(f"in_{name}", v.shape, mybir.dt.from_np(v.dtype), kind="ExternalInput").ap()
    out = nc.dram_tensor("out_dram", (P, DC, T), F32, kind="ExternalOutput").ap()
    build(nc, aps, out)
    r = run_bass_kernel_spmd(nc, [arrays], core_ids=[0])
    return r.results[0]["out_dram"].transpose(2, 1, 0).reshape(1, T, D)
```
